# Optimizing a Trainium2 kernel written in Bass

```python
import jax
import jax.numpy as jnp
from jax import lax
import numpy as np

D_MODEL = 2048
BATCH = 1
SEQ = 256
DEPTH = 1

CHUNK = 64
MEM_LEN = 256
FOX_HEADS = 8
FOX_HEAD_DIM = 128
FOX_WIDTH = FOX_HEADS * FOX_HEAD_DIM
LRU_WIDTH = 1024
LRU_BLOCKS = 8
LRU_BLOCK_DIM = LRU_WIDTH // LRU_BLOCKS
LRU_CONV = 4
LRU_C = 8.0
MEM_HEADS = 4
MEM_HEAD_DIM = 256
MEM_WIDTH = MEM_HEADS * MEM_HEAD_DIM
N_BRANCH = 3
BRANCH_WIDTH = 1024
FFN_HIDDEN = 5632
FFN_CONV = 3
Q_BLOCK = 128
EPS = 1e-6
IN_COLS = 3 * FOX_WIDTH + FOX_HEADS + 2 * LRU_WIDTH + MEM_WIDTH + N_BRANCH * D_MODEL

kernel_name = 'fox_rglru_mem_gated_hybrid'

def rmsnorm(x, g):
    xf = x.astype(jnp.float32)
    y = xf * lax.rsqrt(jnp.mean(xf * xf, axis=-1, keepdims=True) + EPS)
    return (y * g.astype(jnp.float32)).astype(x.dtype)

def causal_depthwise_conv(x, w, b):
    k_width = w.shape[0]
    y = lax.conv_general_dilated(
        x, w[:, None, :].astype(x.dtype), window_strides=(1,),
        padding=[(k_width - 1, 0)], dimension_numbers=('NWC', 'WIO', 'NWC'),
        feature_group_count=x.shape[-1])
    return y + b.astype(x.dtype)

def forgetting_attention(q, k, v, log_f):
    b, h, s, d = q.shape
    n_blocks = s // Q_BLOCK
    c = jnp.cumsum(log_f, axis=-1)
    scale = d ** -0.5
    q_blocks = q.reshape(b, h, n_blocks, Q_BLOCK, d).transpose(2, 0, 1, 3, 4)
    c_blocks = c.reshape(b, h, n_blocks, Q_BLOCK).transpose(2, 0, 1, 3)
    key_pos = jnp.arange(s)

    def block(args):
        q_i, c_i, i = args
        logits = jnp.einsum('bhqd,bhkd->bhqk', q_i, k, preferred_element_type=jnp.float32) * scale
        logits = logits + c_i[..., None] - c[:, :, None, :]
        query_pos = i * Q_BLOCK + jnp.arange(Q_BLOCK)
        mask = key_pos[None, :] <= query_pos[:, None]
        p = jax.nn.softmax(jnp.where(mask, logits, -jnp.inf), axis=-1)
        return jnp.einsum('bhqk,bhkd->bhqd', p.astype(v.dtype), v)

    out = lax.map(block, (q_blocks, c_blocks, jnp.arange(n_blocks)))
    return out.transpose(1, 0, 3, 2, 4).reshape(b, s, h * d)

def rg_lru(x, w_a, b_a, w_x, b_x, lam):
    b, s, w = x.shape
    xb = x.reshape(b, s, LRU_BLOCKS, LRU_BLOCK_DIM)
    r = jax.nn.sigmoid(jnp.einsum('bsni,nij->bsnj', xb, w_a) + b_a).reshape(b, s, w)
    i_gate = jax.nn.sigmoid(jnp.einsum('bsni,nij->bsnj', xb, w_x) + b_x).reshape(b, s, w)
    log_a = LRU_C * r.astype(jnp.float32) * jax.nn.log_sigmoid(lam.astype(jnp.float32))
    a = jnp.exp(log_a)
    u = jnp.sqrt(-jnp.expm1(2.0 * log_a)) * (i_gate * x).astype(jnp.float32)

    def combine(left, right):
        a_l, h_l = left
        a_r, h_r = right
        return a_l * a_r, a_r * h_l + h_r

    _, hs = lax.associative_scan(combine, (a, u), axis=1)
    return hs.astype(x.dtype)

def memory_attention(q, k, v):
    b, s, h, d = q.shape
    logits = jnp.einsum('bshd,bmhd->bhsm', q, k, preferred_element_type=jnp.float32) * (d ** -0.5)
    p = jax.nn.softmax(logits, axis=-1)
    out = jnp.einsum('bhsm,bmhd->bshd', p.astype(v.dtype), v)
    return out.reshape(b, s, h * d)

def hybrid_layer(x, mem, g_mix, w_in, b_f, g_q_fox, g_k_fox, w_lru_conv, b_lru_conv,
                 w_rg_a, b_rg_a, w_rg_x, b_rg_x, lru_lambda, g_mem, w_mem_kv, g_q_mem,
                 g_k_mem, b_gate, w_branch, w_out, g_ffn, w_ffn_up, w_ffn_conv,
                 b_ffn_conv, w_ffn_down):
    b, s, _ = x.shape
    h = rmsnorm(x, g_mix)
    proj = h @ w_in
    cuts = np.cumsum([FOX_WIDTH, FOX_WIDTH, FOX_WIDTH, FOX_HEADS,
                      LRU_WIDTH, LRU_WIDTH, MEM_WIDTH]).tolist()
    fq, fk, fv, ff, lx, lg, mq, gate_logits = jnp.split(proj, cuts, axis=-1)

    q = rmsnorm(fq.reshape(b, s, FOX_HEADS, FOX_HEAD_DIM), g_q_fox).transpose(0, 2, 1, 3)
    k = rmsnorm(fk.reshape(b, s, FOX_HEADS, FOX_HEAD_DIM), g_k_fox).transpose(0, 2, 1, 3)
    v = fv.reshape(b, s, FOX_HEADS, FOX_HEAD_DIM).transpose(0, 2, 1, 3)
    log_f = jax.nn.log_sigmoid(ff.astype(jnp.float32) + b_f.astype(jnp.float32)).transpose(0, 2, 1)
    y_fox = forgetting_attention(q, k, v, log_f)

    xr = causal_depthwise_conv(lx, w_lru_conv, b_lru_conv)
    y_lru = rg_lru(xr, w_rg_a, b_rg_a, w_rg_x, b_rg_x, lru_lambda) * jax.nn.gelu(lg)

    m = mem.shape[1]
    mk, mv = jnp.split(rmsnorm(mem, g_mem) @ w_mem_kv, 2, axis=-1)
    qm = rmsnorm(mq.reshape(b, s, MEM_HEADS, MEM_HEAD_DIM), g_q_mem)
    km = rmsnorm(mk.reshape(b, m, MEM_HEADS, MEM_HEAD_DIM), g_k_mem)
    vm = mv.reshape(b, m, MEM_HEADS, MEM_HEAD_DIM)
    y_mem = memory_attention(qm, km, vm)

    branches = jnp.stack([y_fox, y_lru, y_mem], axis=2)
    y_d = jnp.einsum('bsnc,ncd->bsnd', branches, w_branch)
    gates = jax.nn.sigmoid(gate_logits.reshape(b, s, N_BRANCH, D_MODEL) + b_gate)
    merged = jnp.sum(gates * y_d, axis=2)
    x = x + merged @ w_out

    up = causal_depthwise_conv(rmsnorm(x, g_ffn) @ w_ffn_up, w_ffn_conv, b_ffn_conv)
    u_act, u_val = jnp.split(up, 2, axis=-1)
    return x + (jax.nn.gelu(u_act) * u_val) @ w_ffn_down

def setup_inputs(seed: int = 0) -> dict:
    key = jax.random.key(seed)
    ks = jax.random.split(key, 26)
    L = DEPTH
    f32 = jnp.float32

    def nrm(k, shape, fan_in):
        return jax.random.normal(k, shape, f32) * (fan_in ** -0.5)

    def gain(k, shape):
        return 1.0 + 0.02 * jax.random.normal(k, shape, f32)

    def bias(k, shape):
        return 0.01 * jax.random.normal(k, shape, f32)

    a_c = jax.random.uniform(ks[13], (L, LRU_WIDTH), f32, minval=0.9, maxval=0.999)
    sig = a_c ** (1.0 / LRU_C)
    lru_lambda = jnp.log(sig) - jnp.log1p(-sig)
    return {
        'x': jax.random.normal(ks[0], (BATCH, SEQ, D_MODEL), f32),
        'mem': jax.random.normal(ks[1], (BATCH, MEM_LEN, D_MODEL), f32),
        'g_mix': gain(ks[2], (L, D_MODEL)),
        'w_in': nrm(ks[3], (L, D_MODEL, IN_COLS), D_MODEL),
        'b_f': jax.random.uniform(ks[4], (L, FOX_HEADS), f32, minval=1.0, maxval=6.0),
        'g_q_fox': gain(ks[5], (L, FOX_HEAD_DIM)),
        'g_k_fox': gain(ks[6], (L, FOX_HEAD_DIM)),
        'w_lru_conv': nrm(ks[7], (L, LRU_CONV, LRU_WIDTH), LRU_CONV),
        'b_lru_conv': bias(ks[8], (L, LRU_WIDTH)),
        'w_rg_a': nrm(ks[9], (L, LRU_BLOCKS, LRU_BLOCK_DIM, LRU_BLOCK_DIM), LRU_BLOCK_DIM),
        'b_rg_a': bias(ks[10], (L, LRU_BLOCKS, LRU_BLOCK_DIM)),
        'w_rg_x': nrm(ks[11], (L, LRU_BLOCKS, LRU_BLOCK_DIM, LRU_BLOCK_DIM), LRU_BLOCK_DIM),
        'b_rg_x': bias(ks[12], (L, LRU_BLOCKS, LRU_BLOCK_DIM)),
        'lru_lambda': lru_lambda,
        'g_mem': gain(ks[14], (L, D_MODEL)),
        'w_mem_kv': nrm(ks[15], (L, D_MODEL, 2 * MEM_WIDTH), D_MODEL),
        'g_q_mem': gain(ks[16], (L, MEM_HEAD_DIM)),
        'g_k_mem': gain(ks[17], (L, MEM_HEAD_DIM)),
        'b_gate': bias(ks[18], (L, N_BRANCH, D_MODEL)),
        'w_branch': nrm(ks[19], (L, N_BRANCH, BRANCH_WIDTH, D_MODEL), BRANCH_WIDTH),
        'w_out': nrm(ks[20], (L, D_MODEL, D_MODEL), D_MODEL),
        'g_ffn': gain(ks[21], (L, D_MODEL)),
        'w_ffn_up': nrm(ks[22], (L, D_MODEL, 2 * FFN_HIDDEN), D_MODEL),
        'w_ffn_conv': nrm(ks[23], (L, FFN_CONV, 2 * FFN_HIDDEN), FFN_CONV),
        'b_ffn_conv': bias(ks[24], (L, 2 * FFN_HIDDEN)),
        'w_ffn_down': nrm(ks[25], (L, FFN_HIDDEN, D_MODEL), FFN_HIDDEN),
    }

def reference(x, mem, g_mix, w_in, b_f, g_q_fox, g_k_fox, w_lru_conv, b_lru_conv,
              w_rg_a, b_rg_a, w_rg_x, b_rg_x, lru_lambda, g_mem, w_mem_kv, g_q_mem,
              g_k_mem, b_gate, w_branch, w_out, g_ffn, w_ffn_up, w_ffn_conv,
              b_ffn_conv, w_ffn_down):
    for l in range(DEPTH):
        x = hybrid_layer(
            x, mem, g_mix[l], w_in[l], b_f[l], g_q_fox[l], g_k_fox[l], w_lru_conv[l],
            b_lru_conv[l], w_rg_a[l], b_rg_a[l], w_rg_x[l], b_rg_x[l], lru_lambda[l],
            g_mem[l], w_mem_kv[l], g_q_mem[l], g_k_mem[l], b_gate[l], w_branch[l],
            w_out[l], g_ffn[l], w_ffn_up[l], w_ffn_conv[l], b_ffn_conv[l], w_ffn_down[l])
    return x


_drawn_inputs = setup_inputs


def setup_inputs(seed=0):
    import zlib

    import numpy as np

    out = dict(_drawn_inputs(seed))
    spreads = {}
    factors = {'g_mix': 6.025,
     'g_q_fox': 8.0,
     'g_k_fox': 8.0,
     'b_lru_conv': 4.009,
     'b_rg_a': 50.786,
     'b_rg_x': 40.59,
     'g_mem': 8.0,
     'g_q_mem': 8.0,
     'g_k_mem': 8.0,
     'b_gate': 31.368,
     'g_ffn': 12.454,
     'b_ffn_conv': 25.305}
    for name, (base, spread) in spreads.items():
        noise = np.random.default_rng([zlib.crc32(name.encode()), seed]).standard_normal(out[name].shape)
        drawn = base * np.exp(spread * noise) if base else spread * noise
        out[name] = jnp.asarray(drawn.astype(out[name].dtype))
    for name, factor in factors.items():
        out[name] = (out[name] * factor).astype(out[name].dtype)
    return out
```

```python
from contextlib import ExitStack

import numpy as np
import concourse.bass as bass
from concourse import mybir

ALU = mybir.AluOpType
ACT = mybir.ActivationFunctionType
F32 = mybir.dt.float32
F32R = mybir.dt.float32r
AX_X = mybir.AxisListType.X

P = 128
T = 256
D = 2048
KT = D // P
BW = 1024
BT = BW // P
FFN = 5632
FT = FFN // P
EPS = 1e-6
UK, UC = 4, 256
DK, DC = 11, 128
SLOTS = 4
GELU_C, GELU_S = 0.044715, float(np.sqrt(2.0 / np.pi))
MASKED = -1e30

COL_Q, COL_K, COL_V, COL_FF = 0, BW, 2 * BW, 3 * BW
COL_LX = 3 * BW + 8
COL_LG, COL_MQ, COL_GATE = COL_LX + BW, COL_LX + 2 * BW, COL_LX + 3 * BW

PHASES = [("mv", 2, 4), ("mkq", 4, 4), ("lru", 4, 4), ("v", 2, 4), ("qk", 4, 4)]
for _q in range(4):
    PHASES += [(f"gate{_q}", 3, 4), (f"branch{_q}", 3, 2)]
PHASES += [("out", 4, 4), ("up", FT // 2, 4), ("down", KT // 2, 4)]
U0, G0 = {}, {}
GROUPS = []
_u = 0
for _name, _n, _per in PHASES:
    U0[_name], G0[_name] = _u, len(GROUPS)
    for _i in range(_n):
        for _w in range(2):
            GROUPS.append((_name, _i, _w, _u + _per - 1))
            _u += _per
U_ALL = _u

PAR = {}
_c = 0
for _name, _n in [("g_mix", KT), ("g_mem", KT), ("g_ffn", KT), ("b_gate", 3 * KT), ("w_fconv", 3 * 2 * FT),
                  ("b_fconv", 2 * FT), ("w_lconv", 4 * BT), ("b_lconv", BT), ("b_a", BT), ("b_x", BT),
                  ("lam", BT), ("g_q", 1), ("g_k", 1), ("g_qm", 2), ("g_km", 2), ("b_f", 1)]:
    PAR[_name] = _c
    _c += _n
N_PAR = _c

_ATTENTION = {
    "pe": ["sums", "scores", "transposes", "values"],
    "act": ["squares", "root", "exp", "weights_copied", "y_hi"],
    "dve": ["norm", "normed", "masked", "row_max", "row_inv", "weights", "y_lo"],
    "pool": ["values_staged"],
}
KINDS = [
    ("mem", 4, _ATTENTION),
    ("lru", 4, {
        "pe": ["gates"],
        "act": ["conv0", "gelu_square", "gate_tanh", "exps", "gelu_tanh", "root", "y_hi"],
        "dve": ["tap2", "tap1", "tap0", "log_a", "ix", "decay_sq", "u", "scan", "gelu", "y", "y_lo"],
        "pool": ["gelu_poly", "gelu_cube", "a_sq"],
    }),
    ("decay", 1, {
        "pe": ["logits", "turned"],
        "act": ["exp", "ln"],
        "dve": ["low", "padded", "z", "abs", "one_plus", "is_one", "minus_one", "inverse", "ratio", "ratio1",
                "log1p", "log_f", "c"],
        "pool": ["zeroed", "columns"],
    }),
    ("fox", 4, _ATTENTION),
]
LEN = {k: {e: len(s) for e, s in steps.items()} for k, _, steps in KINDS}
STEP = {k: {e: {n: j + 1 for j, n in enumerate(s)} for e, s in steps.items()} for k, _, steps in KINDS}
BASE, _sum = {}, {"pe": 0, "act": 0, "dve": 1, "pool": 0}
for _k, _n, _ in KINDS:
    BASE[_k] = dict(_sum)
    for _e in _sum:
        _sum[_e] += _n * LEN[_k][_e]
SIDE_ALL = dict(_sum)


def side_count(kind, m, engine, step):
    return m * LEN[kind][engine] + (BASE[kind][engine] + (STEP[kind][engine][step] if step else 0))


def at(const, i, coef):
    return const if i is None else i * coef + const


def hybrid_layer_kernel(nc, xT, memT, par, shapes_const, w_in, w_mem_kv, w_rg, w_branch, w_out, w_up, w_down, outT):
    with ExitStack() as ctx:
        KB = 1024
        SB0 = 16512
        TOP = 212856

        def sb(name, shape, offset, dt=F32):
            return nc.alloc_sbuf_tensor_at(name, shape, dt, offset=SB0 + int(offset))

        def sem(name):
            return ctx.enter_context(nc.semaphore(name))

        W = sb("W", [P, SLOTS, UK, 2, UC], 0, F32R)
        raw = sb("raw", [P, SLOTS, UK, UC], 32 * KB)
        X = sb("X", [P, KT, 2, T], 48 * KB, F32R)
        xs = sb("xs", [P, KT, T], 80 * KB)
        Y = sb("Y", [P, 3, BT, 2, T], 96 * KB, F32R)
        M0, G_0, T0 = 144 * KB, 176 * KB, 192 * KB
        XM = sb("XM", [P, KT, 2, T], M0, F32R)
        merged = sb("merged", [P, KT, 2, T], M0, F32R)
        mem_raw = sb("mem_raw", [P, KT, T], 96 * KB)
        mem_n = sb("mem_n", [P, KT, T], 112 * KB)
        x_n = sb("x_n", [P, KT, T], 128 * KB)
        sq0 = sb("sq0", [P, 2, UK, T], G_0 + 8 * KB)
        rstd0 = sb("rstd0", [P, 2, T], T0)
        ff_raw = sb("ff_raw", [P, KT, 8], T0 + 2 * KB)
        ff_w = sb("ff_w", [P, KT, 2, 8], T0 + 2.5 * KB, F32R)
        mem_v = sb("mem_v", [P, 2, BW], G_0)

        def attention_buffers(tag, base):
            names = [("k_raw", [P, 2, T]), ("q_raw", [P, 2, T]), ("k_n", [P, 2, T]), ("q_n", [P, 2, T]),
                     ("S", [P, 2, 2, T]), ("PT", [P, 2, 2, T]), ("v_cur", [P, 2, T])]
            out, o = {}, base
            for n, shape in names:
                out[n] = sb(f"{tag}_{n}", shape, o)
                if n == "PT":
                    out["rstd"] = sb(f"{tag}_rstd", [P, 2, 2, T], o)
                o += int(np.prod(shape[1:])) * 4
            return out

        att = {"mem": attention_buffers("mem", 96 * KB), "fox": attention_buffers("fox", M0)}
        v_all = sb("v_all", [P, 2, BW], M0 + 22784)
        lx_pad = sb("lx_pad", [P, 2, 3 + T], M0)
        _o = M0 + 2080
        lru = {}
        for n in ["lg", "rg", "xr", "ra", "a", "aa", "tn", "ix", "hs", "gg"]:
            shape = [P, 2, 2, P] if n == "rg" else [P, 2, T]
            lru[n] = sb(f"lru_{n}", shape, _o)
            _o += 2 * KB
        lhs_c = sb("lhs_c", [P, T], T0 + 4 * KB)
        dec = {n: sb(f"dec_{n}", [P, T], G_0 + (12 + j) * KB) for j, n in enumerate(["z", "e", "u", "r"])}
        ff_pad = sb("ff_pad", [P, 2, P], T0)
        ff_low = sb("ff_low", [P, 2, 8], T0 + 1 * KB)
        dec_l = sb("dec_l", [P, T], T0 + 2 * KB + 512)
        rhs_c = sb("rhs_c", [P, 8, T], G_0 + 4 * KB)
        gates = sb("gates", [P, 3, 2, 2, T], G_0)
        acc = sb("acc", [P, 2, 2, T], G_0 + 12 * KB)
        yd = sb("yd", [P, 2, T], T0 + 64)
        sq2 = sb("sq2", [P, 2, 2, T], G_0)
        sum2 = sb("sum2", [P, 2, T], G_0 + 4 * KB)
        rstd2 = sb("rstd2", [P, T], G_0 + 6 * KB)
        h2 = sb("h2", [P, KT, T], 96 * KB)
        hidden = sb("hidden", [P, FT, 2, T], 96 * KB, F32R)
        up_pad = {w: sb(f"up_pad{w}", [P, 2, 2 + T], 184 * KB + w * 2080) for w in range(2)}
        up_c = {w: sb(f"up_c{w}", [P, 2, T], 184 * KB + 4160 + w * 2048) for w in range(2)}
        low = sb("low", [P, 2, 2, T], T0 + 6 * KB)
        raw2 = sb("raw2", [P, SLOTS, DK, DC], 32 * KB)
        W2a = sb("W2a", [P, 2, DK, 2, DC], 0, F32R)
        W2b = sb("W2b", [P, 2, DK, 2, DC], 54 * KB, F32R)

        next_free = [202 * KB]

        def const_sb(name, shape):
            t = sb(name, shape, next_free[0])
            next_free[0] += -(-4 * int(np.prod(shape[1:])) // 32) * 32
            return t

        par_sb = const_sb("par_sb", [P, N_PAR])
        ident = const_sb("ident", [P, P])
        rows_sel = const_sb("rows_sel", [P, 10])
        mask = const_sb("mask", [P, 2, T])
        ones = const_sb("ones", [P, P])
        half_bg = const_sb("half_bg", [P, 3 * KT])
        half_ba = const_sb("half_ba", [P, BT])
        half_bx = const_sb("half_bx", [P, BT])
        ls4 = const_sb("ls4", [P, BT])
        g_s = const_sb("g_s", [P, 3, KT])
        gk_s = const_sb("gk_s", [P, 1])
        gkm_s = const_sb("gkm_s", [P, 2])
        stat = const_sb("stat", [P, 3, 4])
        eps = const_sb("eps", [P, 4])
        lam_t = {n: sb(f"lam_{n}", [P, BT], T0 + 3584 + 32 * j) for j, n in enumerate(["t", "e", "u", "m", "d", "l"])}
        assert next_free[0] <= TOP, next_free[0]

        psG = ctx.enter_context(nc.psum_tensor("psG", [P, 4, 512], F32))
        psM = ctx.enter_context(nc.psum_tensor("psM", [P, 4, 512], F32))

        raw_full = [sem(f"raw_full{s}") for s in range(SLOTS)]
        hi_done, lo_done = sem("hi_done"), sem("lo_done")
        pe_units = sem("pe_units")
        low_copied, evac_done = sem("low_copied"), sem("evac_done")
        side = {e: sem(f"side_{e}") for e in ("pe", "act", "dve", "pool")}
        mem_in = [sem(f"mem_in{c}") for c in range(4)]
        x_in = [sem(f"x_in{c}") for c in range(4)]
        par_in, const_in, ff_in, rg_in = sem("par_in"), sem("const_in"), sem("ff_in"), sem("rg_in")
        setup, ones_set = sem("setup"), sem("ones_set")
        sq_done, ss_done, rstd_done = sem("sq_done"), sem("ss_done"), sem("rstd_done")
        mem_scaled, x_scaled, x_gained = sem("mem_scaled"), sem("x_scaled"), sem("x_gained")
        memX_hi, memX_lo, xX_hi, xX_lo = sem("memX_hi"), sem("memX_lo"), sem("xX_hi"), sem("xX_lo")
        ff_hi, ff_lo = sem("ff_hi"), sem("ff_lo")
        lam_act, lam_dve = sem("lam_act"), sem("lam_dve")
        gate_ready = sem("gate_ready")
        gated, acc_added, merged_hi, merged_lo = sem("gated"), sem("acc_added"), sem("merged_hi"), sem("merged_lo")
        x2_done, x2_sq, x2_sum, x2_ss, root_done = sem("x2_done"), sem("x2_sq"), sem("x2_sum"), sem("x2_ss"), sem("root_done")
        h2_scaled, h2_hi, h2_lo = sem("h2_scaled"), sem("h2_hi"), sem("h2_lo")
        conv0, tap1, tap0, gelu_done = sem("conv0"), sem("tap1"), sem("tap0"), sem("gelu_done")
        prod_done, hidden_hi, hidden_lo = sem("prod_done"), sem("hidden_hi"), sem("hidden_lo")
        yd_free = sem("yd_free")
        out_stored = sem("out_stored")

        def p1(name, j, n=1):
            return par_sb[:, PAR[name] + j:PAR[name] + j + n]

        def par_at(name, j):
            return par_sb[:, bass.ds(j + PAR[name], 1)]

        def f32(ap):
            return ap.bitcast(F32)

        rows = lambda w: w.rearrange("(k p) c -> p k c", p=P)
        w_in_r, w_kv_r, w_br_r, w_out_r, w_up_r, w_down_r = map(rows, (w_in, w_mem_kv, w_branch, w_out, w_up, w_down))

        def unit_source(phase, i, k):
            if phase == "down":
                return w_down_r[:, (k % 4) * DK:(k % 4 + 1) * DK, bass.ds(i * (2 * DC) + (k // 4) * DC, DC)]
            if phase.startswith("branch"):
                q = int(phase[6:])
                return w_br_r[:, bass.ds(i * BT + (k % 2) * UK, UK), (2 * q + k // 2) * UC:(2 * q + k // 2 + 1) * UC]
            w, kk = k // 4, k % 4
            if phase.startswith("gate"):
                q = int(phase[4:])
                src, col = w_in_r, i * D + (COL_GATE + (2 * q + w) * UC)
            elif phase == "mv":
                src, col = w_kv_r, i * (2 * UC) + (BW + w * UC)
            elif phase == "mkq":
                src, col = (w_kv_r, i * UC) if w == 0 else (w_in_r, i * UC + COL_MQ)
            elif phase == "lru":
                src, col = w_in_r, i * UC + (COL_LX if w == 0 else COL_LG)
            elif phase == "v":
                src, col = w_in_r, i * (2 * UC) + (COL_V + w * UC)
            elif phase == "qk":
                src, col = w_in_r, i * UC + (COL_Q if w == 0 else COL_K)
            elif phase == "out":
                src, col = w_out_r, i * (2 * UC) + w * UC
            else:
                src, col = w_up_r, i * UC + w * FFN
            return src[:, kk * UK:(kk + 1) * UK, bass.ds(col, UC)]

        def w2(s):
            return (W2a if s < 2 else W2b)[:, s % 2]

        block = ctx.enter_context(nc.Block())

        @block.sync
        def _(sp):
            def load(phase, i, k, u, coef):
                s = u % SLOTS
                if i is not None or u >= SLOTS:
                    sp.wait_ge(lo_done, at(u - 3, i, coef))
                dst = raw2[:, s] if phase == "down" else raw[:, s]
                sp.dma_start(dst, unit_source(phase, 0 if i is None else i, k)).then_inc(raw_full[s], 16)

            mem_r = memT.rearrange("(k p) t -> p k t", p=P)
            x_r = xT.rearrange("(k p) t -> p k t", p=P)
            for c in range(4):
                sp.dma_start(mem_raw[:, 4 * c:4 * c + 4], mem_r[:, 4 * c:4 * c + 4]).then_inc(mem_in[c], 16)
            sp.dma_start(par_sb[:], par).then_inc(par_in, 16)
            for k in range(4):
                load("mv", None, k, k, 0)
            for c in range(4):
                sp.dma_start(xs[:, 4 * c:4 * c + 4], x_r[:, 4 * c:4 * c + 4]).then_inc(x_in[c], 16)
            sp.dma_start(rows_sel[:], shapes_const[:, P + 2 * T:]).then_inc(const_in, 16)
            sp.dma_start(ident[:], shapes_const[:, 0:P]).then_inc(const_in, 16)
            sp.dma_start(mask[:], shapes_const[:, P:P + 2 * T].rearrange("p (a t) -> p a t", a=2)).then_inc(const_in, 16)
            sp.dma_start(ff_raw[:], w_in_r[:, :, COL_FF:COL_FF + 8]).then_inc(ff_in, 16)
            for k in range(4, 8):
                load("mv", None, k, k, 0)
            for name, n, per in PHASES:
                first = 1 if name == "mv" else 0
                if name == "down":
                    sp.wait_ge(lo_done, U0["down"])
                    for k in range(4):
                        if k == 2:
                            sp.wait_ge(pe_units, U0["down"])
                        sp.dma_start(raw2[:, k], unit_source("down", 0, k)).then_inc(raw_full[k], 16)
                    for k in range(4, 8):
                        load("down", None, k, U0["down"] + k, 0)
                    first = 1
                with sp.Fori(first, n) as i:
                    for k in range(2 * per):
                        load(name, i, k, U0[name] + k, 2 * per)

        @block.tensor
        def _(pe):
            def mm(*a, **kw):
                return nc.tensor.matmul(*a, skip_group_check=True, **kw)

            def group(phase, i, w, operand, hooks, per=4, coef=8, rows_major=False, ready=None):
                b = 2 * w
                g = G0[phase] + w
                if i is not None or g >= 2:
                    pe.wait_ge(evac_done, at(g - 1, i, 2))
                last = per * UK - 1
                for n in range(per):
                    u = U0[phase] + per * w + n
                    s = u % SLOTS
                    pe.wait_ge(lo_done, at(u + 1, i, coef))
                    if ready is not None:
                        ready(n)
                    for k in range(UK):
                        kt = n * UK + k
                        x_hl = operand(kt)
                        for t in range(2):
                            ts = slice(t * P, t * P + P)
                            if rows_major:
                                mm(psG[:, b + t, :], x_hl[:, 0, ts], W[:, s, k], start=kt == 0, stop=False)
                                ins = mm(psG[:, b + t, T:], x_hl[:, 1, ts], W[:, s, k, 0], start=False, stop=kt == last)
                            else:
                                mm(psG[:, b + t, :], W[:, s, k, 0, ts], x_hl, start=kt == 0, stop=False)
                                ins = mm(psG[:, b + t, T:], W[:, s, k, 1, ts], x_hl[:, 0], start=False, stop=kt == last)
                    ins.then_inc(pe_units, 1)
                    if per * w + n in hooks:
                        hooks[per * w + n]()

            def side_waits(**need):
                for e, v in need.items():
                    pe.wait_ge(side[e], v)

            def done(ins):
                ins.then_inc(side["pe"], 1)

            def attention_hooks(kind, m):
                A = att[kind]

                def sums():
                    side_waits(act=side_count(kind, m, "act", "squares"), dve=side_count(kind, m, "dve", None))
                    for j in range(2):
                        if kind == "fox":
                            ins = mm(psM[:, j, :], ones[:], A["S"][:, j].rearrange("p a t -> p (a t)"), start=True, stop=True)
                        else:
                            for t in range(2):
                                ins = mm(psM[:, 0, j * T:(j + 1) * T], ones[:], A["S"][:, j, t], start=t == 0, stop=t == 1)
                    done(ins)

                def scores():
                    side_waits(dve=side_count(kind, m, "dve", "normed"))
                    if kind == "fox":
                        side_waits(pool=side_count("decay", 0, "pool", "columns"))
                    for qt in range(2):
                        qs = slice(qt * P, qt * P + P)
                        if kind == "fox":
                            for h in range(2):
                                mm(psM[:, 2 + h, qt * T:(qt + 1) * T], A["q_n"][:, h, qs], A["k_n"][:, h], start=True, stop=False)
                                ins = mm(psM[:, 2 + h, qt * T:(qt + 1) * T], lhs_c[:, qs],
                                         rhs_c[:, bass.ds(m * 2 + h, 1), :].rearrange("p a t -> p (a t)"), start=False, stop=True)
                        else:
                            for t in range(2):
                                ins = mm(psM[:, 2, qt * T:(qt + 1) * T], A["q_n"][:, t, qs], A["k_n"][:, t],
                                         start=t == 0, stop=t == 1)
                    done(ins)

                def transposes():
                    side_waits(dve=side_count(kind, m, "dve", "weights"))
                    if kind == "mem":
                        pe.wait_ge(const_in, 48)
                    for h in range(2 if kind == "fox" else 1):
                        for kt in range(2):
                            for qt in range(2):
                                o = kt * T + qt * P
                                ins = nc.tensor.transpose(psM[:, h, o:o + P], A["S"][:, h, qt, kt * P:kt * P + P], ident[:])
                    done(ins)

                def values():
                    side_waits(act=side_count(kind, m, "act", "weights_copied"),
                               pool=side_count(kind, m, "pool", "values_staged"))
                    for t in range(2):
                        for kt in range(2):
                            ins = mm(psM[:, 2, t * T:(t + 1) * T], A["v_cur"][:, kt, t * P:t * P + P],
                                     A["PT"][:, t if kind == "fox" else 0, kt], start=kt == 0, stop=kt == 1)
                    done(ins)

                return {0: sums, 2: scores, 4: transposes, 5: values}

            def lru_hooks(m):
                def gates_():
                    pe.wait_ge(rg_in, at(32, m, 32))
                    side_waits(dve=side_count("lru", m, "dve", "tap0"))
                    for j in range(2):
                        for b in range(2):
                            ins = mm(psM[:, j, b * T:(b + 1) * T], lru["rg"][:, j, b], lru["xr"][:, b], start=True, stop=True)
                    done(ins)
                return {1: gates_}

            def decay_hooks():
                def logits():
                    side_waits(dve=side_count("decay", 0, "dve", None), act=side_count("decay", 0, "act", None))
                    pe.wait_ge(ff_lo, 1)
                    for tt in range(2):
                        ts = slice(tt * P, tt * P + P)
                        for kt in range(KT):
                            mm(psM[:, 0, tt * 16:tt * 16 + 16], X[:, kt, 0, ts], ff_w[:, kt], start=kt == 0, stop=False)
                            ins = mm(psM[:, 0, tt * 16 + 8:tt * 16 + 16], X[:, kt, 1, ts], ff_w[:, kt, 0], start=False,
                                     stop=kt == KT - 1)
                    done(ins)

                def turned():
                    side_waits(dve=side_count("decay", 0, "dve", "padded"))
                    for tt in range(2):
                        ins = nc.tensor.transpose(psM[:, 1, tt * P:tt * P + P], ff_pad[:, tt], ident[:])
                    done(ins)
                return {0: logits, 3: turned}

            x_op = lambda kt: X[:, kt]
            m_op = lambda kt: XM[:, kt]

            pe.wait_ge(ones_set, 1)
            for j in range(2):
                for c in range(4):
                    pe.wait_ge(sq_done, 4 * j + c + 1)
                    for k in range(UK):
                        ins = mm(psM[:, j, 0:T], ones[:], sq0[:, c % 2, k], start=c == 0 and k == 0, stop=c == 3 and k == 3)
                    ins.then_inc(ss_done, 1)
                if j == 0:
                    def mem_ready(n):
                        pe.wait_ge(memX_lo, n + 1)
                    group("mv", None, 0, m_op, {}, rows_major=True, ready=mem_ready)
            group("mv", None, 1, m_op, {}, rows_major=True)
            with pe.Fori(1, 2) as i:
                for w in range(2):
                    group("mv", i, w, m_op, {}, rows_major=True)

            def mkq(i, hooks):
                group("mkq", i, 0, m_op, hooks)
                group("mkq", i, 1, x_op, hooks, ready=lambda n: pe.wait_ge(xX_lo, n + 1))

            def plain(phase, i, hooks, operand=x_op, **kw):
                for w in range(2):
                    group(phase, i, w, operand, hooks, **kw)

            mkq(None, {})
            with pe.Fori(1, 4) as i:
                mkq(i, attention_hooks("mem", i - 1))
            plain("lru", None, attention_hooks("mem", 3))
            with pe.Fori(1, 4) as i:
                plain("lru", i, lru_hooks(i - 1))
            plain("v", None, lru_hooks(3), rows_major=True)
            with pe.Fori(1, 2) as i:
                plain("v", i, decay_hooks(), rows_major=True)
            plain("qk", None, {})
            with pe.Fori(1, 4) as i:
                plain("qk", i, attention_hooks("fox", i - 1))
            plain("gate0", None, attention_hooks("fox", 3))

            def quarter_waits():
                pass

            for q in range(4):
                with pe.Fori(1 if q == 0 else 0, 3) as i:
                    plain(f"gate{q}", i, {})
                if q == 0:
                    pe.wait_ge(side["dve"], SIDE_ALL["dve"])
                with pe.Fori(0, 3) as n:
                    for w in range(2):
                        group(f"branch{q}", n, w,
                              lambda kt: Y[:, bass.ds(n, 1), kt].rearrange("p a h t -> p (a h) t"),
                              {}, per=2, coef=4)
            pe.wait_ge(merged_lo, 8)
            with pe.Fori(0, 4) as i:
                plain("out", i, {}, operand=lambda kt: merged[:, kt])

            pe.wait_ge(x2_sum, 8)
            for t in range(2):
                ins = mm(psM[:, 0, 0:T], ones[:], sum2[:, t], start=t == 0, stop=t == 1)
            ins.then_inc(x2_ss, 1)
            with pe.Fori(0, FT // 2) as i:
                plain("up", i, {}, ready=lambda n: pe.wait_ge(h2_lo, n + 1))

            pe.wait_ge(hidden_lo, FT // 2)
            with pe.Fori(0, KT // 2) as i:
                for w in range(2):
                    g = G0["down"] + w
                    pe.wait_ge(evac_done, at(g - 1, i, 2))
                    for n in range(4):
                        u = U0["down"] + 4 * w + n
                        pe.wait_ge(lo_done, at(u + 1, i, 8))
                        for k in range(DK):
                            kt = n * DK + k
                            mm(psG[:, 2 * w, :], w2(n)[:, k, 0], hidden[:, kt], start=kt == 0, stop=False)
                            ins = mm(psG[:, 2 * w, T:], w2(n)[:, k, 1], hidden[:, kt, 0], start=False, stop=kt == FT - 1)
                        ins.then_inc(pe_units, 1)

        evac_at = {last + 4: (g, ph, i, w) for g, (ph, i, w, last) in enumerate(GROUPS) if last + 4 <= U0["up"] + 3}

        def build_hooks(table):
            where = {}
            starts = {"mem": [U0["mkq"] + 8 * (m + 1) for m in range(4)],
                      "lru": [U0["lru"] + 8 * (m + 1) for m in range(4)],
                      "decay": [U0["v"] + 8],
                      "fox": [U0["qk"] + 8 * (m + 1) for m in range(4)]}
            for kind, offs in table.items():
                for m, s in enumerate(starts[kind]):
                    for o, steps in offs.items():
                        for f in steps:
                            where.setdefault(s + o, []).append((f, kind, m))
            return where

        @block.scalar
        def _(act):
            def split(phase, u, i=None, coef=8):
                s = u % SLOTS
                act.wait_ge(raw_full[s], at(16 * (u // SLOTS + 1), i, 16 * coef // SLOTS))
                if phase == "down":
                    if u < U0["down"] + SLOTS:
                        act.wait_ge(pe_units, U0["down"] + (-2, -1, 0, 0)[s] if i is None else 0)
                    else:
                        act.wait_ge(pe_units, at(u - 3, i, coef))
                    nc.scalar.activation(w2(s)[:, :, 0], raw2[:, s], ACT.Copy).then_inc(hi_done, 1)
                    return
                if u >= SLOTS:
                    act.wait_ge(pe_units, at(u - 3, i, coef))
                nc.scalar.activation(W[:, s, :, 0], raw[:, s], ACT.Copy).then_inc(hi_done, 1)

            def copy_low(g, last, i=None, banks=2, coef=8):
                act.wait_ge(pe_units, at(last + 1, i, coef))
                if g >= 2:
                    act.wait_ge(evac_done, at(g - 1, i, 2))
                b = 2 * (g % 2)
                nc.scalar.activation(low[:, g % 2, 0:banks], psG[:, b:b + banks, T:], ACT.Copy).then_inc(low_copied, 1)

            def wait(**need):
                for e, v in need.items():
                    act.wait_ge(side[e], v)

            def done(ins):
                ins.then_inc(side["act"], 1)

            def squares(kind, m):
                A = att[kind]
                own = G0["mkq" if kind == "mem" else "qk"] + 2 * m + 1
                act.wait_ge(evac_done, own + 1)
                wait(**{e: side_count(kind, m, e, None) for e in ("pe", "dve", "act")})
                nc.scalar.activation(A["S"][:, 0], A["k_raw"][:], ACT.Square)
                done(nc.scalar.activation(A["S"][:, 1], A["q_raw"][:], ACT.Square))

            def root(kind, m):
                A = att[kind]
                wait(pe=side_count(kind, m, "pe", "sums"))
                if kind == "mem":
                    src, dst, bias = psM[:, 0, :], A["rstd"][:, 0].rearrange("p a t -> p (a t)"), eps[:, 1:2]
                else:
                    src, dst, bias = psM[:, 0:2, :], A["rstd"].rearrange("p j a t -> p j (a t)"), eps[:, 2:3]
                done(nc.scalar.activation(dst, src, ACT.Sqrt, bias=bias))

            def exp(kind, m):
                A = att[kind]
                wait(dve=side_count(kind, m, "dve", "row_max"))
                n = 0
                for h in range(2 if kind == "fox" else 1):
                    for qt in range(2):
                        src = A["S"][:, h, qt] if kind == "fox" else psM[:, 2, qt * T:(qt + 1) * T]
                        ins = nc.scalar.activation(A["S"][:, h, qt], src, ACT.Exp, bias=stat[:, 0, n:n + 1], scale=1.0,
                                                   accum_out=stat[:, 1, n:n + 1])
                        n += 1
                done(ins)

            def weights_copied(kind, m):
                A = att[kind]
                wait(pe=side_count(kind, m, "pe", "transposes"))
                H = 2 if kind == "fox" else 1
                done(nc.scalar.activation(A["PT"][:, 0:H].rearrange("p h k t -> p h (k t)"), psM[:, 0:H, :], ACT.Copy))

            def attention_hi(kind, m):
                wait(pe=side_count(kind, m, "pe", "values"))
                br = 0 if kind == "fox" else 2
                done(nc.scalar.activation(Y[:, br, 2 * m:2 * m + 2, 0, :], psM[:, 2, :].rearrange("p (a t) -> p a t", a=2),
                                          ACT.Copy))

            L = lru

            def conv0_(kind, m):
                wait(**{e: side_count("lru", m, e, None) for e in ("pe", "dve", "act", "pool")})
                act.wait_ge(evac_done, G0["lru"] + 2 * m + 1)
                for b in range(2):
                    ins = nc.scalar.activation(L["xr"][:, b], lx_pad[:, b, 3:], ACT.Identity,
                                               bias=p1("b_lconv", 2 * m + b), scale=p1("w_lconv", 3 * BT + 2 * m + b))
                done(ins)

            def gelu_square(kind, m):
                act.wait_ge(evac_done, G0["lru"] + 2 * m + 2)
                done(nc.scalar.activation(L["gg"][:], L["lg"][:], ACT.Square))

            def gate_tanh(kind, m):
                wait(pe=side_count("lru", m, "pe", "gates"))
                for j, (n, hb) in enumerate([("ra", half_ba), ("ix", half_bx)]):
                    for b in range(2):
                        ins = nc.scalar.activation(L[n][:, b], psM[:, j, b * T:(b + 1) * T], ACT.Tanh, scale=0.5,
                                                   bias=hb[:, 2 * m + b:2 * m + b + 1])
                done(ins)

            def exps(kind, m):
                wait(dve=side_count("lru", m, "dve", "log_a"))
                nc.scalar.activation(L["a"][:], L["ra"][:], ACT.Exp)
                done(nc.scalar.activation(L["tn"][:], L["ra"][:], ACT.Tanh, scale=-1.0))

            def gelu_tanh(kind, m):
                wait(pool=side_count("lru", m, "pool", "gelu_cube"))
                done(nc.scalar.activation(L["gg"][:], L["gg"][:], ACT.Tanh, scale=GELU_S))

            def lru_root(kind, m):
                wait(dve=side_count("lru", m, "dve", "decay_sq"))
                done(nc.scalar.activation(L["aa"][:], L["aa"][:], ACT.Sqrt, scale=0.25, bias=eps[:, 3:4]))

            def lru_hi(kind, m):
                wait(dve=side_count("lru", m, "dve", "y"))
                done(nc.scalar.activation(Y[:, 1, 2 * m:2 * m + 2, 0, :], L["hs"][:], ACT.Copy))

            def decay_exp(kind, m):
                wait(dve=side_count("decay", 0, "dve", "abs"))
                done(nc.scalar.activation(dec["e"][:], dec["r"][:], ACT.Exp, scale=-1.0))

            def decay_ln(kind, m):
                wait(dve=side_count("decay", 0, "dve", "one_plus"))
                done(nc.scalar.activation(dec_l[:], dec["u"][:], ACT.Ln))

            attention = {3: [squares], 4: [root], 6: [exp], 8: [weights_copied], 9: [attention_hi]}
            hooks = build_hooks({"mem": attention, "fox": attention,
                                 "lru": {3: [conv0_, gelu_square], 5: [gate_tanh], 6: [exps, gelu_tanh], 7: [lru_root], 9: [lru_hi]},
                                 "decay": {7: [decay_exp, decay_ln]}})

            def token_root(dst, src):
                nc.scalar.activation(dst, src, ACT.Sqrt, bias=eps[:, 0:1]).then_inc(root_done, 1)

            act.wait_ge(par_in, 16)
            for c in range(4):
                act.wait_ge(mem_in[c], 16)
                if c >= 2:
                    act.wait_ge(ss_done, c - 1)
                nc.scalar.activation(sq0[:, c % 2], mem_raw[:, 4 * c:4 * c + 4], ACT.Square).then_inc(sq_done, 1)
            act.wait_ge(ones_set, 1)
            act.wait_ge(ss_done, 4)
            token_root(rstd0[:, 0], psM[:, 0, 0:T])
            for k in range(2):
                split("mv", k)
            for c in range(4):
                act.wait_ge(mem_scaled, c + 1)
                nc.scalar.activation(XM[:, 4 * c:4 * c + 4, 0, :], mem_n[:, 4 * c:4 * c + 4], ACT.Copy).then_inc(memX_hi, 1)
                if c < 2:
                    split("mv", c + 2)
            for c in range(4):
                act.wait_ge(x_in[c], 16)
                act.wait_ge(ss_done, min(3 + c, 4 + c - 1) if c < 2 else 4 + c - 1)
                nc.scalar.activation(sq0[:, c % 2], xs[:, 4 * c:4 * c + 4], ACT.Square).then_inc(sq_done, 1)
            act.wait_ge(ss_done, 8)
            token_root(rstd0[:, 1], psM[:, 1, 0:T])
            act.wait_ge(ff_in, 16)
            nc.scalar.activation(ff_w[:, :, 0, :], ff_raw[:], ACT.Copy).then_inc(ff_hi, 1)
            act.wait_ge(lam_dve, 1)
            nc.scalar.activation(lam_t["e"][:], lam_t["t"][:], ACT.Exp, scale=-1.0).then_inc(lam_act, 1)
            act.wait_ge(lam_dve, 2)
            nc.scalar.activation(lam_t["l"][:], lam_t["u"][:], ACT.Ln).then_inc(lam_act, 1)

            for u in range(4, U0["up"] + 4):
                if u in evac_at:
                    g, ph, i, w = evac_at[u]
                    copy_low(g, u - 4)
                split("", u)
                if 8 <= u < 12:
                    c = u - 8
                    act.wait_ge(x_gained, c + 1)
                    nc.scalar.activation(X[:, 4 * c:4 * c + 4, 0, :], x_n[:, 4 * c:4 * c + 4], ACT.Copy).then_inc(xX_hi, 1)
                for f, kind, m in hooks.get(u, []):
                    f(kind, m)
                if u in evac_at:
                    if ph.startswith("gate"):
                        q = int(ph[4:])
                        act.wait_ge(evac_done, g + 1)
                        for t in range(2):
                            j = i * KT + 4 * q + 2 * w + t
                            ins = nc.scalar.activation(gates[:, i, w, t], gates[:, i, w, t], ACT.Tanh, scale=0.5,
                                                       bias=half_bg[:, j:j + 1])
                        ins.then_inc(gate_ready, 1)
                    if ph.startswith("branch") and i == 2:
                        q = int(ph[6:])
                        act.wait_ge(acc_added, 4 * q + 3 + w)
                        r = 4 * q + 2 * w
                        nc.scalar.activation(merged[:, r:r + 2, 0, :], acc[:, w], ACT.Copy, scale=0.5).then_inc(merged_hi, 1)
                    if ph == "out":
                        n = 2 * i + w
                        act.wait_ge(x2_done, n + 1)
                        if n >= 2:
                            act.wait_ge(x2_sum, n - 1)
                        nc.scalar.activation(sq2[:, n % 2], xs[:, 2 * n:2 * n + 2], ACT.Square).then_inc(x2_sq, 1)
            act.wait_ge(x2_ss, 1)
            token_root(rstd2[:], psM[:, 0, 0:T])
            for c in range(4):
                act.wait_ge(h2_scaled, c + 1)
                nc.scalar.activation(X[:, 4 * c:4 * c + 4, 0, :], h2[:, 4 * c:4 * c + 4], ACT.Copy).then_inc(h2_hi, 1)

            def up_conv0(i, w):
                act.wait_ge(evac_done, at(G0["up"] + w + 1, i, 2))
                for t in range(2):
                    ins = nc.scalar.activation(up_c[w][:, t], up_pad[w][:, t, 2:], ACT.Identity,
                                               bias=par_at("b_fconv", i * 2 + (w * FT + t)),
                                               scale=par_at("w_fconv", i * 2 + (2 * 2 * FT + w * FT + t)))
                ins.then_inc(conv0, 1)

            def up_iteration(i, split_next):
                U = U0["up"]
                for k in range(4, 7):
                    split("up", U + k, i)
                copy_low(G0["up"], U + 3, i)
                split("up", U + 7, i)
                up_conv0(i, 0)
                split_next(0)
                act.wait_ge(tap0, i * 2 + 1)
                nc.scalar.activation(up_c[0][:], up_c[0][:], ACT.Gelu_apprx_tanh).then_inc(gelu_done, 1)
                split_next(1)
                split_next(2)
                copy_low(G0["up"] + 1, U + 7, i)
                split_next(3)
                up_conv0(i, 1)
                act.wait_ge(prod_done, i + 1)
                nc.scalar.activation(hidden[:, bass.ds(i * 2, 2), 0, :], up_c[1][:], ACT.Copy).then_inc(hidden_hi, 1)

            with act.Fori(0, FT // 2 - 1) as i:
                up_iteration(i, lambda k: split("up", U0["up"] + 8 + k, i))
            with act.Fori(FT // 2 - 1, FT // 2) as i:
                up_iteration(i, lambda k: split("down", U0["down"] + k))

            def down_iteration(i, more):
                U = U0["down"]
                for k in range(4, 7):
                    split("down", U + k, i)
                copy_low(G0["down"], U + 3, i, banks=1)
                split("down", U + 7, i)
                if more:
                    for k in range(8, 11):
                        split("down", U + k, i)
                copy_low(G0["down"] + 1, U + 7, i, banks=1)
                if more:
                    split("down", U + 11, i)

            with act.Fori(0, KT // 2 - 1) as i:
                down_iteration(i, True)
            with act.Fori(KT // 2 - 1, KT // 2) as i:
                down_iteration(i, False)

        @block.vector
        def _(dve):
            V = nc.vector

            def split(phase, u, i=None, coef=8):
                s = u % SLOTS
                dve.wait_ge(hi_done, at(u + 1, i, coef))
                if phase == "down":
                    V.tensor_tensor(w2(s)[:, :, 1], raw2[:, s], f32(w2(s)[:, :, 0]), ALU.subtract).then_inc(lo_done, 1)
                else:
                    V.tensor_tensor(W[:, s, :, 1], raw[:, s], f32(W[:, s, :, 0]), ALU.subtract).then_inc(lo_done, 1)

            def add_low(g, dst, i=None, banks=2):
                dve.wait_ge(low_copied, at(g + 1, i, 2))
                b = 2 * (g % 2)
                V.tensor_tensor(dst, psG[:, b:b + banks, 0:T], low[:, g % 2, 0:banks], ALU.add).then_inc(evac_done, 1)

            def wait(**need):
                for e, v in need.items():
                    dve.wait_ge(side[e], v)

            def done(ins):
                ins.then_inc(side["dve"], 1)

            def chained(kind, m, step):
                dve.wait_ge(side["dve"], side_count(kind, m, "dve", step))

            def norm(kind, m):
                A = att[kind]
                n = 1 if kind == "mem" else 2
                wait(act=side_count(kind, m, "act", "root"))
                rstd = A["rstd"][:, 0:n].rearrange("p j a t -> p (j a t)")
                done(V.reciprocal(rstd, rstd))

            def normed(kind, m):
                A = att[kind]
                chained(kind, m, "norm")
                if kind == "mem":
                    for t in range(2):
                        V.scalar_tensor_tensor(A["k_n"][:, t], A["k_raw"][:, t], gkm_s[:, t:t + 1], A["rstd"][:, 0, 0], ALU.mult, ALU.mult)
                        ins = V.scalar_tensor_tensor(A["q_n"][:, t], A["q_raw"][:, t], p1("g_qm", t), A["rstd"][:, 0, 1], ALU.mult, ALU.mult)
                else:
                    V.scalar_tensor_tensor(A["k_n"][:], A["k_raw"][:], gk_s[:, 0:1], A["rstd"][:, 0], ALU.mult, ALU.mult)
                    ins = V.scalar_tensor_tensor(A["q_n"][:], A["q_raw"][:], p1("g_q", 0), A["rstd"][:, 1], ALU.mult, ALU.mult)
                done(ins)

            def masked(kind, m):
                A = att[kind]
                wait(pe=side_count(kind, m, "pe", "scores"))
                if kind == "mem":
                    done(V.memset(stat[:, 2], 0.0))
                    return
                for h in range(2):
                    ins = V.tensor_tensor(A["S"][:, h].rearrange("p a t -> p (a t)"), psM[:, 2 + h, :], mask.rearrange("p a t -> p (a t)"), ALU.add)
                done(ins)

            def row_max(kind, m):
                A = att[kind]
                chained(kind, m, "masked")
                if kind == "mem":
                    done(V.tensor_reduce(stat[:, 0, 0:2], psM[:, 2, :].rearrange("p (a t) -> p a t", a=2), AX_X, ALU.max, negate=True))
                else:
                    done(V.tensor_reduce(stat[:, 0, 0:4], A["S"].rearrange("p h a t -> p (h a) t"), AX_X, ALU.max, negate=True))

            def row_inv(kind, m):
                wait(act=side_count(kind, m, "act", "exp"))
                n = 4 if kind == "fox" else 2
                done(V.reciprocal(stat[:, 2, 0:n], stat[:, 1, 0:n]))

            def weights(kind, m):
                A = att[kind]
                chained(kind, m, "row_inv")
                n = 0
                for h in range(2 if kind == "fox" else 1):
                    for qt in range(2):
                        ins = V.tensor_scalar(A["S"][:, h, qt], A["S"][:, h, qt], stat[:, 2, n:n + 1], None, ALU.mult)
                        n += 1
                done(ins)

            def attention_lo(kind, m):
                wait(act=side_count(kind, m, "act", "y_hi"))
                br = 0 if kind == "fox" else 2
                ys = Y[:, br, 2 * m:2 * m + 2]
                done(V.tensor_tensor(ys[:, :, 1, :], psM[:, 2, :].rearrange("p (a t) -> p a t", a=2), f32(ys[:, :, 0, :]), ALU.subtract))

            L = lru

            def taps(kind, m):
                for n, name in ((2, "tap2"), (1, "tap1"), (0, "tap0")):
                    if n == 2:
                        wait(act=side_count("lru", m, "act", "conv0"))
                    else:
                        chained("lru", m, f"tap{n + 1}")
                    for b in range(2):
                        ins = V.scalar_tensor_tensor(L["xr"][:, b], lx_pad[:, b, n:n + T], p1("w_lconv", n * BT + 2 * m + b),
                                                     L["xr"][:, b], ALU.mult, ALU.add)
                    done(ins)

            def log_a(kind, m):
                wait(act=side_count("lru", m, "act", "gate_tanh"))
                for b in range(2):
                    ins = V.tensor_scalar(L["ra"][:, b], L["ra"][:, b], 1.0, ls4[:, 2 * m + b:2 * m + b + 1], ALU.add, ALU.mult)
                done(ins)
                done(V.scalar_tensor_tensor(L["ix"][:], L["ix"][:], 1.0, L["xr"][:], ALU.add, ALU.mult))

            def decay_sq(kind, m):
                wait(pool=side_count("lru", m, "pool", "a_sq"), act=side_count("lru", m, "act", "exps"))
                done(V.scalar_tensor_tensor(L["aa"][:], L["aa"][:], 1.0, L["tn"][:], ALU.add, ALU.mult))

            def recurrence(kind, m):
                wait(act=side_count("lru", m, "act", "root"))
                done(V.tensor_tensor(L["ix"][:], L["ix"][:], L["aa"][:], ALU.mult))
                chained("lru", m, "u")
                for b in range(2):
                    ins = V.tensor_tensor_scan(out=L["hs"][:, b], data0=L["a"][:, b], data1=L["ix"][:, b], initial=0.0,
                                               op0=ALU.mult, op1=ALU.add)
                done(ins)

            def gated_y(kind, m):
                wait(act=side_count("lru", m, "act", "gelu_tanh"))
                done(V.scalar_tensor_tensor(L["gg"][:], L["gg"][:], 1.0, L["lg"][:], ALU.add, ALU.mult))
                chained("lru", m, "gelu")
                done(V.scalar_tensor_tensor(L["hs"][:], L["hs"][:], 0.5, L["gg"][:], ALU.mult, ALU.mult))

            def lru_lo(kind, m):
                wait(act=side_count("lru", m, "act", "y_hi"))
                ys = Y[:, 1, 2 * m:2 * m + 2]
                done(V.tensor_tensor(ys[:, :, 1, :], L["hs"][:], f32(ys[:, :, 0, :]), ALU.subtract))

            def decay_a(kind, m):
                wait(pe=side_count("decay", 0, "pe", "logits"))
                part = psM[:, 0, 0:32].rearrange("p (a c) -> p a c", a=2)
                done(V.tensor_copy(ff_low[:], part[:, :, 8:16]))
                chained("decay", 0, "low")
                wait(pool=side_count("decay", 0, "pool", "zeroed"))
                V.tensor_tensor(ff_pad[:, :, 0:8], part[:, :, 0:8], ff_low[:], ALU.add)
                done(V.tensor_tensor(ff_pad[:, :, 32:40], part[:, :, 0:8], ff_low[:], ALU.add))

            def decay_b(kind, m):
                wait(pe=side_count("decay", 0, "pe", "turned"))
                done(V.tensor_scalar(dec["z"][:], psM[:, 1, 0:T], p1("b_f", 0), None, ALU.add))
                chained("decay", 0, "z")
                done(V.scalar_tensor_tensor(dec["r"][:], dec["z"][:], -1.0, dec["z"][:], ALU.mult, ALU.max))
                wait(act=side_count("decay", 0, "act", "exp"))
                done(V.tensor_scalar(dec["u"][:], dec["e"][:], 1.0, None, ALU.add))

            def decay_c(kind, m):
                chained("decay", 0, "one_plus")
                done(V.tensor_scalar(dec["r"][:], dec["u"][:], 1.0, None, ALU.is_equal))
                chained("decay", 0, "is_one")
                wait(act=side_count("decay", 0, "act", "ln"))
                done(V.scalar_tensor_tensor(dec["u"][:], dec["u"][:], -1.0, dec["r"][:], ALU.add, ALU.add))
                chained("decay", 0, "minus_one")
                done(V.reciprocal(dec["u"][:], dec["u"][:]))
                chained("decay", 0, "inverse")
                done(V.tensor_tensor(dec["u"][:], dec["u"][:], dec_l[:], ALU.mult))
                chained("decay", 0, "ratio")
                done(V.tensor_tensor(dec["u"][:], dec["u"][:], dec["r"][:], ALU.add))
                chained("decay", 0, "ratio1")
                done(V.tensor_tensor(dec["e"][:], dec["u"][:], dec["e"][:], ALU.mult))
                chained("decay", 0, "log1p")
                done(V.scalar_tensor_tensor(dec["z"][:], dec["z"][:], 0.0, dec["e"][:], ALU.min, ALU.subtract))
                chained("decay", 0, "log_f")
                V.memset(dec["r"][:], 1.0).then_inc(setup, 1)
                dve.wait_ge(setup, 2)
                done(V.tensor_tensor_scan(out=dec["u"][:], data0=dec["r"][:], data1=dec["z"][:], initial=0.0,
                                          op0=ALU.mult, op1=ALU.add))

            attention = {4: [norm, normed], 6: [masked, row_max], 7: [row_inv, weights], 9: [attention_lo]}
            hooks = build_hooks({"mem": attention, "fox": attention,
                                 "lru": {4: [taps], 6: [log_a], 7: [decay_sq], 8: [recurrence, gated_y], 9: [lru_lo]},
                                 "decay": {5: [decay_a], 7: [decay_b], 8: [decay_c]}})

            for j, e in enumerate((D * EPS, 256 * EPS, 128 * EPS, 1e-33)):
                V.memset(eps[:, j:j + 1], e)
            V.memset(ones[:], 1.0).then_inc(ones_set, 1)
            dve.wait_ge(par_in, 16)
            for j, n in enumerate(("g_mix", "g_mem", "g_ffn")):
                V.tensor_scalar(g_s[:, j], p1(n, 0, KT), float(np.sqrt(D)), None, ALU.mult)
            V.tensor_scalar(gk_s[:], p1("g_k", 0), float(np.sqrt(128)), None, ALU.mult)
            V.tensor_scalar(gkm_s[:], p1("g_km", 0, 2), 16.0, None, ALU.mult)
            V.tensor_scalar(half_bg[:], p1("b_gate", 0, 3 * KT), 0.5, None, ALU.mult)
            V.tensor_scalar(half_ba[:], p1("b_a", 0, BT), 0.5, None, ALU.mult)
            V.tensor_scalar(half_bx[:], p1("b_x", 0, BT), 0.5, None, ALU.mult).then_inc(setup, 1)
            V.scalar_tensor_tensor(lam_t["t"][:], p1("lam", 0, BT), -1.0, p1("lam", 0, BT), ALU.mult, ALU.max).then_inc(lam_dve, 1)
            split("mv", 0)
            split("mv", 1)
            dve.wait_ge(setup, 1)
            dve.wait_ge(root_done, 1)
            V.reciprocal(rstd0[:, 0], rstd0[:, 0]).then_inc(rstd_done, 1)
            dve.wait_ge(rstd_done, 1)
            for c in range(4):
                for k in range(4 * c, 4 * c + 4):
                    ins = V.scalar_tensor_tensor(mem_n[:, k], mem_raw[:, k], g_s[:, 1, k:k + 1], rstd0[:, 0], ALU.mult, ALU.mult)
                ins.then_inc(mem_scaled, 1)
                dve.wait_ge(memX_hi, c + 1)
                V.tensor_tensor(XM[:, 4 * c:4 * c + 4, 1, :], mem_n[:, 4 * c:4 * c + 4], f32(XM[:, 4 * c:4 * c + 4, 0, :]),
                                ALU.subtract).then_inc(memX_lo, 1)
            split("mv", 2)
            split("mv", 3)
            dve.wait_ge(root_done, 2)
            V.reciprocal(rstd0[:, 1], rstd0[:, 1]).then_inc(rstd_done, 1)
            dve.wait_ge(ff_hi, 1)
            V.tensor_tensor(ff_w[:, :, 1, :], ff_raw[:], f32(ff_w[:, :, 0, :]), ALU.subtract).then_inc(ff_lo, 1)
            lt = lam_t
            dve.wait_ge(lam_act, 1)
            V.tensor_scalar(lt["u"][:], lt["e"][:], 1.0, None, ALU.add).then_inc(lam_dve, 1)
            dve.wait_ge(lam_dve, 2)
            V.tensor_scalar(lt["m"][:], lt["u"][:], 1.0, None, ALU.is_equal).then_inc(lam_dve, 1)
            dve.wait_ge(lam_dve, 3)
            V.scalar_tensor_tensor(lt["d"][:], lt["u"][:], -1.0, lt["m"][:], ALU.add, ALU.add).then_inc(lam_dve, 1)
            dve.wait_ge(lam_dve, 4)
            V.reciprocal(lt["d"][:], lt["d"][:]).then_inc(lam_dve, 1)
            dve.wait_ge(lam_act, 2)
            dve.wait_ge(lam_dve, 5)
            V.tensor_tensor(lt["d"][:], lt["d"][:], lt["l"][:], ALU.mult).then_inc(lam_dve, 1)
            dve.wait_ge(lam_dve, 6)
            V.tensor_tensor(lt["d"][:], lt["d"][:], lt["m"][:], ALU.add).then_inc(lam_dve, 1)
            dve.wait_ge(lam_dve, 7)
            V.tensor_tensor(lt["e"][:], lt["d"][:], lt["e"][:], ALU.mult).then_inc(lam_dve, 1)
            dve.wait_ge(lam_dve, 8)
            V.scalar_tensor_tensor(lt["d"][:], p1("lam", 0, BT), 0.0, lt["e"][:], ALU.min, ALU.subtract).then_inc(lam_dve, 1)
            dve.wait_ge(lam_dve, 9)
            V.tensor_scalar(ls4[:], lt["d"][:], 4.0, None, ALU.mult).then_inc(side["dve"], 1)

            def destination(ph, i, w):
                if ph in ("mv", "v"):
                    c = (2 * i + w) * UC
                    return (mem_v if ph == "mv" else v_all)[:, :, c:c + UC]
                if ph in ("mkq", "qk"):
                    A = att["mem" if ph == "mkq" else "fox"]
                    return A["k_raw" if (w == 0) == (ph == "mkq") else "q_raw"][:]
                if ph == "lru":
                    return lx_pad[:, :, 3:] if w == 0 else lru["lg"][:]
                if ph.startswith("gate"):
                    return gates[:, i, w]
                return yd[:]

            n_gated = 0
            for u in range(4, U0["up"] + 4):
                if u in evac_at:
                    g, ph, i, w = evac_at[u]
                    if ph == "lru" and i == 0 and w == 0:
                        dve.wait_ge(side["pool"], side_count("mem", 3, "pool", "values_staged"))
                        V.memset(lx_pad[:, :, 0:3], 0.0)
                    if ph == "gate0" and i == 1 and w == 0:
                        dve.wait_ge(side["pe"], side_count("fox", 3, "pe", "scores"))
                    if ph.startswith("branch"):
                        dve.wait_ge(gated, n_gated)
                    if ph == "out":
                        dve.wait_ge(x2_done if 2 * i + w else gated, 2 * i + w or n_gated)
                    if ph.startswith("gate") and ph != "gate0" and i == 0:
                        dve.wait_ge(acc_added, 4 * int(ph[4:]))
                    add_low(g, destination(ph, i, w))
                    if ph.startswith("branch"):
                        q = int(ph[6:])
                        dve.wait_ge(evac_done, g + 1)
                        dve.wait_ge(gate_ready, 6 * q + 2 * i + w + 1)
                        n_gated += 1
                        dst = acc[:, w] if i == 0 else gates[:, i, w]
                        V.scalar_tensor_tensor(dst, gates[:, i, w], 1.0, yd[:], ALU.add, ALU.mult).then_inc(gated, 1)
                        if i > 0:
                            dve.wait_ge(gated, n_gated)
                            if i == 2:
                                dve.wait_ge(acc_added, 4 * int(ph[6:]) + 1 + w)
                            V.tensor_tensor(acc[:, w], acc[:, w], gates[:, i, w], ALU.add).then_inc(acc_added, 1)
                    if ph == "out":
                        n = 2 * i + w
                        dve.wait_ge(evac_done, g + 1)
                        V.tensor_tensor(xs[:, 2 * n:2 * n + 2], xs[:, 2 * n:2 * n + 2], yd[:], ALU.add).then_inc(x2_done, 1)
                split("", u)
                if 8 <= u < 12:
                    c = u - 8
                    dve.wait_ge(xX_hi, c + 1)
                    V.tensor_tensor(X[:, 4 * c:4 * c + 4, 1, :], x_n[:, 4 * c:4 * c + 4], f32(X[:, 4 * c:4 * c + 4, 0, :]),
                                    ALU.subtract).then_inc(xX_lo, 1)
                for f, kind, m in hooks.get(u, []):
                    f(kind, m)
                if u in evac_at and ph.startswith("branch") and i == 2:
                    q = int(ph[6:])
                    r = 4 * q + 2 * w
                    dve.wait_ge(merged_hi, 2 * q + w + 1)
                    V.scalar_tensor_tensor(merged[:, r:r + 2, 1, :], acc[:, w], 0.5, f32(merged[:, r:r + 2, 0, :]),
                                           ALU.mult, ALU.subtract).then_inc(merged_lo, 1)

            def h2_low(c):
                dve.wait_ge(h2_hi, c + 1)
                V.tensor_tensor(X[:, 4 * c:4 * c + 4, 1, :], h2[:, 4 * c:4 * c + 4], f32(X[:, 4 * c:4 * c + 4, 0, :]),
                                ALU.subtract).then_inc(h2_lo, 1)

            dve.wait_ge(root_done, 3)
            V.reciprocal(rstd2[:], rstd2[:]).then_inc(rstd_done, 1)
            dve.wait_ge(rstd_done, 3)
            for c in range(4):
                for k in range(4 * c, 4 * c + 4):
                    ins = V.scalar_tensor_tensor(h2[:, k], xs[:, k], g_s[:, 2, k:k + 1], rstd2[:], ALU.mult, ALU.mult)
                ins.then_inc(h2_scaled, 1)
                if c > 0:
                    h2_low(c - 1)
            h2_low(3)
            for w in range(2):
                ins = V.memset(up_pad[w][:, :, 0:2], 0.0)
            ins.then_inc(setup, 1)
            dve.wait_ge(setup, 3)

            def up_taps(i, w):
                for n, s_from, s_to in ((1, conv0, tap1), (0, tap1, tap0)):
                    dve.wait_ge(s_from, i * 2 + (w + 1))
                    for t in range(2):
                        ins = V.scalar_tensor_tensor(up_c[w][:, t], up_pad[w][:, t, n:n + T],
                                                     par_at("w_fconv", i * 2 + (n * 2 * FT + w * FT + t)),
                                                     up_c[w][:, t], ALU.mult, ALU.add)
                    ins.then_inc(s_to, 1)

            def up_iteration(i, split_next):
                U = U0["up"]
                for k in range(4, 7):
                    split("up", U + k, i)
                add_low(G0["up"], up_pad[0][:, :, 2:], i)
                split("up", U + 7, i)
                up_taps(i, 0)
                for k in range(3):
                    split_next(k)
                add_low(G0["up"] + 1, up_pad[1][:, :, 2:], i)
                split_next(3)
                up_taps(i, 1)
                dve.wait_ge(tap0, i * 2 + 2)
                dve.wait_ge(gelu_done, i + 1)
                V.tensor_tensor(up_c[1][:], up_c[0][:], up_c[1][:], ALU.mult).then_inc(prod_done, 1)
                dve.wait_ge(hidden_hi, i + 1)
                hs = hidden[:, bass.ds(i * 2, 2)]
                V.tensor_tensor(hs[:, :, 1, :], up_c[1][:], f32(hs[:, :, 0, :]), ALU.subtract).then_inc(hidden_lo, 1)

            with dve.Fori(0, FT // 2 - 1) as i:
                up_iteration(i, lambda k: split("up", U0["up"] + 8 + k, i))
            with dve.Fori(FT // 2 - 1, FT // 2) as i:
                up_iteration(i, lambda k: split("down", U0["down"] + k))

            dve.wait_ge(x2_done, 8)
            V.memset(yd[:], 0.0).then_inc(yd_free, 1)

            def down_out(i, w):
                g = G0["down"] + w
                dve.wait_ge(yd_free, i * 2 + (w + 1))
                add_low(g, yd[:, 0:1], i, banks=1)
                dve.wait_ge(evac_done, at(g + 1, i, 2))
                tile = xs[:, bass.ds(i * 2 + w, 1)].rearrange("p a t -> p (a t)")
                V.tensor_tensor(tile, yd[:, 0], tile, ALU.add).then_inc(yd_free, 1)

            def down_iteration(i, more):
                U = U0["down"]
                for k in range(4, 7):
                    split("down", U + k, i)
                down_out(i, 0)
                split("down", U + 7, i)
                if more:
                    for k in range(8, 11):
                        split("down", U + k, i)
                down_out(i, 1)
                if more:
                    split("down", U + 11, i)

            with dve.Fori(0, KT // 2 - 1) as i:
                down_iteration(i, True)
            with dve.Fori(KT // 2 - 1, KT // 2) as i:
                down_iteration(i, False)

        @block.gpsimd
        def _(pool):
            G = nc.gpsimd

            def wait(**need):
                for e, v in need.items():
                    pool.wait_ge(side[e], v)

            def done(ins):
                ins.then_inc(side["pool"], 1)

            pool.wait_ge(rstd_done, 2)
            for c in range(4):
                G.tensor_tensor(x_n[:, 4 * c:4 * c + 4], xs[:, 4 * c:4 * c + 4],
                                rstd0[:, 1:2].to_broadcast([P, 4, T]), ALU.mult).then_inc(x_scaled, 1)
                pool.wait_ge(x_scaled, c + 1)
                for k in range(4 * c, 4 * c + 4):
                    ins = G.tensor_scalar(x_n[:, k], x_n[:, k], g_s[:, 0, k:k + 1], None, ALU.mult)
                ins.then_inc(x_gained, 1)

            def stage_values(kind, m):
                A = att[kind]
                wait(pe=side_count(kind, m, "pe", None))
                last = G0["mv"] + 3 if kind == "mem" else G0["v"] + 3
                pool.wait_ge(evac_done, last + 1)
                if kind == "mem":
                    pool.wait_ge(memX_hi, 4)
                src = mem_v if kind == "mem" else v_all
                done(G.tensor_copy(A["v_cur"][:], src[:, :, m * T:(m + 1) * T]))

            def load_gates(m):
                if m == 0:
                    pool.wait_ge(pe_units, U0["lru"])
                wait(pe=side_count("lru", m, "pe", None))
                for j in range(2):
                    G.dma_start(lru["rg"][:, j], w_rg[j, 2 * m:2 * m + 2].rearrange("b n c -> n b c")).then_inc(rg_in, 16)

            L = lru
            for m in range(4):
                stage_values("mem", m)
            for m in range(4):
                load_gates(m)
                wait(act=side_count("lru", m, "act", "gelu_square"))
                done(G.tensor_scalar(L["gg"][:], L["gg"][:], GELU_C, 1.0, ALU.mult, ALU.add))
                wait(pool=side_count("lru", m, "pool", "gelu_poly"))
                done(G.tensor_tensor(L["gg"][:], L["gg"][:], L["lg"][:], ALU.mult))
                wait(act=side_count("lru", m, "act", "exps"))
                done(G.tensor_tensor(L["aa"][:], L["a"][:], L["a"][:], ALU.mult))
            wait(dve=side_count("decay", 0, "dve", None))
            done(G.memset(ff_pad[:], 0.0))
            wait(pool=side_count("decay", 0, "pool", "zeroed"))
            wait(dve=side_count("decay", 0, "dve", "c"))
            for h in range(8):
                G.tensor_scalar(rhs_c[:, h], dec["u"][:], rows_sel[:, h:h + 1], ident[:, 32 + h:33 + h], ALU.mult, ALU.add)
            done(G.tensor_scalar(lhs_c[:], dec["u"][:], rows_sel[:, 8:9], rows_sel[:, 9:10], ALU.mult, ALU.add))
            for m in range(4):
                stage_values("fox", m)

            for n in range(8):
                pool.wait_ge(x2_sq, n + 1)
                if n == 0:
                    G.tensor_copy(sum2[:], sq2[:, 0]).then_inc(x2_sum, 1)
                else:
                    pool.wait_ge(x2_sum, n)
                    G.tensor_tensor(sum2[:], sum2[:], sq2[:, n % 2], ALU.add).then_inc(x2_sum, 1)

            with pool.Fori(0, KT // 2) as i:
                for w in range(2):
                    pool.wait_ge(yd_free, i * 2 + (w + 2))
                    G.dma_start(outT[bass.ds(i * (2 * P) + w * P, P), :], xs[:, bass.ds(i * 2 + w, 1)].rearrange("p a t -> p (a t)")
                                ).then_inc(out_stored, 16)
            pool.wait_ge(out_stored, 16 * KT)


def _columns(v):
    return np.reshape(v, (-1, P)).T


def kernel(x, mem, g_mix, w_in, b_f, g_q_fox, g_k_fox, w_lru_conv, b_lru_conv, w_rg_a, b_rg_a, w_rg_x, b_rg_x,
           lru_lambda, g_mem, w_mem_kv, g_q_mem, g_k_mem, b_gate, w_branch, w_out, g_ffn, w_ffn_up, w_ffn_conv,
           b_ffn_conv, w_ffn_down):
    import concourse.bacc as bacc
    from concourse.bass_utils import run_bass_kernel_spmd

    A = np.asarray
    bf = np.zeros((P, 1), A(b_f).dtype)
    bf[0:8, 0] = A(b_f)[0]
    bf[32:40, 0] = A(b_f)[0]
    packed = [_columns(A(v)[0].reshape(-1)) for v in
              (g_mix, g_mem, g_ffn, b_gate, w_ffn_conv, b_ffn_conv, w_lru_conv, b_lru_conv, b_rg_a, b_rg_x, lru_lambda,
               g_q_fox, g_k_fox, g_q_mem, g_k_mem)]
    par = np.ascontiguousarray(np.concatenate(packed + [bf], axis=1))
    assert par.shape == (P, N_PAR)
    key = np.arange(T)
    mask = [np.where(key[None, :] <= (qt * P + np.arange(P))[:, None], 0.0, MASKED) for qt in range(2)]
    high = ((np.arange(P) >= 32) & (np.arange(P) < 64))[:, None]
    shapes_const = np.concatenate([np.eye(P)] + mask + [-np.eye(P)[:, 0:8], high, ~high], axis=1).astype(np.float32)
    arrays = {
        "xT": np.ascontiguousarray(A(x)[0].T), "memT": np.ascontiguousarray(A(mem)[0].T), "par": par,
        "shapes_const": shapes_const, "w_in": A(w_in)[0], "w_mem_kv": A(w_mem_kv)[0],
        "w_rg": np.stack([A(w_rg_a)[0], A(w_rg_x)[0]]), "w_branch": A(w_branch)[0].reshape(3 * BW, D),
        "w_out": A(w_out)[0], "w_up": A(w_ffn_up)[0], "w_down": A(w_ffn_down)[0],
    }
    nc = bacc.Bacc("TRN2", target_bir_lowering=False, num_devices=1)
    args = [nc.dram_tensor(n, a.shape, mybir.dt.from_np(a.dtype), kind="ExternalInput").ap() for n, a in arrays.items()]
    args.append(nc.dram_tensor("outT", (D, T), F32, kind="ExternalOutput").ap())
    hybrid_layer_kernel(nc, *args)
    r = run_bass_kernel_spmd(nc, [arrays], core_ids=[0])
    return np.ascontiguousarray(r.results[0]["outT"].T)[None]
```

```python
from contextlib import ExitStack

import numpy as np
import concourse.bass as bass
from concourse import mybir

ALU = mybir.AluOpType
ACT = mybir.ActivationFunctionType
F32 = mybir.dt.float32
F32R = mybir.dt.float32r
AX_X = mybir.AxisListType.X

P = 128
T = 256
D = 2048
KT = D // P
BW = 1024
BT = BW // P
FFN = 5632
FT = FFN // P
EPS = 1e-6
UK, UC = 4, 256
SLOTS = 4
GELU_C, GELU_S = 0.044715, float(np.sqrt(2.0 / np.pi))
MASKED = -1e30
HR = 40
CW = P + T

COL_Q, COL_K, COL_V, COL_FF = 0, BW, 2 * BW, 3 * BW
COL_LX = 3 * BW + 8
COL_LG, COL_MQ, COL_GATE = COL_LX + BW, COL_LX + 2 * BW, COL_LX + 3 * BW

PHASES = [("mv", 2, 4), ("mkq", 4, 4), ("lru", 4, 4), ("v", 2, 4), ("qk", 4, 4)]
for _q in range(4):
    PHASES += [(f"gate{_q}", 3, 4), (f"branch{_q}", 3, 2)]
PHASES += [("out", 4, 4), ("up", FT // 2, 4), ("down", 2, FT // UK)]
NG = {_name: 4 if _name == "down" else 2 for _name, _, _ in PHASES}
U0, G0 = {}, {}
GROUPS = []
_u = 0
for _name, _n, _per in PHASES:
    U0[_name], G0[_name] = _u, len(GROUPS)
    for _i in range(_n):
        for _w in range(NG[_name]):
            GROUPS.append((_name, _i, _w, _u + _per - 1))
            _u += _per
U_ALL = _u

PAR = {}
_c = 0
for _name, _n in [("g_mix", KT), ("g_mem", KT), ("g_ffn", KT), ("b_gate", 3 * KT), ("w_fconv", 3 * 2 * FT),
                  ("b_fconv", 2 * FT), ("w_lconv", 4 * BT), ("b_lconv", BT), ("b_a", BT), ("b_x", BT),
                  ("lam", BT), ("g_q", 1), ("g_k", 1), ("g_qm", 2), ("g_km", 2), ("b_f", 1)]:
    PAR[_name] = _c
    _c += _n
N_PAR = _c

_ATTENTION = lambda pool: {
    "pe": ["sums", "scores", "transposes", "values"],
    "act": ["squares", "root", "exp", "weights_copied", "y_hi"],
    "dve": ["norm_k", "norm_q", "normed", "masked", "row_max", "row_inv", "weights", "y_lo"],
    "pool": pool,
}
KINDS = [
    ("mem", 4, _ATTENTION(["k_scaled", "values_staged"])),
    ("lru", 4, {
        "pe": ["gates"],
        "act": ["gelu_square", "gate_tanh", "exps", "gelu_tanh", "root", "y_hi"],
        "dve": ["log_a", "ix", "decay_sq", "u", "scan", "gelu", "y", "y_lo"],
        "pool": ["gelu_poly", "gelu_cube", "a_sq"],
    }),
    ("decay", 1, {
        "pe": ["logits"],
        "act": ["exp", "ln"],
        "dve": ["low", "z", "abs", "one_plus", "is_one", "minus_one", "inverse", "ratio", "ratio1",
                "log1p", "log_f", "c"],
        "pool": ["columns"],
    }),
    ("fox", 4, _ATTENTION(["values_staged"])),
]
LEN = {k: {e: len(s) for e, s in steps.items()} for k, _, steps in KINDS}
STEP = {k: {e: {n: j + 1 for j, n in enumerate(s)} for e, s in steps.items()} for k, _, steps in KINDS}
BASE, _sum = {}, {"pe": 0, "act": 0, "dve": 1, "pool": 0}
for _k, _n, _ in KINDS:
    BASE[_k] = dict(_sum)
    for _e in _sum:
        _sum[_e] += _n * LEN[_k][_e]
SIDE_ALL = dict(_sum)


def side_count(kind, m, engine, step):
    return m * LEN[kind][engine] + (BASE[kind][engine] + (STEP[kind][engine][step] if step else 0))


def at(const, i, coef):
    return const if i is None else i * coef + const


def hybrid_layer_kernel(nc, xT, memT, par, shapes_const, w_in, w_mem_kv, w_rg, w_branch, w_out, w_up, w_down, outT):
    with ExitStack() as ctx:
        KB = 1024
        SB0 = 16512
        TOP = 212856

        def sb(name, shape, offset, dt=F32):
            return nc.alloc_sbuf_tensor_at(name, shape, dt, offset=SB0 + int(offset))

        def sem(name):
            return ctx.enter_context(nc.semaphore(name))

        W = sb("W", [P, SLOTS, UK, 2, UC], 0, F32R)
        raw = sb("raw", [P, SLOTS, UK, UC], 32 * KB)
        X = sb("X", [P, KT, 2, T], 48 * KB, F32R)
        xs = sb("xs", [P, KT, T], 80 * KB)
        Y = sb("Y", [P, 3, BT, 2, T], 96 * KB, F32R)
        M0, G_0, T0 = 144 * KB, 176 * KB, 192 * KB
        XM = sb("XM", [P, KT, 2, T], M0, F32R)
        merged = sb("merged", [P, KT, 2, T], M0, F32R)
        mem_raw = sb("mem_raw", [P, KT, T], 96 * KB)
        x_n = sb("x_n", [P, KT, T], 128 * KB)
        sq0 = sb("sq0", [P, UK, T], 112 * KB)
        sum0 = sb("sum0", [P, 2, UK, T], 116 * KB)
        rstd0 = sb("rstd0", [P, 2, T], G_0 + 8 * KB)
        ff_raw = sb("ff_raw", [P, KT, 8], G_0 + 10 * KB)
        ff_w = sb("ff_w", [P, KT, 2, HR], T0, F32R)
        mem_v = sb("mem_v", [P, 2, BW], G_0)

        def attention_buffers(tag, base):
            names = [("k_raw", [P, 2, T]), ("q_raw", [P, 2, T]), ("k_n", [P, 2, T]), ("q_n", [P, 2, T]),
                     ("S", [P, 2, 2, T]), ("PT", [P, 2, 2, T]), ("v_cur", [P, 2, T])]
            out, o = {}, base
            for n, shape in names:
                out[n] = sb(f"{tag}_{n}", shape, o)
                if n == "PT":
                    out["rstd"] = sb(f"{tag}_rstd", [P, 2, 2, T], o)
                o += int(np.prod(shape[1:])) * 4
            return out

        att = {"mem": attention_buffers("mem", 96 * KB), "fox": attention_buffers("fox", M0)}
        causal = lambda t: t.rearrange("p h a t -> p h (a t)")[:, :, 0:CW]
        v_all = sb("v_all", [P, 2, BW], M0 + 22784)
        lx_pad = sb("lx_pad", [P, 2, 3 + T], M0)
        _o = M0 + 2080
        lru = {}
        for n in ["lg", "rg", "xr", "ra", "a", "aa", "tn", "ix", "hs", "gg"]:
            shape = [P, 2, 2, P] if n == "rg" else [P, 2, T]
            lru[n] = sb(f"lru_{n}", shape, _o)
            _o += 2 * KB
        lhs_c = sb("lhs_c", [HR, T], T0 + 4 * KB)
        dec = {n: sb(f"dec_{n}", [HR, T], G_0 + (12 + j) * KB) for j, n in enumerate(["z", "e", "u", "r"])}
        dec_l = sb("dec_l", [HR, T], T0 + 2 * KB + 512)
        rhs_c = sb("rhs_c", [HR, 8, T], G_0 + 4 * KB)
        gates = sb("gates", [P, 3, 2, 2, T], G_0)
        acc = sb("acc", [P, 2, 2, T], G_0 + 12 * KB)
        yd = sb("yd", [P, 2, T], T0 + 64)
        sq2 = sb("sq2", [P, 2, 2, T], G_0)
        sum2 = sb("sum2", [P, 2, T], G_0 + 4 * KB)
        rstd2 = sb("rstd2", [P, T], T0 + 5 * KB)
        hidden = sb("hidden", [P, FT, 2, T], 96 * KB, F32R)
        up_pad = {w: sb(f"up_pad{w}", [P, 2, 2 + T], 184 * KB + w * 2080) for w in range(2)}
        up_c = {w: sb(f"up_c{w}", [P, 2, T], 184 * KB + 4160 + w * 2048) for w in range(2)}
        low = sb("low", [P, 2, 2, T], T0 + 6 * KB)

        next_free = [202 * KB]

        def const_sb(name, shape):
            t = sb(name, shape, next_free[0])
            next_free[0] += -(-4 * int(np.prod(shape[1:])) // 32) * 32
            return t

        par_sb = const_sb("par_sb", [P, N_PAR])
        ident = const_sb("ident", [P, P])
        rows_sel = const_sb("rows_sel", [P, 10])
        mask = const_sb("mask", [P, CW])
        ones = const_sb("ones", [P, P])
        half_bg = const_sb("half_bg", [P, 3 * KT])
        half_ba = const_sb("half_ba", [P, BT])
        half_bx = const_sb("half_bx", [P, BT])
        ls4 = const_sb("ls4", [P, BT])
        rstd_tok = const_sb("rstd_tok", [P, 2])
        gk_s = const_sb("gk_s", [P, 1])
        gkm_s = const_sb("gkm_s", [P, 2])
        stat = const_sb("stat", [P, 3, 4])
        eps = const_sb("eps", [P, 4])
        lam_t = {n: sb(f"lam_{n}", [P, BT], G_0 + 11 * KB + 32 * j) for j, n in enumerate(["t", "e", "u", "m", "d", "l"])}
        assert next_free[0] <= TOP, next_free[0]

        psG = ctx.enter_context(nc.psum_tensor("psG", [P, 4, 512], F32))
        psM = ctx.enter_context(nc.psum_tensor("psM", [P, 4, 512], F32))

        raw_full = [sem(f"raw_full{s}") for s in range(SLOTS)]
        hi_done, lo_done = sem("hi_done"), sem("lo_done")
        pe_units = sem("pe_units")
        low_copied, evac_done = sem("low_copied"), sem("evac_done")
        side = {e: sem(f"side_{e}") for e in ("pe", "act", "dve", "pool")}
        mem_in = [sem(f"mem_in{c}") for c in range(4)]
        x_in = [sem(f"x_in{c}") for c in range(4)]
        par_in, const_in, ff_in, rg_in = sem("par_in"), sem("const_in"), sem("ff_in"), sem("rg_in")
        setup, ones_set, pool_step = sem("setup"), sem("ones_set"), sem("pool_step")
        act_warm = sem("act_warm")
        sq_done, ss_done, rstd_done = sem("sq_done"), sem("ss_done"), sem("rstd_done")
        x_scaled = sem("x_scaled")
        memX_hi, memX_lo, xX_hi, xX_lo = sem("memX_hi"), sem("memX_lo"), sem("xX_hi"), sem("xX_lo")
        ff_hi, ff_lo = sem("ff_hi"), sem("ff_lo")
        lam_act, lam_dve = sem("lam_act"), sem("lam_dve")
        lru_conv0, lru_taps = sem("lru_conv0"), sem("lru_taps")
        gate_ready = sem("gate_ready")
        gated, acc_added, merged_hi, merged_lo = sem("gated"), sem("acc_added"), sem("merged_hi"), sem("merged_lo")
        x2_done, x2_sq, x2_sum, x2_ss, root_done = \
            sem("x2_done"), sem("x2_sq"), sem("x2_sum"), sem("x2_ss"), sem("root_done")
        h2_hi, h2_lo, up_scaled = sem("h2_hi"), sem("h2_lo"), sem("up_scaled")
        conv0, tap1, tap0, gelu_done = sem("conv0"), sem("tap1"), sem("tap0"), sem("gelu_done")
        prod_done, hidden_hi, hidden_lo = sem("prod_done"), sem("hidden_hi"), sem("hidden_lo")
        out_done = sem("out_done")
        out_stored, last_stored = sem("out_stored"), sem("last_stored")

        def p1(name, j, n=1):
            return par_sb[:, PAR[name] + j:PAR[name] + j + n]

        def par_at(name, j):
            return par_sb[:, bass.ds(j + PAR[name], 1)]

        def f32(ap):
            return ap.bitcast(F32)

        rows = lambda w: w.rearrange("(k p) c -> p k c", p=P)
        w_in_r, w_kv_r, w_br_r, w_out_r, w_up_r, w_down_r = map(rows, (w_in, w_mem_kv, w_branch, w_out, w_up, w_down))

        def unit_source(phase, i, k):
            if phase == "down":
                w, kk = k // (FT // UK), k % (FT // UK)
                return w_down_r[:, kk * UK:(kk + 1) * UK, bass.ds(i * (4 * UC) + w * UC, UC)]
            if phase.startswith("branch"):
                q = int(phase[6:])
                return w_br_r[:, bass.ds(i * BT + (k % 2) * UK, UK), (2 * q + k // 2) * UC:(2 * q + k // 2 + 1) * UC]
            w, kk = k // 4, k % 4
            if phase.startswith("gate"):
                q = int(phase[4:])
                src, col = w_in_r, i * D + (COL_GATE + (2 * q + w) * UC)
            elif phase == "mv":
                src, col = w_kv_r, i * (2 * UC) + (BW + w * UC)
            elif phase == "mkq":
                src, col = (w_kv_r, i * UC) if w == 0 else (w_in_r, i * UC + COL_MQ)
            elif phase == "lru":
                src, col = w_in_r, i * UC + (COL_LX if w == 0 else COL_LG)
            elif phase == "v":
                src, col = w_in_r, i * (2 * UC) + (COL_V + w * UC)
            elif phase == "qk":
                src, col = w_in_r, i * UC + (COL_Q if w == 0 else COL_K)
            elif phase == "out":
                src, col = w_out_r, i * (2 * UC) + w * UC
            else:
                src, col = w_up_r, i * UC + w * FFN
            return src[:, kk * UK:(kk + 1) * UK, bass.ds(col, UC)]

        block = ctx.enter_context(nc.Block())

        @block.sync
        def _(sp):
            def load(phase, i, k, u, coef):
                s = u % SLOTS
                if i is not None or u >= SLOTS:
                    sp.wait_ge(lo_done, at(u - 3, i, coef))
                sp.dma_start(raw[:, s], unit_source(phase, 0 if i is None else i, k)).then_inc(raw_full[s], 16)

            mem_r = memT.rearrange("(k p) t -> p k t", p=P)
            x_r = xT.rearrange("(k p) t -> p k t", p=P)
            sp.dma_start(par_sb[:], par).then_inc(par_in, 16)
            for c in range(4):
                sp.dma_start(mem_raw[:, 4 * c:4 * c + 4], mem_r[:, 4 * c:4 * c + 4]).then_inc(mem_in[c], 16)
                load("mv", None, c, c, 0)
            for c in range(4):
                sp.dma_start(xs[:, 4 * c:4 * c + 4], x_r[:, 4 * c:4 * c + 4]).then_inc(x_in[c], 16)
                load("mv", None, 4 + c, 4 + c, 0)
            sp.dma_start(rows_sel[:], shapes_const[:, P + CW:]).then_inc(const_in, 16)
            sp.dma_start(ident[:], shapes_const[:, 0:P]).then_inc(const_in, 16)
            sp.dma_start(mask[:], shapes_const[:, P:P + CW]).then_inc(const_in, 16)
            sp.dma_start(ff_raw[:], w_in_r[:, :, COL_FF:COL_FF + 8]).then_inc(ff_in, 16)
            for name, n, per in PHASES:
                with sp.Fori(1 if name == "mv" else 0, n) as i:
                    for k in range(NG[name] * per):
                        load(name, i, k, U0[name] + k, NG[name] * per)
            for t in (KT - 2, KT - 1):
                sp.wait_ge(out_done, KT // 2)
                sp.dma_start(outT[t * P:(t + 1) * P], xs[:, t]).then_inc(last_stored, 16)
            sp.wait_ge(last_stored, 32)

        @block.tensor
        def _(pe):
            def mm(*a, **kw):
                return nc.tensor.matmul(*a, skip_group_check=True, **kw)

            def group(phase, i, w, operand, hooks, per=4, coef=8, rows_major=False, ready=None):
                b = 2 * (w % 2)
                g = G0[phase] + w
                if i is not None or g >= 2:
                    pe.wait_ge(evac_done, at(g - 1, i, NG[phase]))
                last = per * UK - 1
                for n in range(per):
                    u = U0[phase] + per * w + n
                    s = u % SLOTS
                    pe.wait_ge(lo_done, at(u + 1, i, coef))
                    if ready is not None:
                        ready(n)
                    for k in range(UK):
                        kt = n * UK + k
                        x_hl = operand(kt)
                        for t in range(2):
                            ts = slice(t * P, t * P + P)
                            if rows_major:
                                mm(psG[:, b + t, :], x_hl[:, 0, ts], W[:, s, k], start=kt == 0, stop=False)
                                ins = mm(psG[:, b + t, T:], x_hl[:, 1, ts], W[:, s, k, 0], start=False, stop=kt == last)
                            else:
                                mm(psG[:, b + t, :], W[:, s, k, 0, ts], x_hl, start=kt == 0, stop=False)
                                ins = mm(psG[:, b + t, T:], W[:, s, k, 1, ts], x_hl[:, 0], start=False, stop=kt == last)
                    ins.then_inc(pe_units, 1)
                    if per * w + n in hooks:
                        hooks[per * w + n]()

            def side_waits(**need):
                for e, v in need.items():
                    pe.wait_ge(side[e], v)

            def done(ins):
                ins.then_inc(side["pe"], 1)

            def attention_hooks(kind, m):
                A = att[kind]

                def sums():
                    side_waits(act=side_count(kind, m, "act", "squares"))
                    for j in range(2):
                        if kind == "fox":
                            ins = mm(psM[:, j, :], ones[:], A["S"][:, j].rearrange("p a t -> p (a t)"), start=True, stop=True)
                        else:
                            for t in range(2):
                                ins = mm(psM[:, 0, j * T:(j + 1) * T], ones[:], A["S"][:, j, t], start=t == 0, stop=t == 1)
                    done(ins)

                def scores():
                    side_waits(dve=side_count(kind, m, "dve", "normed"))
                    if kind == "fox":
                        side_waits(pool=side_count("decay", 0, "pool", "columns"))
                    for qt in range(2):
                        qs = slice(qt * P, qt * P + P)
                        if kind == "fox":
                            keys = slice(0, qt * P + P)
                            for h in range(2):
                                dst = psM[:, 2 + h, 0:P] if qt == 0 else psM[:, 2 + h, P:CW]
                                mm(dst, A["q_n"][:, h, qs], A["k_n"][:, h, keys], start=True, stop=False)
                                ins = mm(dst, lhs_c[:, qs], rhs_c[:, bass.ds(m * 2 + h, 1), keys].rearrange("p a t -> p (a t)"),
                                         start=False, stop=True)
                        else:
                            for t in range(2):
                                ins = mm(psM[:, 2, qt * T:(qt + 1) * T], A["q_n"][:, t, qs], A["k_n"][:, t],
                                         start=t == 0, stop=t == 1)
                    done(ins)

                def transposes():
                    side_waits(dve=side_count(kind, m, "dve", "weights"))
                    if kind == "mem":
                        pe.wait_ge(const_in, 48)
                    for h in range(2 if kind == "fox" else 1):
                        for kt in range(2):
                            for qt in range(2):
                                if kind == "mem":
                                    o = kt * T + qt * P
                                    ins = nc.tensor.transpose(psM[:, h, o:o + P], A["S"][:, h, qt, kt * P:kt * P + P], ident[:])
                                elif qt >= kt:
                                    ins = nc.tensor.transpose(psM[:, h, (qt + kt) * P:(qt + kt + 1) * P],
                                                              causal(A["S"])[:, h, (qt + kt) * P:(qt + kt + 1) * P], ident[:])
                    done(ins)

                def values():
                    side_waits(act=side_count(kind, m, "act", "weights_copied"),
                               pool=side_count(kind, m, "pool", "values_staged"))
                    for t in range(2):
                        for kt in range(2):
                            if kind == "mem":
                                dst, wts = psM[:, 2, t * T:(t + 1) * T], A["PT"][:, 0, kt]
                            elif kt == 0:
                                dst, wts = psM[:, 2, t * T:(t + 1) * T], causal(A["PT"])[:, t, 0:T]
                            else:
                                dst, wts = psM[:, 2, t * T + P:(t + 1) * T], causal(A["PT"])[:, t, T:CW]
                            ins = mm(dst, A["v_cur"][:, kt, t * P:t * P + P], wts, start=kt == 0, stop=kt == 1)
                    done(ins)

                return {0: sums, 4: scores, 6: transposes, 7: values}

            def lru_hooks(m):
                def gates_():
                    pe.wait_ge(rg_in, at(32, m, 32))
                    pe.wait_ge(lru_taps, at(3, m, 3))
                    side_waits(act=side_count("lru", m - 1, "act", "gate_tanh"))
                    for j in range(2):
                        for b in range(2):
                            ins = mm(psM[:, j, b * T:(b + 1) * T], lru["rg"][:, j, b], lru["xr"][:, b], start=True, stop=True)
                    done(ins)
                return {1: gates_}

            def decay_hooks():
                def logits():
                    side_waits(dve=side_count("decay", 0, "dve", None), act=side_count("decay", 0, "act", None))
                    pe.wait_ge(ff_lo, 1)
                    for kt in range(KT):
                        mm(psM[0:HR, 0, :], ff_w[:, kt, 0], X[:, kt], start=kt == 0, stop=False)
                        ins = mm(psM[0:HR, 0, T:], ff_w[:, kt, 1], X[:, kt, 0], start=False, stop=kt == KT - 1)
                    done(ins)
                return {1: logits}

            x_op = lambda kt: X[:, kt]
            m_op = lambda kt: XM[:, kt]

            def channel_sums():
                pe.wait_ge(sq_done, 2)
                for j in range(2):
                    for k in range(UK):
                        mm(psM[:, 0, j * T:(j + 1) * T], ones[:], sum0[:, j, k], start=k == 0, stop=k == UK - 1)
                for t in range(2):
                    for k in range(UK):
                        ins = mm(psM[:, 1, t:t + 1], sum0[:, 0, k, t * P:t * P + P], ones[:, 0:1], start=k == 0, stop=k == UK - 1)
                ins.then_inc(ss_done, 1)

            group("mv", None, 0, m_op, {}, rows_major=True, ready=lambda n: pe.wait_ge(memX_lo, n + 1))
            group("mv", None, 1, m_op, {}, rows_major=True)
            with pe.Fori(1, 2) as i:
                for w in range(2):
                    group("mv", i, w, m_op, {2: channel_sums}, rows_major=True)

            def mkq(i, hooks):
                group("mkq", i, 0, m_op, hooks)
                group("mkq", i, 1, x_op, hooks, ready=lambda n: pe.wait_ge(xX_lo, n + 1))

            def plain(phase, i, hooks, operand=x_op, **kw):
                for w in range(2):
                    group(phase, i, w, operand, hooks, **kw)

            mkq(None, {})
            with pe.Fori(1, 4) as i:
                mkq(i, attention_hooks("mem", i - 1))
            plain("lru", None, attention_hooks("mem", 3))
            with pe.Fori(1, 4) as i:
                plain("lru", i, lru_hooks(i - 1))
            plain("v", None, lru_hooks(3), rows_major=True)
            with pe.Fori(1, 2) as i:
                plain("v", i, decay_hooks(), rows_major=True)
            plain("qk", None, {})
            with pe.Fori(1, 4) as i:
                plain("qk", i, attention_hooks("fox", i - 1))
            plain("gate0", None, attention_hooks("fox", 3))

            for q in range(4):
                with pe.Fori(1 if q == 0 else 0, 3) as i:
                    plain(f"gate{q}", i, {})
                if q == 0:
                    pe.wait_ge(side["dve"], SIDE_ALL["dve"])
                with pe.Fori(0, 3) as n:
                    for w in range(2):
                        group(f"branch{q}", n, w,
                              lambda kt: Y[:, bass.ds(n, 1), kt].rearrange("p a h t -> p (a h) t"),
                              {}, per=2, coef=4)
            with pe.Fori(0, 4) as i:
                plain("out", i, {}, operand=lambda kt: merged[:, kt], ready=lambda n: pe.wait_ge(merged_lo, 2 * n + 2))

            def x2_sums():
                pe.wait_ge(x2_sum, 8)
                for t in range(2):
                    ins = mm(psM[:, 0, 0:T], ones[:], sum2[:, t], start=t == 0, stop=t == 1)
                ins.then_inc(x2_ss, 1)

            plain("up", None, {3: x2_sums}, ready=lambda n: pe.wait_ge(h2_lo, 2 * n + 2))
            with pe.Fori(1, FT // 2) as i:
                plain("up", i, {})

            with pe.Fori(0, 2) as i:
                for w in range(4):
                    group("down", i, w, lambda kt: hidden[:, kt], {}, per=FT // UK, coef=4 * (FT // UK),
                          ready=lambda n: pe.wait_ge(hidden_lo, 2 * n + 2))

        evac_at = {last + 4: (g, ph, i, w) for g, (ph, i, w, last) in enumerate(GROUPS) if last + 4 <= U0["up"] + 3}

        def build_hooks(table):
            where = {}
            starts = {"mem": [U0["mkq"] + 8 * (m + 1) for m in range(4)],
                      "lru": [U0["lru"] + 8 * (m + 1) for m in range(4)],
                      "decay": [U0["v"] + 8],
                      "fox": [U0["qk"] + 8 * (m + 1) for m in range(4)]}
            for kind, offs in table.items():
                for m, s in enumerate(starts[kind]):
                    for o, steps in offs.items():
                        for f in steps:
                            where.setdefault(s + o, []).append((f, kind, m))
            return where

        @block.scalar
        def _(act):
            def split(phase, u, i=None, coef=8):
                s = u % SLOTS
                act.wait_ge(raw_full[s], at(16 * (u // SLOTS + 1), i, 16 * coef // SLOTS))
                if u >= SLOTS:
                    act.wait_ge(pe_units, at(u - 3, i, coef))
                nc.scalar.activation(W[:, s, :, 0], raw[:, s], ACT.Copy).then_inc(hi_done, 1)

            def copy_low(g, last, i=None, coef=8, groups=2):
                act.wait_ge(pe_units, at(last + 1, i, coef))
                if g >= 2:
                    act.wait_ge(evac_done, at(g - 1, i, groups))
                b = 2 * (g % 2)
                nc.scalar.activation(low[:, g % 2], psG[:, b:b + 2, T:], ACT.Copy).then_inc(low_copied, 1)

            def wait(**need):
                for e, v in need.items():
                    act.wait_ge(side[e], v)

            def done(ins):
                ins.then_inc(side["act"], 1)

            def squares(kind, m):
                A = att[kind]
                own = G0["mkq" if kind == "mem" else "qk"] + 2 * m + 1
                act.wait_ge(evac_done, own + 1)
                wait(pe=side_count(kind, m, "pe", None), act=side_count(kind, m, "act", None))
                if m == 0:
                    wait(dve=side_count(kind, m, "dve", None))
                if kind == "mem":
                    wait(pool=side_count(kind, m, "pool", "k_scaled"))
                nc.scalar.activation(A["S"][:, 0], A["k_raw"][:], ACT.Square)
                done(nc.scalar.activation(A["S"][:, 1], A["q_raw"][:], ACT.Square))

            def root(kind, m):
                A = att[kind]
                wait(pe=side_count(kind, m, "pe", "sums"))
                if kind == "mem":
                    src, dst, bias = psM[:, 0, :], A["rstd"][:, 0].rearrange("p a t -> p (a t)"), eps[:, 1:2]
                else:
                    src, dst, bias = psM[:, 0:2, :], A["rstd"].rearrange("p j a t -> p j (a t)"), eps[:, 2:3]
                done(nc.scalar.activation(dst, src, ACT.Sqrt, bias=bias))

            def exp(kind, m):
                A = att[kind]
                wait(dve=side_count(kind, m, "dve", "row_max"))
                n = 0
                for h in range(2 if kind == "fox" else 1):
                    for qt in range(2):
                        if kind == "fox":
                            src = dst = causal(A["S"])[:, h, slice(0, P) if qt == 0 else slice(P, CW)]
                        else:
                            src, dst = psM[:, 2, qt * T:(qt + 1) * T], A["S"][:, 0, qt]
                        ins = nc.scalar.activation(dst, src, ACT.Exp, bias=stat[:, 0, n:n + 1], scale=1.0,
                                                   accum_out=stat[:, 1, n:n + 1])
                        n += 1
                done(ins)

            def weights_copied(kind, m):
                A = att[kind]
                wait(pe=side_count(kind, m, "pe", "transposes"))
                if kind == "fox":
                    done(nc.scalar.activation(causal(A["PT"]), psM[:, 0:2, 0:CW], ACT.Copy))
                else:
                    done(nc.scalar.activation(A["PT"][:, 0].rearrange("p k t -> p (k t)"), psM[:, 0, :], ACT.Copy))

            def attention_hi(kind, m):
                wait(pe=side_count(kind, m, "pe", "values"))
                br = 0 if kind == "fox" else 2
                done(nc.scalar.activation(Y[:, br, 2 * m:2 * m + 2, 0, :], psM[:, 2, :].rearrange("p (a t) -> p a t", a=2),
                                          ACT.Copy))

            L = lru

            def conv0_(kind, m):
                act.wait_ge(evac_done, G0["lru"] + 2 * m + 1)
                if m > 0:
                    wait(pe=side_count("lru", m - 1, "pe", "gates"), dve=side_count("lru", m - 1, "dve", "ix"))
                for b in range(2):
                    ins = nc.scalar.activation(L["xr"][:, b], lx_pad[:, b, 3:], ACT.Identity,
                                               bias=p1("b_lconv", 2 * m + b), scale=p1("w_lconv", 3 * BT + 2 * m + b))
                ins.then_inc(lru_conv0, 1)

            def gelu_square(kind, m):
                wait(**{e: side_count("lru", m, e, None) for e in ("pe", "dve", "act", "pool")})
                act.wait_ge(evac_done, G0["lru"] + 2 * m + 2)
                done(nc.scalar.activation(L["gg"][:], L["lg"][:], ACT.Square))

            def gate_tanh(kind, m):
                wait(pe=side_count("lru", m, "pe", "gates"))
                for j, (n, hb) in enumerate([("ra", half_ba), ("ix", half_bx)]):
                    for b in range(2):
                        ins = nc.scalar.activation(L[n][:, b], psM[:, j, b * T:(b + 1) * T], ACT.Tanh, scale=0.5,
                                                   bias=hb[:, 2 * m + b:2 * m + b + 1])
                done(ins)

            def exps(kind, m):
                wait(dve=side_count("lru", m, "dve", "log_a"))
                nc.scalar.activation(L["a"][:], L["ra"][:], ACT.Exp)
                done(nc.scalar.activation(L["tn"][:], L["ra"][:], ACT.Tanh, scale=-1.0))

            def gelu_tanh(kind, m):
                wait(pool=side_count("lru", m, "pool", "gelu_cube"))
                done(nc.scalar.activation(L["gg"][:], L["gg"][:], ACT.Tanh, scale=GELU_S))

            def lru_root(kind, m):
                wait(dve=side_count("lru", m, "dve", "decay_sq"))
                done(nc.scalar.activation(L["aa"][:], L["aa"][:], ACT.Sqrt, scale=0.25, bias=eps[:, 3:4]))

            def lru_hi(kind, m):
                wait(dve=side_count("lru", m, "dve", "y"))
                done(nc.scalar.activation(Y[:, 1, 2 * m:2 * m + 2, 0, :], L["hs"][:], ACT.Copy))

            def decay_exp(kind, m):
                wait(dve=side_count("decay", 0, "dve", "abs"))
                done(nc.scalar.activation(dec["e"][:], dec["r"][:], ACT.Exp, scale=-1.0))

            def decay_ln(kind, m):
                wait(dve=side_count("decay", 0, "dve", "one_plus"))
                done(nc.scalar.activation(dec_l[:], dec["u"][:], ACT.Ln))

            attention = {3: [squares], 4: [root], 8: [exp], 10: [weights_copied], 11: [attention_hi]}
            hooks = build_hooks({"mem": attention, "fox": attention,
                                 "lru": {0: [conv0_], 3: [gelu_square], 5: [gate_tanh], 7: [exps, gelu_tanh], 9: [lru_root], 10: [lru_hi]},
                                 "decay": {6: [decay_exp], 8: [decay_ln]}})

            def root_mean_square(dst, src):
                return nc.scalar.activation(dst, src, ACT.Sqrt, bias=eps[:, 0:1], scale=1.0 / D)

            def gained_hi(dst, src, gain, tiles):
                for k in tiles:
                    ins = nc.scalar.activation(dst[:, k, 0, :], src[:, k], ACT.Copy, scale=p1(gain, k))
                return ins

            act.wait_ge(ones_set, 1)
            nc.scalar.activation(stat[:, 0, 0:1], ones[:, 0:1], ACT.Copy).then_inc(act_warm, 1)
            act.wait_ge(par_in, 16)
            for c in range(4):
                act.wait_ge(mem_in[c], 16)
                for k in range(4 * c, 4 * c + 4):
                    gained_hi(XM, mem_raw, "g_mem", (k,)).then_inc(memX_hi, 1)
                split("mv", c)

            def start_steps(u):
                if u == 10:
                    act.wait_ge(ff_in, 16)
                    for c in (0, 32):
                        ins = nc.scalar.activation(ff_w[:, :, 0, c:c + 8], ff_raw[:], ACT.Copy)
                    ins.then_inc(ff_hi, 1)
                if u == 6:
                    act.wait_ge(lam_dve, 1)
                    nc.scalar.activation(lam_t["e"][:], lam_t["t"][:], ACT.Exp, scale=-1.0).then_inc(lam_act, 1)
                if u == 7:
                    act.wait_ge(lam_dve, 2)
                    nc.scalar.activation(lam_t["l"][:], lam_t["u"][:], ACT.Ln).then_inc(lam_act, 1)
                if u == 14:
                    act.wait_ge(ss_done, 1)
                    root_mean_square(rstd0.rearrange("p j t -> p (j t)"), psM[:, 0, :])
                    root_mean_square(rstd_tok[:], psM[:, 1, 0:2]).then_inc(root_done, 1)
                if 16 <= u < 20:
                    c = u - 16
                    act.wait_ge(x_scaled, c + 1)
                    gained_hi(X, x_n, "g_mix", range(4 * c, 4 * c + 4)).then_inc(xX_hi, 1)

            for u in range(4, U0["up"] + 4):
                if u in evac_at:
                    g, ph, i, w = evac_at[u]
                    copy_low(g, u - 4)
                split("", u)
                start_steps(u)
                for f, kind, m in hooks.get(u, []):
                    f(kind, m)
                if u in evac_at:
                    if ph.startswith("gate"):
                        q = int(ph[4:])
                        act.wait_ge(evac_done, g + 1)
                        for t in range(2):
                            j = i * KT + 4 * q + 2 * w + t
                            ins = nc.scalar.activation(gates[:, i, w, t], gates[:, i, w, t], ACT.Tanh, scale=0.5,
                                                       bias=half_bg[:, j:j + 1])
                        ins.then_inc(gate_ready, 1)
                    if ph.startswith("branch") and i == 2:
                        q = int(ph[6:])
                        act.wait_ge(acc_added, 4 * q + 3 + w)
                        r = 4 * q + 2 * w
                        nc.scalar.activation(merged[:, r:r + 2, 0, :], acc[:, w], ACT.Copy, scale=0.5).then_inc(merged_hi, 1)
                    if ph == "out":
                        n = 2 * i + w
                        act.wait_ge(x2_done, n + 1)
                        if n >= 2:
                            act.wait_ge(x2_sum, n - 1)
                        nc.scalar.activation(sq2[:, n % 2], xs[:, 2 * n:2 * n + 2], ACT.Square).then_inc(x2_sq, 1)
                        gained_hi(X, xs, "g_ffn", (2 * n, 2 * n + 1)).then_inc(h2_hi, 1)

            def up_conv0(i, w):
                act.wait_ge(up_scaled, i * 2 + (w + 1))
                for t in range(2):
                    ins = nc.scalar.activation(up_c[w][:, t], up_pad[w][:, t, 2:], ACT.Identity,
                                               bias=par_at("b_fconv", i * 2 + (w * FT + t)),
                                               scale=par_at("w_fconv", i * 2 + (2 * 2 * FT + w * FT + t)))
                ins.then_inc(conv0, 1)

            def up_iteration(i, split_next, first=False):
                U = U0["up"]
                for k in range(4, 7):
                    split("up", U + k, i)
                copy_low(G0["up"], U + 3, i)
                split("up", U + 7, i)
                if first:
                    act.wait_ge(x2_ss, 1)
                    root_mean_square(rstd2[:], psM[:, 0, 0:T]).then_inc(root_done, 1)
                up_conv0(i, 0)
                split_next(0)
                act.wait_ge(tap0, i * 2 + 1)
                nc.scalar.activation(up_c[0][:], up_c[0][:], ACT.Gelu_apprx_tanh).then_inc(gelu_done, 1)
                split_next(1)
                split_next(2)
                copy_low(G0["up"] + 1, U + 7, i)
                split_next(3)
                up_conv0(i, 1)
                act.wait_ge(prod_done, i + 1)
                nc.scalar.activation(hidden[:, bass.ds(i * 2, 2), 0, :], up_c[1][:], ACT.Copy).then_inc(hidden_hi, 1)

            up_iteration(0, lambda k: split("up", U0["up"] + 8 + k), first=True)
            with act.Fori(1, FT // 2 - 1) as i:
                up_iteration(i, lambda k: split("up", U0["up"] + 8 + k, i))
            with act.Fori(FT // 2 - 1, FT // 2) as i:
                up_iteration(i, lambda k: split("down", U0["down"] + k))

            def down_iteration(i, more):
                per = FT // UK
                for k in range(4, 4 * per + 4):
                    w = (k - 4) // per
                    if (k - 4) % per == per - 1:
                        copy_low(G0["down"] + w, U0["down"] + k - 4, i, coef=4 * per, groups=4)
                    if k < 4 * per or more:
                        split("down", U0["down"] + k, i, coef=4 * per)

            with act.Fori(0, 1) as i:
                down_iteration(i, True)
            with act.Fori(1, 2) as i:
                down_iteration(i, False)

        @block.vector
        def _(dve):
            V = nc.vector

            def split(phase, u, i=None, coef=8):
                s = u % SLOTS
                dve.wait_ge(hi_done, at(u + 1, i, coef))
                V.tensor_tensor(W[:, s, :, 1], raw[:, s], f32(W[:, s, :, 0]), ALU.subtract).then_inc(lo_done, 1)

            def add_low(g, dst, i=None, groups=2):
                dve.wait_ge(low_copied, at(g + 1, i, groups))
                b = 2 * (g % 2)
                V.tensor_tensor(dst, psG[:, b:b + 2, 0:T], low[:, g % 2], ALU.add).then_inc(evac_done, 1)

            def wait(**need):
                for e, v in need.items():
                    dve.wait_ge(side[e], v)

            def done(ins):
                ins.then_inc(side["dve"], 1)

            def chained(kind, m, step):
                dve.wait_ge(side["dve"], side_count(kind, m, "dve", step))

            def inverse_root(kind, m, j):
                A = att[kind]
                rstd = A["rstd"][:, 0, j] if kind == "mem" else A["rstd"][:, j].rearrange("p a t -> p (a t)")
                done(V.reciprocal(rstd, rstd))

            def norm_k(kind, m):
                wait(act=side_count(kind, m, "act", "root"))
                inverse_root(kind, m, 0)

            def normed(kind, m):
                A = att[kind]
                inverse_root(kind, m, 1)
                chained(kind, m, "norm_q")
                if kind == "mem":
                    for t in range(2):
                        V.scalar_tensor_tensor(A["k_n"][:, t], A["k_raw"][:, t], gkm_s[:, t:t + 1], A["rstd"][:, 0, 0], ALU.mult, ALU.mult)
                        ins = V.scalar_tensor_tensor(A["q_n"][:, t], A["q_raw"][:, t], p1("g_qm", t), A["rstd"][:, 0, 1], ALU.mult, ALU.mult)
                else:
                    V.scalar_tensor_tensor(A["k_n"][:], A["k_raw"][:], gk_s[:, 0:1], A["rstd"][:, 0], ALU.mult, ALU.mult)
                    ins = V.scalar_tensor_tensor(A["q_n"][:], A["q_raw"][:], p1("g_q", 0), A["rstd"][:, 1], ALU.mult, ALU.mult)
                done(ins)

            def masked(kind, m):
                A = att[kind]
                wait(pe=side_count(kind, m, "pe", "scores"))
                if kind == "mem":
                    done(V.memset(stat[:, 2], 0.0))
                    return
                done(V.tensor_tensor(causal(A["S"]), psM[:, 2:4, 0:CW], mask.rearrange("p (a t) -> p a t", a=1).to_broadcast([P, 2, CW]),
                                     ALU.add))

            def row_max(kind, m):
                A = att[kind]
                chained(kind, m, "masked")
                if kind == "mem":
                    done(V.tensor_reduce(stat[:, 0, 0:2], psM[:, 2, :].rearrange("p (a t) -> p a t", a=2), AX_X, ALU.max, negate=True))
                else:
                    by_head = stat[:, 0].rearrange("p (h q) -> p h q", h=2)
                    V.tensor_reduce(by_head[:, :, 0:1], causal(A["S"])[:, :, 0:P], AX_X, ALU.max, negate=True)
                    done(V.tensor_reduce(by_head[:, :, 1:2], causal(A["S"])[:, :, P:CW], AX_X, ALU.max, negate=True))

            def row_inv(kind, m):
                wait(act=side_count(kind, m, "act", "exp"))
                n = 4 if kind == "fox" else 2
                done(V.reciprocal(stat[:, 2, 0:n], stat[:, 1, 0:n]))

            def weights(kind, m):
                A = att[kind]
                chained(kind, m, "row_inv")
                n = 0
                for h in range(2 if kind == "fox" else 1):
                    for qt in range(2):
                        S = A["S"][:, h, qt] if kind == "mem" else causal(A["S"])[:, h, slice(0, P) if qt == 0 else slice(P, CW)]
                        ins = V.tensor_scalar(S, S, stat[:, 2, n:n + 1], None, ALU.mult)
                        n += 1
                done(ins)

            def attention_lo(kind, m):
                wait(act=side_count(kind, m, "act", "y_hi"))
                br = 0 if kind == "fox" else 2
                ys = Y[:, br, 2 * m:2 * m + 2]
                done(V.tensor_tensor(ys[:, :, 1, :], psM[:, 2, :].rearrange("p (a t) -> p a t", a=2), f32(ys[:, :, 0, :]), ALU.subtract))

            L = lru

            def taps(kind, m):
                for n in (2, 1, 0):
                    if n == 2:
                        dve.wait_ge(lru_conv0, m + 1)
                    else:
                        dve.wait_ge(lru_taps, 3 * m + 2 - n)
                    for b in range(2):
                        ins = V.scalar_tensor_tensor(L["xr"][:, b], lx_pad[:, b, n:n + T], p1("w_lconv", n * BT + 2 * m + b),
                                                     L["xr"][:, b], ALU.mult, ALU.add)
                    ins.then_inc(lru_taps, 1)

            def log_a(kind, m):
                wait(act=side_count("lru", m, "act", "gate_tanh"))
                for b in range(2):
                    ins = V.tensor_scalar(L["ra"][:, b], L["ra"][:, b], 1.0, ls4[:, 2 * m + b:2 * m + b + 1], ALU.add, ALU.mult)
                done(ins)
                done(V.scalar_tensor_tensor(L["ix"][:], L["ix"][:], 1.0, L["xr"][:], ALU.add, ALU.mult))

            def decay_sq(kind, m):
                wait(pool=side_count("lru", m, "pool", "a_sq"), act=side_count("lru", m, "act", "exps"))
                done(V.scalar_tensor_tensor(L["aa"][:], L["aa"][:], 1.0, L["tn"][:], ALU.add, ALU.mult))

            def recurrence(kind, m):
                wait(act=side_count("lru", m, "act", "root"))
                done(V.tensor_tensor(L["ix"][:], L["ix"][:], L["aa"][:], ALU.mult))
                chained("lru", m, "u")
                for b in range(2):
                    ins = V.tensor_tensor_scan(out=L["hs"][:, b], data0=L["a"][:, b], data1=L["ix"][:, b], initial=0.0,
                                               op0=ALU.mult, op1=ALU.add)
                done(ins)

            def gated_y(kind, m):
                wait(act=side_count("lru", m, "act", "gelu_tanh"))
                done(V.scalar_tensor_tensor(L["gg"][:], L["gg"][:], 1.0, L["lg"][:], ALU.add, ALU.mult))
                chained("lru", m, "gelu")
                done(V.scalar_tensor_tensor(L["hs"][:], L["hs"][:], 0.5, L["gg"][:], ALU.mult, ALU.mult))

            def lru_lo(kind, m):
                wait(act=side_count("lru", m, "act", "y_hi"))
                ys = Y[:, 1, 2 * m:2 * m + 2]
                done(V.tensor_tensor(ys[:, :, 1, :], L["hs"][:], f32(ys[:, :, 0, :]), ALU.subtract))

            def decay_z(kind, m):
                wait(pe=side_count("decay", 0, "pe", "logits"))
                done(V.tensor_copy(dec["e"][:], psM[0:HR, 0, T:]))
                chained("decay", 0, "low")
                done(V.scalar_tensor_tensor(dec["z"][:], psM[0:HR, 0, 0:T], p1("b_f", 0)[0:HR], dec["e"][:], ALU.add, ALU.add))
                chained("decay", 0, "z")
                done(V.scalar_tensor_tensor(dec["r"][:], dec["z"][:], -1.0, dec["z"][:], ALU.mult, ALU.max))

            def decay_one_plus(kind, m):
                wait(act=side_count("decay", 0, "act", "exp"))
                done(V.tensor_scalar(dec["u"][:], dec["e"][:], 1.0, None, ALU.add))

            def decay_inverse(kind, m):
                chained("decay", 0, "one_plus")
                done(V.tensor_scalar(dec["r"][:], dec["u"][:], 1.0, None, ALU.is_equal))
                chained("decay", 0, "is_one")
                wait(act=side_count("decay", 0, "act", "ln"))
                done(V.scalar_tensor_tensor(dec["u"][:], dec["u"][:], -1.0, dec["r"][:], ALU.add, ALU.add))
                chained("decay", 0, "minus_one")
                done(V.reciprocal(dec["u"][:], dec["u"][:]))

            def decay_c(kind, m):
                chained("decay", 0, "inverse")
                done(V.tensor_tensor(dec["u"][:], dec["u"][:], dec_l[:], ALU.mult))
                chained("decay", 0, "ratio")
                done(V.tensor_tensor(dec["u"][:], dec["u"][:], dec["r"][:], ALU.add))
                chained("decay", 0, "ratio1")
                done(V.tensor_tensor(dec["e"][:], dec["u"][:], dec["e"][:], ALU.mult))
                chained("decay", 0, "log1p")
                done(V.scalar_tensor_tensor(dec["z"][:], dec["z"][:], 0.0, dec["e"][:], ALU.min, ALU.subtract))
                chained("decay", 0, "log_f")
                V.memset(dec["r"][:], 1.0).then_inc(setup, 1)
                dve.wait_ge(setup, 2)
                done(V.tensor_tensor_scan(out=dec["u"][:], data0=dec["r"][:], data1=dec["z"][:], initial=0.0,
                                          op0=ALU.mult, op1=ALU.add))

            attention = {4: [norm_k], 5: [normed], 8: [masked, row_max, row_inv, weights], 11: [attention_lo]}
            hooks = build_hooks({"mem": attention, "fox": attention,
                                 "lru": {1: [taps], 6: [log_a], 8: [decay_sq], 9: [recurrence, gated_y], 10: [lru_lo]},
                                 "decay": {5: [decay_z], 7: [decay_one_plus], 8: [decay_inverse], 9: [decay_c]}})

            def gained_lo(dst, src, gain, tiles):
                for k in tiles:
                    ins = V.scalar_tensor_tensor(dst[:, k, 1, :], src[:, k], p1(gain, k), f32(dst[:, k, 0, :]), ALU.mult, ALU.subtract)
                return ins

            V.memset(ones[:], 1.0).then_inc(ones_set, 1)
            V.memset(f32(ff_w[:, :, :, 8:32]), 0.0)
            for j, e in enumerate((EPS, 256 * EPS, 128 * EPS, 1e-33)):
                V.memset(eps[:, j:j + 1], e)
            for c in range(4):
                for k in range(4 * c, 4 * c + 4):
                    dve.wait_ge(memX_hi, k + 1)
                    ins = gained_lo(XM, mem_raw, "g_mem", (k,))
                ins.then_inc(memX_lo, 1)
                split("mv", c)

            def start_steps(u):
                lt = lam_t
                if u == 4:
                    V.tensor_scalar(gk_s[:], p1("g_k", 0), float(np.sqrt(128)), None, ALU.mult)
                    V.tensor_scalar(gkm_s[:], p1("g_km", 0, 2), 16.0, None, ALU.mult)
                    V.tensor_scalar(half_bg[:], p1("b_gate", 0, 3 * KT), 0.5, None, ALU.mult)
                    V.tensor_scalar(half_ba[:], p1("b_a", 0, BT), 0.5, None, ALU.mult)
                    V.tensor_scalar(half_bx[:], p1("b_x", 0, BT), 0.5, None, ALU.mult).then_inc(setup, 1)
                    V.scalar_tensor_tensor(lt["t"][:], p1("lam", 0, BT), -1.0, p1("lam", 0, BT), ALU.mult, ALU.max).then_inc(lam_dve, 1)
                if u == 5:
                    dve.wait_ge(setup, 1)
                if u == 10:
                    dve.wait_ge(ff_hi, 1)
                    for c in (0, 32):
                        ins = V.tensor_tensor(ff_w[:, :, 1, c:c + 8], ff_raw[:], f32(ff_w[:, :, 0, c:c + 8]), ALU.subtract)
                    ins.then_inc(ff_lo, 1)
                if u == 6:
                    dve.wait_ge(lam_act, 1)
                    V.tensor_scalar(lt["u"][:], lt["e"][:], 1.0, None, ALU.add).then_inc(lam_dve, 1)
                    dve.wait_ge(lam_dve, 2)
                    V.tensor_scalar(lt["m"][:], lt["u"][:], 1.0, None, ALU.is_equal).then_inc(lam_dve, 1)
                    dve.wait_ge(lam_dve, 3)
                    V.scalar_tensor_tensor(lt["d"][:], lt["u"][:], -1.0, lt["m"][:], ALU.add, ALU.add).then_inc(lam_dve, 1)
                    dve.wait_ge(lam_dve, 4)
                    V.reciprocal(lt["d"][:], lt["d"][:]).then_inc(lam_dve, 1)
                if u == 8:
                    dve.wait_ge(lam_act, 2)
                    dve.wait_ge(lam_dve, 5)
                    V.tensor_tensor(lt["d"][:], lt["d"][:], lt["l"][:], ALU.mult).then_inc(lam_dve, 1)
                    dve.wait_ge(lam_dve, 6)
                    V.tensor_tensor(lt["d"][:], lt["d"][:], lt["m"][:], ALU.add).then_inc(lam_dve, 1)
                    dve.wait_ge(lam_dve, 7)
                    V.tensor_tensor(lt["e"][:], lt["d"][:], lt["e"][:], ALU.mult).then_inc(lam_dve, 1)
                    dve.wait_ge(lam_dve, 8)
                    V.scalar_tensor_tensor(lt["d"][:], p1("lam", 0, BT), 0.0, lt["e"][:], ALU.min, ALU.subtract).then_inc(lam_dve, 1)
                    dve.wait_ge(lam_dve, 9)
                    V.tensor_scalar(ls4[:], lt["d"][:], 4.0, None, ALU.mult).then_inc(side["dve"], 1)
                if u == 14:
                    dve.wait_ge(root_done, 1)
                    V.reciprocal(rstd0[:], rstd0[:])
                    V.reciprocal(rstd_tok[:], rstd_tok[:]).then_inc(rstd_done, 1)
                if 16 <= u < 20:
                    c = u - 16
                    dve.wait_ge(xX_hi, c + 1)
                    gained_lo(X, x_n, "g_mix", range(4 * c, 4 * c + 4)).then_inc(xX_lo, 1)

            def destination(ph, i, w):
                if ph in ("mv", "v"):
                    c = (2 * i + w) * UC
                    return (mem_v if ph == "mv" else v_all)[:, :, c:c + UC]
                if ph in ("mkq", "qk"):
                    A = att["mem" if ph == "mkq" else "fox"]
                    return A["k_raw" if (w == 0) == (ph == "mkq") else "q_raw"][:]
                if ph == "lru":
                    return lx_pad[:, :, 3:] if w == 0 else lru["lg"][:]
                if ph.startswith("gate"):
                    return gates[:, i, w]
                return yd[:]

            n_gated = 0
            for u in range(4, U0["up"] + 4):
                if u in evac_at:
                    g, ph, i, w = evac_at[u]
                    if ph == "lru" and i == 0 and w == 0:
                        dve.wait_ge(side["pool"], side_count("mem", 3, "pool", "values_staged"))
                        V.memset(lx_pad[:, :, 0:3], 0.0)
                    if ph in ("mkq", "qk") and i > 0 and w == 0:
                        chained("mem" if ph == "mkq" else "fox", i - 1, "normed")
                    if ph == "lru" and i > 0 and w == 0:
                        dve.wait_ge(lru_taps, 3 * i)
                    if ph == "gate0" and i == 1 and w == 0:
                        dve.wait_ge(side["pe"], side_count("fox", 3, "pe", "scores"))
                    if ph.startswith("branch"):
                        dve.wait_ge(gated, n_gated)
                    if ph == "out":
                        dve.wait_ge(x2_done if 2 * i + w else gated, 2 * i + w or n_gated)
                    if ph.startswith("gate") and ph != "gate0" and i == 0:
                        dve.wait_ge(acc_added, 4 * int(ph[4:]))
                    add_low(g, destination(ph, i, w))
                    if ph.startswith("branch"):
                        q = int(ph[6:])
                        dve.wait_ge(evac_done, g + 1)
                        dve.wait_ge(gate_ready, 6 * q + 2 * i + w + 1)
                        n_gated += 1
                        dst = acc[:, w] if i == 0 else gates[:, i, w]
                        V.scalar_tensor_tensor(dst, gates[:, i, w], 1.0, yd[:], ALU.add, ALU.mult).then_inc(gated, 1)
                        if i > 0:
                            dve.wait_ge(gated, n_gated)
                            if i == 2:
                                dve.wait_ge(acc_added, 4 * int(ph[6:]) + 1 + w)
                            V.tensor_tensor(acc[:, w], acc[:, w], gates[:, i, w], ALU.add).then_inc(acc_added, 1)
                    if ph == "out":
                        n = 2 * i + w
                        dve.wait_ge(evac_done, g + 1)
                        V.tensor_tensor(xs[:, 2 * n:2 * n + 2], xs[:, 2 * n:2 * n + 2], yd[:], ALU.add).then_inc(x2_done, 1)
                split("", u)
                start_steps(u)
                for f, kind, m in hooks.get(u, []):
                    f(kind, m)
                if u in evac_at and ph.startswith("branch") and i == 2:
                    q = int(ph[6:])
                    r = 4 * q + 2 * w
                    dve.wait_ge(merged_hi, 2 * q + w + 1)
                    V.scalar_tensor_tensor(merged[:, r:r + 2, 1, :], acc[:, w], 0.5, f32(merged[:, r:r + 2, 0, :]),
                                           ALU.mult, ALU.subtract).then_inc(merged_lo, 1)
                if u in evac_at and ph == "out":
                    n = 2 * i + w
                    dve.wait_ge(h2_hi, n + 1)
                    gained_lo(X, xs, "g_ffn", (2 * n, 2 * n + 1)).then_inc(h2_lo, 1)

            for w in range(2):
                ins = V.memset(up_pad[w][:, :, 0:2], 0.0)
            ins.then_inc(setup, 1)
            dve.wait_ge(setup, 3)

            def up_scale(i, w):
                dve.wait_ge(evac_done, at(G0["up"] + w + 1, i, 2))
                V.tensor_tensor(up_pad[w][:, :, 2:], up_pad[w][:, :, 2:], rstd2.rearrange("p (a t) -> p a t", a=1).to_broadcast([P, 2, T]),
                                ALU.mult).then_inc(up_scaled, 1)

            def up_taps(i, w):
                for n, s_from, s_to in ((1, conv0, tap1), (0, tap1, tap0)):
                    dve.wait_ge(s_from, i * 2 + (w + 1))
                    for t in range(2):
                        ins = V.scalar_tensor_tensor(up_c[w][:, t], up_pad[w][:, t, n:n + T],
                                                     par_at("w_fconv", i * 2 + (n * 2 * FT + w * FT + t)),
                                                     up_c[w][:, t], ALU.mult, ALU.add)
                    ins.then_inc(s_to, 1)

            def up_iteration(i, split_next, first=False):
                U = U0["up"]
                for k in range(4, 7):
                    split("up", U + k, i)
                add_low(G0["up"], up_pad[0][:, :, 2:], i)
                split("up", U + 7, i)
                if first:
                    dve.wait_ge(root_done, 2)
                    V.reciprocal(rstd2[:], rstd2[:]).then_inc(rstd_done, 1)
                    dve.wait_ge(rstd_done, 2)
                up_scale(i, 0)
                up_taps(i, 0)
                for k in range(3):
                    split_next(k)
                add_low(G0["up"] + 1, up_pad[1][:, :, 2:], i)
                up_scale(i, 1)
                split_next(3)
                up_taps(i, 1)
                dve.wait_ge(tap0, i * 2 + 2)
                dve.wait_ge(gelu_done, i + 1)
                V.tensor_tensor(up_c[1][:], up_c[0][:], up_c[1][:], ALU.mult).then_inc(prod_done, 1)
                dve.wait_ge(hidden_hi, i + 1)
                hs = hidden[:, bass.ds(i * 2, 2)]
                V.tensor_tensor(hs[:, :, 1, :], up_c[1][:], f32(hs[:, :, 0, :]), ALU.subtract).then_inc(hidden_lo, 1)

            up_iteration(0, lambda k: split("up", U0["up"] + 8 + k), first=True)
            with dve.Fori(1, FT // 2 - 1) as i:
                up_iteration(i, lambda k: split("up", U0["up"] + 8 + k, i))
            with dve.Fori(FT // 2 - 1, FT // 2) as i:
                up_iteration(i, lambda k: split("down", U0["down"] + k))

            def down_iteration(i, more):
                per = FT // UK
                for k in range(4, 4 * per + 4):
                    w = (k - 4) // per
                    if (k - 4) % per == per - 1:
                        g = G0["down"] + w
                        dve.wait_ge(out_done, i * 4 + w) if w else None
                        add_low(g, yd[:], i, groups=4)
                        dve.wait_ge(evac_done, at(g + 1, i, 4))
                        tiles = xs[:, bass.ds(i * 8 + 2 * w, 2)]
                        V.tensor_tensor(tiles, yd[:], tiles, ALU.add).then_inc(out_done, 1)
                    if k < 4 * per or more:
                        split("down", U0["down"] + k, i, coef=4 * per)

            with dve.Fori(0, 1) as i:
                down_iteration(i, True)
            with dve.Fori(1, 2) as i:
                down_iteration(i, False)

        @block.gpsimd
        def _(pool):
            G = nc.gpsimd

            def wait(**need):
                for e, v in need.items():
                    pool.wait_ge(side[e], v)

            def done(ins):
                ins.then_inc(side["pool"], 1)

            for j, (src, arrived) in enumerate(((mem_raw, mem_in), (xs, x_in))):
                for c in range(4):
                    pool.wait_ge(arrived[c], 16)
                    chunk = src[:, 4 * c:4 * c + 4]
                    if c == 0:
                        G.tensor_tensor(sum0[:, j], chunk, chunk, ALU.mult).then_inc(pool_step, 1)
                        continue
                    pool.wait_ge(pool_step, 6 * j + 2 * c - 1)
                    G.tensor_tensor(sq0[:], chunk, chunk, ALU.mult).then_inc(pool_step, 1)
                    pool.wait_ge(pool_step, 6 * j + 2 * c)
                    ins = G.tensor_tensor(sum0[:, j], sum0[:, j], sq0[:], ALU.add).then_inc(pool_step if c < 3 else sq_done, 1)

            pool.wait_ge(rstd_done, 1)
            for c in range(4):
                G.tensor_tensor(x_n[:, 4 * c:4 * c + 4], xs[:, 4 * c:4 * c + 4],
                                rstd0[:, 1:2].to_broadcast([P, 4, T]), ALU.mult).then_inc(x_scaled, 1)

            def scale_k(m):
                k_raw = att["mem"]["k_raw"]
                pool.wait_ge(evac_done, G0["mkq"] + 2 * m + 1)
                done(G.tensor_tensor(k_raw[:], k_raw[:], rstd0[:, 0:1].to_broadcast([P, 2, T]), ALU.mult))

            def stage_values(kind, m):
                A = att[kind]
                wait(pe=side_count(kind, m, "pe", None))
                last = G0["mv"] + 3 if kind == "mem" else G0["v"] + 3
                pool.wait_ge(evac_done, last + 1)
                if kind == "mem":
                    for t in range(2):
                        ins = G.tensor_scalar(A["v_cur"][:, t], mem_v[:, t, m * T:(m + 1) * T], rstd_tok[:, t:t + 1], None, ALU.mult)
                    done(ins)
                else:
                    done(G.tensor_copy(A["v_cur"][:], v_all[:, :, m * T:(m + 1) * T]))

            def load_gates(m):
                if m == 0:
                    pool.wait_ge(pe_units, U0["lru"])
                wait(pe=side_count("lru", m, "pe", None))
                for j in range(2):
                    G.dma_start(lru["rg"][:, j], w_rg[j, 2 * m:2 * m + 2].rearrange("b n c -> n b c")).then_inc(rg_in, 16)

            L = lru
            for m in range(4):
                scale_k(m)
                stage_values("mem", m)
            for m in range(4):
                load_gates(m)
                wait(act=side_count("lru", m, "act", "gelu_square"))
                done(G.tensor_scalar(L["gg"][:], L["gg"][:], GELU_C, 1.0, ALU.mult, ALU.add))
                wait(pool=side_count("lru", m, "pool", "gelu_poly"))
                done(G.tensor_tensor(L["gg"][:], L["gg"][:], L["lg"][:], ALU.mult))
                wait(act=side_count("lru", m, "act", "exps"))
                done(G.tensor_tensor(L["aa"][:], L["a"][:], L["a"][:], ALU.mult))
            wait(dve=side_count("decay", 0, "dve", "c"))
            for h in range(8):
                G.tensor_scalar(rhs_c[:, h], dec["u"][:], rows_sel[0:HR, h:h + 1], ident[0:HR, 32 + h:33 + h], ALU.mult, ALU.add)
            done(G.tensor_scalar(lhs_c[:], dec["u"][:], rows_sel[0:HR, 8:9], rows_sel[0:HR, 9:10], ALU.mult, ALU.add))
            for m in range(4):
                stage_values("fox", m)

            for n in range(8):
                pool.wait_ge(x2_sq, n + 1)
                if n == 0:
                    G.tensor_copy(sum2[:], sq2[:, 0]).then_inc(x2_sum, 1)
                else:
                    pool.wait_ge(x2_sum, n)
                    G.tensor_tensor(sum2[:], sum2[:], sq2[:, n % 2], ALU.add).then_inc(x2_sum, 1)

            with pool.Fori(0, KT // 2 - 1) as i:
                pool.wait_ge(out_done, i + 1)
                G.dma_start(outT[bass.ds(i * UC, UC), :].rearrange("(a p) t -> p a t", p=P), xs[:, bass.ds(i * 2, 2)]).then_inc(out_stored, 16)
            pool.wait_ge(out_stored, 16 * (KT // 2 - 1))


def _columns(v):
    return np.reshape(v, (-1, P)).T


def kernel(x, mem, g_mix, w_in, b_f, g_q_fox, g_k_fox, w_lru_conv, b_lru_conv, w_rg_a, b_rg_a, w_rg_x, b_rg_x,
           lru_lambda, g_mem, w_mem_kv, g_q_mem, g_k_mem, b_gate, w_branch, w_out, g_ffn, w_ffn_up, w_ffn_conv,
           b_ffn_conv, w_ffn_down):
    import concourse.bacc as bacc
    from concourse.bass_utils import run_bass_kernel_spmd

    A = np.asarray
    bf = np.zeros((P, 1), A(b_f).dtype)
    bf[0:8, 0] = A(b_f)[0]
    bf[32:40, 0] = A(b_f)[0]
    packed = [_columns(A(v)[0].reshape(-1)) for v in
              (g_mix, g_mem, g_ffn, b_gate, w_ffn_conv, b_ffn_conv, w_lru_conv, b_lru_conv, b_rg_a, b_rg_x, lru_lambda,
               g_q_fox, g_k_fox, g_q_mem, g_k_mem)]
    par = np.ascontiguousarray(np.concatenate(packed + [bf], axis=1))
    assert par.shape == (P, N_PAR)
    key = np.arange(T)
    mask = [np.where(key[None, :(qt + 1) * P] <= (qt * P + np.arange(P))[:, None], 0.0, MASKED) for qt in range(2)]
    high = ((np.arange(P) >= 32) & (np.arange(P) < 64))[:, None]
    shapes_const = np.concatenate([np.eye(P)] + mask + [-np.eye(P)[:, 0:8], high, ~high], axis=1).astype(np.float32)
    arrays = {
        "xT": np.ascontiguousarray(A(x)[0].T), "memT": np.ascontiguousarray(A(mem)[0].T), "par": par,
        "shapes_const": shapes_const, "w_in": A(w_in)[0], "w_mem_kv": A(w_mem_kv)[0],
        "w_rg": np.stack([A(w_rg_a)[0], A(w_rg_x)[0]]), "w_branch": A(w_branch)[0].reshape(3 * BW, D),
        "w_out": A(w_out)[0], "w_up": A(w_ffn_up)[0], "w_down": A(w_ffn_down)[0],
    }
    nc = bacc.Bacc("TRN2", target_bir_lowering=False, num_devices=1)
    args = [nc.dram_tensor(n, a.shape, mybir.dt.from_np(a.dtype), kind="ExternalInput").ap() for n, a in arrays.items()]
    args.append(nc.dram_tensor("outT", (D, T), F32, kind="ExternalOutput").ap())
    hybrid_layer_kernel(nc, *args)
    r = run_bass_kernel_spmd(nc, [arrays], core_ids=[0])
    return np.ascontiguousarray(r.results[0]["outT"].T)[None]
```

```python
from contextlib import ExitStack

import numpy as np
import concourse.bass as bass
from concourse import mybir

ALU = mybir.AluOpType
ACT = mybir.ActivationFunctionType
F32 = mybir.dt.float32
F32R = mybir.dt.float32r
AX_X = mybir.AxisListType.X

P = 128
T = 256
D = 2048
KT = D // P
BW = 1024
BT = BW // P
FFN = 5632
FT = FFN // P
EPS = 1e-6
UK, UC = 4, 256
SLOTS = 4
GELU_C, GELU_S = 0.044715, float(np.sqrt(2.0 / np.pi))
MASKED = -1e30
HR = 40
CW = P + T

COL_Q, COL_K, COL_V, COL_FF = 0, BW, 2 * BW, 3 * BW
COL_LX = 3 * BW + 8
COL_LG, COL_MQ, COL_GATE = COL_LX + BW, COL_LX + 2 * BW, COL_LX + 3 * BW

PHASES = [("mv", 2, 4), ("mkq", 4, 4), ("lru", 4, 4), ("v", 2, 4), ("qk", 4, 4)]
for _q in range(4):
    PHASES += [(f"gate{_q}", 3, 4), (f"branch{_q}", 3, 2)]
PHASES += [("out", 4, 4), ("up", FT // 2, 4), ("down", 2, FT // UK)]
NG = {_name: 4 if _name == "down" else 2 for _name, _, _ in PHASES}
U0, G0 = {}, {}
GROUPS = []
_u = 0
for _name, _n, _per in PHASES:
    U0[_name], G0[_name] = _u, len(GROUPS)
    for _i in range(_n):
        for _w in range(NG[_name]):
            GROUPS.append((_name, _i, _w, _u + _per - 1))
            _u += _per

PAR = {}
_c = 0
for _name, _n in [("g_mix", KT), ("g_mem", KT), ("g_ffn", KT), ("b_gate", 3 * KT), ("w_fconv", 3 * 2 * FT),
                  ("b_fconv", 2 * FT), ("w_lconv", 4 * BT), ("b_lconv", BT), ("b_a", BT), ("b_x", BT),
                  ("lam", BT), ("g_q", 1), ("g_k", 1), ("g_qm", 2), ("g_km", 2), ("b_f", 1)]:
    PAR[_name] = _c
    _c += _n
N_PAR = _c

def _attention(heads, pool):
    by_head = lambda *steps: [f"{step}{h}" for h in range(heads) for step in steps]
    return {
        "pe": ["sums", "scores", "transposes", "values"],
        "act": ["squares", "root"] + by_head("exp") + ["weights_copied", "y_hi"],
        "dve": ["norm_k", "norm_q", "normed"] + by_head(*(["masked"] if heads > 1 else []), "row_max")
               + by_head("row_inv", "weights") + ["y_lo"],
        "pool": pool,
    }


KINDS = [
    ("mem", 4, _attention(1, ["k_scaled", "squares_added", "values_staged"])),
    ("lru", 4, {
        "pe": ["gates"],
        "act": ["gelu_square", "gate_tanh", "exps", "gelu_tanh", "root", "y_hi"],
        "dve": ["log_a", "ix", "decay_sq", "u", "scan", "gelu", "y", "y_lo"],
        "pool": ["gelu_poly", "gelu_cube", "a_sq"],
    }),
    ("decay", 1, {
        "pe": ["logits"],
        "act": ["exp", "ln"],
        "dve": ["low", "z", "abs", "one_plus", "is_one", "minus_one", "inverse", "ratio", "ratio1",
                "log1p", "log_f", "c"],
        "pool": ["columns"],
    }),
    ("fox", 4, _attention(2, ["values_staged"])),
]
LEN = {k: {e: len(s) for e, s in steps.items()} for k, _, steps in KINDS}
STEP = {k: {e: {n: j + 1 for j, n in enumerate(s)} for e, s in steps.items()} for k, _, steps in KINDS}
BASE, _sum = {}, {"pe": 0, "act": 0, "dve": 1, "pool": 0}
for _k, _n, _ in KINDS:
    BASE[_k] = dict(_sum)
    for _e in _sum:
        _sum[_e] += _n * LEN[_k][_e]
SIDE_ALL = dict(_sum)


def side_count(kind, m, engine, step):
    return m * LEN[kind][engine] + (BASE[kind][engine] + (STEP[kind][engine][step] if step else 0))


def at(const, i, coef):
    return const if i is None else i * coef + const


def hybrid_layer_kernel(nc, xT, memT, par, shapes_const, w_in, w_mem_kv, w_rg, w_branch, w_out, w_up, w_down, outT):
    with ExitStack() as ctx:
        KB = 1024
        SB0 = 16512
        TOP = 212856

        def sb(name, shape, offset, dt=F32):
            return nc.alloc_sbuf_tensor_at(name, shape, dt, offset=SB0 + int(offset))

        def sem(name):
            return ctx.enter_context(nc.semaphore(name))

        W = sb("W", [P, SLOTS, UK, 2, UC], 0, F32R)
        raw = sb("raw", [P, SLOTS, UK, UC], 32 * KB)
        X = sb("X", [P, KT, 2, T], 48 * KB, F32R)
        xs = sb("xs", [P, KT, T], 80 * KB)
        Y = sb("Y", [P, 3, BT, 2, T], 96 * KB, F32R)
        M0, G_0, T0 = 144 * KB, 176 * KB, 192 * KB
        XM = sb("XM", [P, KT, 2, T], M0, F32R)
        merged = sb("merged", [P, KT, 2, T], M0, F32R)
        mem_raw = sb("mem_raw", [P, KT, T], 96 * KB)
        x_n = sb("x_n", [P, KT, T], 128 * KB)
        sq0 = sb("sq0", [P, UK, T], 112 * KB)
        sum0 = sb("sum0", [P, 2, UK, T], 116 * KB)
        sum1 = sb("sum1", [P, 2, T], 124 * KB)
        rstd0 = sb("rstd0", [P, 2, T], G_0 + 8 * KB)
        ff_raw = sb("ff_raw", [P, KT, 8], G_0 + 10 * KB)
        ff_w = sb("ff_w", [P, KT, 2, HR], T0, F32R)
        mem_v = sb("mem_v", [P, 2, BW], G_0)

        def attention_buffers(tag, base):
            names = [("k_raw", [P, 2, T]), ("q_raw", [P, 2, T]), ("k_n", [P, 2, T]), ("q_n", [P, 2, T]),
                     ("S", [P, 2, 2, T]), ("PT", [P, 2, 2, T]), ("v_cur", [P, 2, T])]
            out, o = {}, base
            for n, shape in names:
                out[n] = sb(f"{tag}_{n}", shape, o)
                if n == "PT":
                    out["rstd"] = sb(f"{tag}_rstd", [P, 2, 2, T], o)
                o += int(np.prod(shape[1:])) * 4
            return out

        att = {"mem": attention_buffers("mem", 96 * KB), "fox": attention_buffers("fox", M0)}
        causal = lambda t: t.rearrange("p h a t -> p h (a t)")[:, :, 0:CW]
        v_all = sb("v_all", [P, 2, BW], M0 + 22784)
        lx_pad = sb("lx_pad", [P, 2, 3 + T], M0)
        _o = M0 + 2080
        lru = {}
        for n in ["lg", "rg", "xr", "ra", "a", "aa", "tn", "ix", "hs", "gg"]:
            shape = [P, 2, 2, P] if n == "rg" else [P, 2, T]
            lru[n] = sb(f"lru_{n}", shape, _o)
            _o += 2 * KB
        lhs_c = sb("lhs_c", [HR, T], T0 + 4 * KB)
        dec = {n: sb(f"dec_{n}", [HR, T], G_0 + (12 + j) * KB) for j, n in enumerate(["z", "e", "u", "r"])}
        dec_l = sb("dec_l", [HR, T], T0 + 2 * KB + 512)
        rhs_c = sb("rhs_c", [HR, 8, T], G_0 + 4 * KB)
        gates = sb("gates", [P, 3, 2, 2, T], G_0)
        acc = sb("acc", [P, 2, 2, T], G_0 + 12 * KB)
        yd = sb("yd", [P, 2, T], T0 + 64)
        sq2 = sb("sq2", [P, 2, 2, T], G_0)
        sum2 = sb("sum2", [P, 2, T], G_0 + 4 * KB)
        rstd2 = sb("rstd2", [P, T], T0 + 5 * KB)
        hidden = sb("hidden", [P, FT, 2, T], 96 * KB, F32R)
        up_pad = {w: sb(f"up_pad{w}", [P, 2, 2 + T], 184 * KB + w * 2080) for w in range(2)}
        up_c = {w: sb(f"up_c{w}", [P, 2, T], 184 * KB + 4160 + w * 2048) for w in range(2)}
        low = sb("low", [P, 2, 2, T], T0 + 6 * KB)

        next_free = [202 * KB]

        def const_sb(name, shape):
            t = sb(name, shape, next_free[0])
            next_free[0] += -(-4 * int(np.prod(shape[1:])) // 32) * 32
            return t

        par_sb = const_sb("par_sb", [P, N_PAR])
        ident = const_sb("ident", [P, P])
        rows_sel = const_sb("rows_sel", [P, 10])
        mask = const_sb("mask", [P, CW])
        ones = const_sb("ones", [P, P])
        half_bg = const_sb("half_bg", [P, 3 * KT])
        half_ba = const_sb("half_ba", [P, BT])
        half_bx = const_sb("half_bx", [P, BT])
        ls4 = const_sb("ls4", [P, BT])
        rstd_tok = const_sb("rstd_tok", [P, 2])
        gk_s = const_sb("gk_s", [P, 1])
        gkm_s = const_sb("gkm_s", [P, 2])
        stat = const_sb("stat", [P, 3, 4])
        eps = const_sb("eps", [P, 4])
        lam_t = {n: sb(f"lam_{n}", [P, BT], G_0 + 11 * KB + 32 * j) for j, n in enumerate(["t", "e", "u", "m", "d", "l"])}
        assert next_free[0] <= TOP, next_free[0]

        psG = ctx.enter_context(nc.psum_tensor("psG", [P, 4, 512], F32))
        psM = ctx.enter_context(nc.psum_tensor("psM", [P, 4, 512], F32))

        raw_full = [sem(f"raw_full{s}") for s in range(SLOTS)]
        hi_done, lo_done = sem("hi_done"), sem("lo_done")
        pe_units = sem("pe_units")
        low_copied, evac_done = sem("low_copied"), sem("evac_done")
        side = {e: sem(f"side_{e}") for e in ("pe", "act", "dve", "pool")}
        mem_in = [sem(f"mem_in{c}") for c in range(4)]
        x_in = [sem(f"x_in{c}") for c in range(4)]
        par_in, const_in, ff_in, rg_in = sem("par_in"), sem("const_in"), sem("ff_in"), sem("rg_in")
        setup, ones_set, pool_step = sem("setup"), sem("ones_set"), sem("pool_step")
        act_warm = sem("act_warm")
        sq_done, ss_done, rstd_done = sem("sq_done"), sem("ss_done"), sem("rstd_done")
        x_scaled = sem("x_scaled")
        memX_hi, memX_lo, xX_hi, xX_lo = sem("memX_hi"), sem("memX_lo"), sem("xX_hi"), sem("xX_lo")
        ff_hi, ff_lo = sem("ff_hi"), sem("ff_lo")
        lam_act, lam_dve = sem("lam_act"), sem("lam_dve")
        lru_conv0, lru_taps = sem("lru_conv0"), sem("lru_taps")
        gate_ready = sem("gate_ready")
        gated, acc_added, merged_hi, merged_lo = sem("gated"), sem("acc_added"), sem("merged_hi"), sem("merged_lo")
        x2_done, x2_sq, x2_sum, x2_ss, root_done = \
            sem("x2_done"), sem("x2_sq"), sem("x2_sum"), sem("x2_ss"), sem("root_done")
        h2_hi, h2_lo, up_scaled = sem("h2_hi"), sem("h2_lo"), sem("up_scaled")
        conv0, tap1, tap0, gelu_done = sem("conv0"), sem("tap1"), sem("tap0"), sem("gelu_done")
        prod_done, hidden_hi, hidden_lo = sem("prod_done"), sem("hidden_hi"), sem("hidden_lo")
        out_done = sem("out_done")
        out_stored, last_stored = sem("out_stored"), sem("last_stored")

        def p1(name, j, n=1):
            return par_sb[:, bass.ds(j + PAR[name], n)]

        def is_zero(m):
            return isinstance(m, int) and m == 0

        def f32(ap):
            return ap.bitcast(F32)

        rows = lambda w: w.rearrange("(k p) c -> p k c", p=P)
        w_in_r, w_kv_r, w_br_r, w_out_r, w_up_r, w_down_r = map(rows, (w_in, w_mem_kv, w_branch, w_out, w_up, w_down))

        def unit_source(phase, i, k, q):
            if phase == "down":
                w, kk = k // (FT // UK), k % (FT // UK)
                return w_down_r[:, kk * UK:(kk + 1) * UK, bass.ds(i * (4 * UC) + w * UC, UC)]
            if phase == "branch0":
                return w_br_r[:, bass.ds(i * BT + (k % 2) * UK, UK), bass.ds(q * (2 * UC) + (k // 2) * UC, UC)]
            w, kk = k // 4, k % 4
            if phase == "gate0":
                src, col = w_in_r, i * D + q * (2 * UC) + (COL_GATE + w * UC)
            elif phase == "mv":
                src, col = w_kv_r, i * (2 * UC) + (BW + w * UC)
            elif phase == "mkq":
                src, col = (w_kv_r, i * UC) if w == 0 else (w_in_r, i * UC + COL_MQ)
            elif phase == "lru":
                src, col = w_in_r, i * UC + (COL_LX if w == 0 else COL_LG)
            elif phase == "v":
                src, col = w_in_r, i * (2 * UC) + (COL_V + w * UC)
            elif phase == "qk":
                src, col = w_in_r, i * UC + (COL_Q if w == 0 else COL_K)
            elif phase == "out":
                src, col = w_out_r, i * (2 * UC) + w * UC
            else:
                src, col = w_up_r, i * UC + w * FFN
            return src[:, kk * UK:(kk + 1) * UK, bass.ds(col, UC)]

        QUARTER0, QUARTER_UNITS = U0["gate0"], U0["gate1"] - U0["gate0"]
        QUARTER_GROUPS = G0["gate1"] - G0["gate0"]
        quarter_groups = {last + 4 - QUARTER0: (ph[:-1], i, w, g - G0["gate0"])
                          for g, (ph, i, w, last) in enumerate(GROUPS) if ph in ("gate0", "branch0")}

        block = ctx.enter_context(nc.Block())

        @block.sync
        def _(sp):
            def load(phase, i, k, u, coef, before=0, q=0):
                s = u % SLOTS
                if i is not None or u >= SLOTS:
                    sp.wait_ge(lo_done, at(u - 3, i, coef) + before)
                sp.dma_start(raw[:, s], unit_source(phase, 0 if i is None else i, k, q)).then_inc(raw_full[s], 16)

            mem_r = memT.rearrange("(k p) t -> p k t", p=P)
            x_r = xT.rearrange("(k p) t -> p k t", p=P)
            sp.dma_start(par_sb[:], par).then_inc(par_in, 16)
            for c in range(4):
                load("mv", None, c, c, 0)
                sp.dma_start(mem_raw[:, 4 * c:4 * c + 4], mem_r[:, 4 * c:4 * c + 4]).then_inc(mem_in[c], 16)
            for c in range(4):
                sp.dma_start(xs[:, 4 * c:4 * c + 4], x_r[:, 4 * c:4 * c + 4]).then_inc(x_in[c], 16)
                load("mv", None, 4 + c, 4 + c, 0)
            sp.dma_start(rows_sel[:], shapes_const[:, P + CW:]).then_inc(const_in, 16)
            sp.dma_start(ident[:], shapes_const[:, 0:P]).then_inc(const_in, 16)
            sp.dma_start(mask[:], shapes_const[:, P:P + CW]).then_inc(const_in, 16)
            sp.dma_start(ff_raw[:], w_in_r[:, :, COL_FF:COL_FF + 8]).then_inc(ff_in, 16)
            def load_phase(name, first=0, before=0, q=0):
                n, per = next((n, per) for ph, n, per in PHASES if ph == name)
                with sp.Fori(first, n) as i:
                    for k in range(NG[name] * per):
                        load(name, i, k, U0[name] + k, NG[name] * per, before, q)

            load_phase("mv", first=1)
            for name in ("mkq", "lru", "v", "qk"):
                load_phase(name)
            with sp.Fori(0, 4) as q:
                load_phase("gate0", before=q * QUARTER_UNITS, q=q)
                load_phase("branch0", before=q * QUARTER_UNITS, q=q)
            for name in ("out", "up", "down"):
                load_phase(name)
            for t in (KT - 2, KT - 1):
                sp.wait_ge(out_done, KT // 2)
                sp.dma_start(outT[t * P:(t + 1) * P], xs[:, t]).then_inc(last_stored, 16)
            sp.wait_ge(last_stored, 32)

        @block.tensor
        def _(pe):
            def mm(*a, **kw):
                return nc.tensor.matmul(*a, skip_group_check=True, **kw)

            def group(phase, i, w, operand, hooks, per=4, coef=8, rows_major=False, ready=None,
                      tile_ready=None, before=(0, 0)):
                b = 2 * (w % 2)
                g = G0[phase] + w
                if i is not None or g >= 2:
                    pe.wait_ge(evac_done, at(g - 1, i, NG[phase]) + before[1])
                last = per * UK - 1
                for n in range(per):
                    u = U0[phase] + per * w + n
                    s = u % SLOTS
                    pe.wait_ge(lo_done, at(u + 1, i, coef) + before[0])
                    if ready is not None:
                        ready(n)
                    for k in range(UK):
                        kt = n * UK + k
                        if tile_ready is not None:
                            tile_ready(kt)
                        x_hl = operand(kt)
                        for t in range(2):
                            ts = slice(t * P, t * P + P)
                            if rows_major:
                                mm(psG[:, b + t, :], x_hl[:, 0, ts], W[:, s, k], start=kt == 0, stop=False)
                                ins = mm(psG[:, b + t, T:], x_hl[:, 1, ts], W[:, s, k, 0], start=False, stop=kt == last)
                            else:
                                mm(psG[:, b + t, :], W[:, s, k, 0, ts], x_hl, start=kt == 0, stop=False)
                                ins = mm(psG[:, b + t, T:], W[:, s, k, 1, ts], x_hl[:, 0], start=False, stop=kt == last)
                    ins.then_inc(pe_units, 1)
                    if per * w + n in hooks:
                        hooks[per * w + n]()

            def side_waits(**need):
                for e, v in need.items():
                    if not is_zero(v):
                        pe.wait_ge(side[e], v)

            def done(ins):
                ins.then_inc(side["pe"], 1)

            def attention_hooks(kind, m):
                A = att[kind]

                def sums():
                    if kind == "fox":
                        side_waits(act=side_count(kind, m, "act", "squares"))
                        for j in range(2):
                            ins = mm(psM[:, j, :], ones[:], A["S"][:, j].rearrange("p a t -> p (a t)"), start=True, stop=True)
                    else:
                        side_waits(pool=side_count(kind, m, "pool", "squares_added"))
                        ins = mm(psM[:, 0, :].rearrange("p (j t) -> p j t", j=2), ones[:], A["S"][:, :, 0], start=True, stop=True)
                    done(ins)

                def scores():
                    side_waits(dve=side_count(kind, m, "dve", "normed"))
                    if kind == "fox":
                        side_waits(pool=side_count("decay", 0, "pool", "columns"))
                    for qt in range(2):
                        qs = slice(qt * P, qt * P + P)
                        if kind == "fox":
                            keys = slice(0, qt * P + P)
                            for h in range(2):
                                dst = psM[:, 2 + h, 0:P] if qt == 0 else psM[:, 2 + h, P:CW]
                                mm(dst, A["q_n"][:, h, qs], A["k_n"][:, h, keys], start=True, stop=False)
                                ins = mm(dst, lhs_c[:, qs], rhs_c[:, bass.ds(m * 2 + h, 1), keys].rearrange("p a t -> p (a t)"),
                                         start=False, stop=True)
                        else:
                            for t in range(2):
                                ins = mm(psM[:, 2, qt * T:(qt + 1) * T], A["q_n"][:, t, qs], A["k_n"][:, t],
                                         start=t == 0, stop=t == 1)
                    done(ins)

                def transposes():
                    side_waits(dve=side_count(kind, m, "dve", "weights1" if kind == "fox" else "weights0"))
                    if kind == "mem":
                        pe.wait_ge(const_in, 48)
                    for h in range(2 if kind == "fox" else 1):
                        for kt in range(2):
                            for qt in range(2):
                                if kind == "mem":
                                    o = kt * T + qt * P
                                    ins = nc.tensor.transpose(psM[:, h, o:o + P], A["S"][:, h, qt, kt * P:kt * P + P], ident[:])
                                elif qt >= kt:
                                    ins = nc.tensor.transpose(psM[:, h, (qt + kt) * P:(qt + kt + 1) * P],
                                                              causal(A["S"])[:, h, (qt + kt) * P:(qt + kt + 1) * P], ident[:])
                    done(ins)

                def values():
                    side_waits(act=side_count(kind, m, "act", "weights_copied"),
                               pool=side_count(kind, m, "pool", "values_staged"))
                    for t in range(2):
                        for kt in range(2):
                            if kind == "mem":
                                dst, wts = psM[:, 2, t * T:(t + 1) * T], A["PT"][:, 0, kt]
                            elif kt == 0:
                                dst, wts = psM[:, 2, t * T:(t + 1) * T], causal(A["PT"])[:, t, 0:T]
                            else:
                                dst, wts = psM[:, 2, t * T + P:(t + 1) * T], causal(A["PT"])[:, t, T:CW]
                            ins = mm(dst, A["v_cur"][:, kt, t * P:t * P + P], wts, start=kt == 0, stop=kt == 1)
                    done(ins)

                return {0 if kind == "fox" else 1: sums, 4: scores, 6: transposes, 7: values}

            def lru_hooks(m):
                def gates_():
                    pe.wait_ge(rg_in, at(32, m, 32))
                    pe.wait_ge(lru_taps, at(3, m, 3))
                    side_waits(act=side_count("lru", m - 1, "act", "gate_tanh"))
                    for j in range(2):
                        for b in range(2):
                            ins = mm(psM[:, j, b * T:(b + 1) * T], lru["rg"][:, j, b], lru["xr"][:, b], start=True, stop=True)
                    done(ins)
                return {1: gates_}

            def decay_hooks():
                def logits():
                    side_waits(dve=side_count("decay", 0, "dve", None), act=side_count("decay", 0, "act", None))
                    pe.wait_ge(ff_lo, 1)
                    for kt in range(KT):
                        mm(psM[0:HR, 0, :], ff_w[:, kt, 0], X[:, kt], start=kt == 0, stop=False)
                        ins = mm(psM[0:HR, 0, T:], ff_w[:, kt, 1], X[:, kt, 0], start=False, stop=kt == KT - 1)
                    done(ins)
                return {1: logits}

            x_op = lambda kt: X[:, kt]
            m_op = lambda kt: XM[:, kt]

            def channel_sums():
                pe.wait_ge(sq_done, 2)
                mm(psM[:, 0, :], ones[:], sum1.rearrange("p j t -> p (j t)"), start=True, stop=True)
                for t in range(2):
                    ins = mm(psM[:, 1, t:t + 1], sum1[:, 0, t * P:t * P + P], ones[:, 0:1], start=True, stop=True)
                ins.then_inc(ss_done, 1)

            group("mv", None, 0, m_op, {}, rows_major=True, tile_ready=lambda kt: pe.wait_ge(memX_lo, kt + 1))
            group("mv", None, 1, m_op, {}, rows_major=True)
            with pe.Fori(1, 2) as i:
                for w in range(2):
                    group("mv", i, w, m_op, {4: channel_sums}, rows_major=True)

            def mkq(i, hooks):
                group("mkq", i, 0, m_op, hooks)
                group("mkq", i, 1, x_op, hooks, ready=lambda n: pe.wait_ge(xX_lo, n + 1))

            def plain(phase, i, hooks, operand=x_op, **kw):
                for w in range(2):
                    group(phase, i, w, operand, hooks, **kw)

            mkq(None, {})
            with pe.Fori(1, 4) as i:
                mkq(i, attention_hooks("mem", i - 1))
            plain("lru", None, attention_hooks("mem", 3))
            with pe.Fori(1, 4) as i:
                plain("lru", i, lru_hooks(i - 1))
            plain("v", None, lru_hooks(3), rows_major=True)
            with pe.Fori(1, 2) as i:
                plain("v", i, decay_hooks(), rows_major=True)
            plain("qk", None, {})
            with pe.Fori(1, 4) as i:
                plain("qk", i, attention_hooks("fox", i - 1))
            plain("gate0", None, attention_hooks("fox", 3))

            def quarter(q, first_gate):
                before = (q * QUARTER_UNITS, q * QUARTER_GROUPS)
                with pe.Fori(first_gate, 3) as i:
                    plain("gate0", i, {}, before=before)
                if first_gate:
                    pe.wait_ge(side["dve"], SIDE_ALL["dve"])
                with pe.Fori(0, 3) as n:
                    for w in range(2):
                        group("branch0", n, w,
                              lambda kt: Y[:, bass.ds(n, 1), kt].rearrange("p a h t -> p (a h) t"),
                              {}, per=2, coef=4, before=before)

            quarter(0, 1)
            with pe.Fori(1, 4) as q:
                quarter(q, 0)
            with pe.Fori(0, 4) as i:
                plain("out", i, {}, operand=lambda kt: merged[:, kt], ready=lambda n: pe.wait_ge(merged_lo, 2 * n + 2))

            def x2_sums():
                pe.wait_ge(x2_sum, 8)
                for t in range(2):
                    ins = mm(psM[:, 0, 0:T], ones[:], sum2[:, t], start=t == 0, stop=t == 1)
                ins.then_inc(x2_ss, 1)

            plain("up", None, {3: x2_sums}, ready=lambda n: pe.wait_ge(h2_lo, 2 * n + 2))
            with pe.Fori(1, FT // 2) as i:
                plain("up", i, {})

            with pe.Fori(0, 2) as i:
                for w in range(4):
                    group("down", i, w, lambda kt: hidden[:, kt], {}, per=FT // UK, coef=4 * (FT // UK),
                          ready=lambda n: pe.wait_ge(hidden_lo, 2 * n + 2))

        evac_at = {last + 4: (g, ph, i, w) for g, (ph, i, w, last) in enumerate(GROUPS) if last + 4 <= U0["gate0"] + 3}
        def build_hooks(table):
            where = {}
            starts = {"mem": [U0["mkq"] + 8 * (m + 1) for m in range(4)],
                      "lru": [U0["lru"] + 8 * (m + 1) for m in range(4)],
                      "decay": [U0["v"] + 8],
                      "fox": [U0["qk"] + 8 * (m + 1) for m in range(4)]}
            for kind, offs in table.items():
                for m, s in enumerate(starts[kind]):
                    for o, steps in offs.items():
                        for f in steps:
                            where.setdefault(s + o, []).append((f, kind, m))
            return where

        @block.scalar
        def _(act):
            def split(u, i=None, coef=8):
                s = u % SLOTS
                act.wait_ge(raw_full[s], at(16 * (u // SLOTS + 1), i, 16 * coef // SLOTS))
                if u >= SLOTS:
                    act.wait_ge(pe_units, at(u - 3, i, coef))
                nc.scalar.activation(W[:, s, :, 0], raw[:, s], ACT.Copy).then_inc(hi_done, 1)

            def copy_low(g, last, i=None, coef=8, groups=2):
                act.wait_ge(pe_units, at(last + 1, i, coef))
                if g >= 2:
                    act.wait_ge(evac_done, at(g - 1, i, groups))
                b = 2 * (g % 2)
                nc.scalar.activation(low[:, g % 2], psG[:, b:b + 2, T:], ACT.Copy).then_inc(low_copied, 1)

            def wait(**need):
                for e, v in need.items():
                    if not is_zero(v):
                        act.wait_ge(side[e], v)

            def done(ins):
                ins.then_inc(side["act"], 1)

            def squares(kind, m):
                A = att[kind]
                own = G0["mkq" if kind == "mem" else "qk"] + 1
                act.wait_ge(evac_done, at(own + 1, m, 2))
                wait(pe=side_count(kind, m, "pe", None), act=side_count(kind, m, "act", None))
                if is_zero(m):
                    wait(dve=side_count(kind, m, "dve", None))
                if kind == "mem":
                    wait(pool=side_count(kind, m, "pool", "k_scaled"))
                nc.scalar.activation(A["S"][:, 0], A["k_raw"][:], ACT.Square)
                done(nc.scalar.activation(A["S"][:, 1], A["q_raw"][:], ACT.Square))

            def root(kind, m):
                A = att[kind]
                wait(pe=side_count(kind, m, "pe", "sums"))
                if kind == "mem":
                    src, dst, bias = psM[:, 0, :], A["rstd"][:, 0].rearrange("p a t -> p (a t)"), eps[:, 1:2]
                else:
                    src, dst, bias = psM[:, 0:2, :], A["rstd"].rearrange("p j a t -> p j (a t)"), eps[:, 2:3]
                done(nc.scalar.activation(dst, src, ACT.Sqrt, bias=bias))

            def exp(kind, m):
                A = att[kind]
                for h in range(2 if kind == "fox" else 1):
                    wait(dve=side_count(kind, m, "dve", f"row_max{h}"))
                    for qt in range(2):
                        if kind == "fox":
                            src = dst = causal(A["S"])[:, h, slice(0, P) if qt == 0 else slice(P, CW)]
                        else:
                            src, dst = psM[:, 2, qt * T:(qt + 1) * T], A["S"][:, 0, qt]
                        n = 2 * h + qt
                        ins = nc.scalar.activation(dst, src, ACT.Exp, bias=stat[:, 0, n:n + 1], scale=1.0,
                                                   accum_out=stat[:, 1, n:n + 1])
                    done(ins)

            def weights_copied(kind, m):
                A = att[kind]
                wait(pe=side_count(kind, m, "pe", "transposes"))
                if kind == "fox":
                    done(nc.scalar.activation(causal(A["PT"]), psM[:, 0:2, 0:CW], ACT.Copy))
                else:
                    done(nc.scalar.activation(A["PT"][:, 0].rearrange("p k t -> p (k t)"), psM[:, 0, :], ACT.Copy))

            def attention_hi(kind, m):
                wait(pe=side_count(kind, m, "pe", "values"))
                br = 0 if kind == "fox" else 2
                done(nc.scalar.activation(Y[:, br, bass.ds(m * 2, 2), 0, :], psM[:, 2, :].rearrange("p (a t) -> p a t", a=2),
                                          ACT.Copy))

            L = lru

            def conv0_(kind, m):
                act.wait_ge(evac_done, at(G0["lru"] + 1, m, 2))
                if not is_zero(m):
                    wait(pe=side_count("lru", m - 1, "pe", "gates"), dve=side_count("lru", m - 1, "dve", "ix"))
                for b in range(2):
                    ins = nc.scalar.activation(L["xr"][:, b], lx_pad[:, b, 3:], ACT.Identity,
                                               bias=p1("b_lconv", m * 2 + b), scale=p1("w_lconv", m * 2 + (3 * BT + b)))
                ins.then_inc(lru_conv0, 1)

            def gelu_square(kind, m):
                wait(**{e: side_count("lru", m, e, None) for e in ("pe", "dve", "act", "pool")})
                act.wait_ge(evac_done, at(G0["lru"] + 2, m, 2))
                done(nc.scalar.activation(L["gg"][:], L["lg"][:], ACT.Square))

            def gate_tanh(kind, m):
                wait(pe=side_count("lru", m, "pe", "gates"))
                for j, (n, hb) in enumerate([("ra", half_ba), ("ix", half_bx)]):
                    for b in range(2):
                        ins = nc.scalar.activation(L[n][:, b], psM[:, j, b * T:(b + 1) * T], ACT.Tanh, scale=0.5,
                                                   bias=hb[:, bass.ds(m * 2 + b, 1)])
                done(ins)

            def exps(kind, m):
                wait(dve=side_count("lru", m, "dve", "log_a"))
                nc.scalar.activation(L["a"][:], L["ra"][:], ACT.Exp)
                done(nc.scalar.activation(L["tn"][:], L["ra"][:], ACT.Tanh, scale=-1.0))

            def gelu_tanh(kind, m):
                wait(pool=side_count("lru", m, "pool", "gelu_cube"))
                done(nc.scalar.activation(L["gg"][:], L["gg"][:], ACT.Tanh, scale=GELU_S))

            def lru_root(kind, m):
                wait(dve=side_count("lru", m, "dve", "decay_sq"))
                done(nc.scalar.activation(L["aa"][:], L["aa"][:], ACT.Sqrt, scale=0.25, bias=eps[:, 3:4]))

            def lru_hi(kind, m):
                wait(dve=side_count("lru", m, "dve", "y"))
                done(nc.scalar.activation(Y[:, 1, bass.ds(m * 2, 2), 0, :], L["hs"][:], ACT.Copy))

            def decay_exp(kind, m):
                wait(dve=side_count("decay", 0, "dve", "abs"))
                done(nc.scalar.activation(dec["e"][:], dec["r"][:], ACT.Exp, scale=-1.0))

            def decay_ln(kind, m):
                wait(dve=side_count("decay", 0, "dve", "one_plus"))
                done(nc.scalar.activation(dec_l[:], dec["u"][:], ACT.Ln))

            softmax = {8: [exp], 10: [weights_copied], 11: [attention_hi]}
            steps_at = {"mem": {3: [squares], 5: [root], **softmax}, "fox": {3: [squares], 4: [root], **softmax},
                        "lru": {0: [conv0_], 3: [gelu_square], 5: [gate_tanh], 7: [exps, gelu_tanh], 9: [lru_root], 10: [lru_hi]},
                        "decay": {6: [decay_exp], 8: [decay_ln]}}
            hooks = build_hooks(steps_at)

            def root_mean_square(dst, src):
                return nc.scalar.activation(dst, src, ACT.Sqrt, bias=eps[:, 0:1], scale=1.0 / D)

            def gained_hi(dst, src, gain, tiles):
                for k in tiles:
                    ins = nc.scalar.activation(dst[:, k, 0, :], src[:, k], ACT.Copy, scale=p1(gain, k))
                return ins

            act.wait_ge(ones_set, 1)
            nc.scalar.activation(stat[:, 0, 0:1], ones[:, 0:1], ACT.Copy).then_inc(act_warm, 1)
            act.wait_ge(par_in, 16)
            for c in range(4):
                split(c)
                act.wait_ge(mem_in[c], 16)
                for k in range(4 * c, 4 * c + 4):
                    gained_hi(XM, mem_raw, "g_mem", (k,)).then_inc(memX_hi, 1)

            def start_steps(u):
                if u == 10:
                    act.wait_ge(ff_in, 16)
                    for c in (0, 32):
                        ins = nc.scalar.activation(ff_w[:, :, 0, c:c + 8], ff_raw[:], ACT.Copy)
                    ins.then_inc(ff_hi, 1)
                if u == 11:
                    act.wait_ge(lam_dve, 1)
                    nc.scalar.activation(lam_t["e"][:], lam_t["t"][:], ACT.Exp, scale=-1.0).then_inc(lam_act, 1)
                if u == 12:
                    act.wait_ge(lam_dve, 2)
                    nc.scalar.activation(lam_t["l"][:], lam_t["u"][:], ACT.Ln).then_inc(lam_act, 1)
                if u == 16:
                    act.wait_ge(ss_done, 1)
                    root_mean_square(rstd0.rearrange("p j t -> p (j t)"), psM[:, 0, :])
                    root_mean_square(rstd_tok[:], psM[:, 1, 0:2]).then_inc(root_done, 1)
                if 18 <= u < 22:
                    c = u - 18
                    act.wait_ge(x_scaled, c + 1)
                    gained_hi(X, x_n, "g_mix", range(4 * c, 4 * c + 4)).then_inc(xX_hi, 1)

            def run_units(first, last):
                for u in range(first, last):
                    if u in evac_at:
                        g, ph, i, w = evac_at[u]
                        copy_low(g, u - 4)
                    split(u)
                    start_steps(u)
                    for f, kind, m in hooks.get(u, []):
                        f(kind, m)

            def iteration(phase, kind, i):
                for k in range(4, 12):
                    if k in (7, 11):
                        copy_low(G0[phase] + k // 11, U0[phase] + k - 4, i)
                    split(U0[phase] + k, i)
                    for offset, m in ((k, i - 1), (k - 8, i)):
                        for f in steps_at[kind].get(offset, []):
                            f(kind, m)

            run_units(4, U0["mkq"] + 12)
            with act.Fori(1, 4) as i:
                iteration("mkq", "mem", i)
            run_units(U0["lru"] + 4, U0["lru"] + 12)
            with act.Fori(1, 4) as i:
                iteration("lru", "lru", i)
            run_units(U0["v"] + 4, U0["qk"] + 12)
            with act.Fori(1, 4) as i:
                iteration("qk", "fox", i)

            def quarter(q, first=False):
                for k in range(4, QUARTER_UNITS + 4):
                    group = quarter_groups.get(k)
                    if group:
                        kind, i, w, n = group
                        copy_low(G0["gate0"] + n, QUARTER0 + k - 4, q, coef=QUARTER_UNITS, groups=QUARTER_GROUPS)
                    split(QUARTER0 + k, q, coef=QUARTER_UNITS)
                    if first:
                        for f, side_kind, m in hooks.get(QUARTER0 + k, []):
                            f(side_kind, m)
                    if group and kind == "gate":
                        act.wait_ge(evac_done, at(G0["gate0"] + n + 1, q, QUARTER_GROUPS))
                        for t in range(2):
                            ins = nc.scalar.activation(gates[:, i, w, t], gates[:, i, w, t], ACT.Tanh, scale=0.5,
                                                       bias=half_bg[:, bass.ds(q * 4 + (i * KT + 2 * w + t), 1)])
                        ins.then_inc(gate_ready, 1)
                    if group and kind == "branch" and i == 2:
                        act.wait_ge(acc_added, q * 4 + (3 + w))
                        nc.scalar.activation(merged[:, bass.ds(q * 4 + 2 * w, 2), 0, :], acc[:, w], ACT.Copy, scale=0.5
                                             ).then_inc(merged_hi, 1)

            quarter(0, first=True)
            with act.Fori(1, 4) as q:
                quarter(q)

            def out_iteration(i, first=False):
                for k in range(4, 12):
                    w = {7: 0, 11: 1}.get(k)
                    if w is not None:
                        copy_low(G0["out"] + w, U0["out"] + k - 4, i)
                    split(U0["out"] + k, i)
                    if w is not None:
                        act.wait_ge(x2_done, i * 2 + (w + 1))
                        if not first:
                            act.wait_ge(x2_sum, i * 2 + (w - 1))
                        nc.scalar.activation(sq2[:, w], xs[:, bass.ds(i * 4 + 2 * w, 2)], ACT.Square).then_inc(x2_sq, 1)
                        for t in range(2):
                            row = i * 4 + (2 * w + t)
                            ins = nc.scalar.activation(X[:, bass.ds(row, 1), 0, :], xs[:, bass.ds(row, 1)], ACT.Copy, scale=p1("g_ffn", row))
                        ins.then_inc(h2_hi, 1)

            out_iteration(0, first=True)
            with act.Fori(1, 4) as i:
                out_iteration(i)

            def up_conv0(i, w):
                act.wait_ge(up_scaled, i * 2 + (w + 1))
                for t in range(2):
                    ins = nc.scalar.activation(up_c[w][:, t], up_pad[w][:, t, 2:], ACT.Identity,
                                               bias=p1("b_fconv", i * 2 + (w * FT + t)),
                                               scale=p1("w_fconv", i * 2 + (2 * 2 * FT + w * FT + t)))
                ins.then_inc(conv0, 1)

            def up_iteration(i, split_next, first=False):
                U = U0["up"]
                for k in range(4, 7):
                    split(U + k, i)
                copy_low(G0["up"], U + 3, i)
                split(U + 7, i)
                if first:
                    act.wait_ge(x2_ss, 1)
                    root_mean_square(rstd2[:], psM[:, 0, 0:T]).then_inc(root_done, 1)
                up_conv0(i, 0)
                split_next(0)
                act.wait_ge(tap0, i * 2 + 1)
                nc.scalar.activation(up_c[0][:], up_c[0][:], ACT.Gelu_apprx_tanh).then_inc(gelu_done, 1)
                split_next(1)
                split_next(2)
                copy_low(G0["up"] + 1, U + 7, i)
                split_next(3)
                up_conv0(i, 1)
                act.wait_ge(prod_done, i + 1)
                nc.scalar.activation(hidden[:, bass.ds(i * 2, 2), 0, :], up_c[1][:], ACT.Copy).then_inc(hidden_hi, 1)

            up_iteration(0, lambda k: split(U0["up"] + 8 + k), first=True)
            with act.Fori(1, FT // 2 - 1) as i:
                up_iteration(i, lambda k: split(U0["up"] + 8 + k, i))
            with act.Fori(FT // 2 - 1, FT // 2) as i:
                up_iteration(i, lambda k: split(U0["down"] + k))

            def down_iteration(i, more):
                per = FT // UK
                for k in range(4, 4 * per + 4):
                    w = (k - 4) // per
                    if (k - 4) % per == per - 1:
                        copy_low(G0["down"] + w, U0["down"] + k - 4, i, coef=4 * per, groups=4)
                    if k < 4 * per or more:
                        split(U0["down"] + k, i, coef=4 * per)

            with act.Fori(0, 1) as i:
                down_iteration(i, True)
            with act.Fori(1, 2) as i:
                down_iteration(i, False)

        @block.vector
        def _(dve):
            V = nc.vector

            def split(u, i=None, coef=8):
                s = u % SLOTS
                dve.wait_ge(hi_done, at(u + 1, i, coef))
                V.tensor_tensor(W[:, s, :, 1], raw[:, s], f32(W[:, s, :, 0]), ALU.subtract).then_inc(lo_done, 1)

            def add_low(g, dst, i=None, groups=2):
                dve.wait_ge(low_copied, at(g + 1, i, groups))
                b = 2 * (g % 2)
                V.tensor_tensor(dst, psG[:, b:b + 2, 0:T], low[:, g % 2], ALU.add).then_inc(evac_done, 1)

            def wait(**need):
                for e, v in need.items():
                    if not is_zero(v):
                        dve.wait_ge(side[e], v)

            def done(ins):
                ins.then_inc(side["dve"], 1)

            def chained(kind, m, step):
                dve.wait_ge(side["dve"], side_count(kind, m, "dve", step))

            def inverse_root(kind, m, j):
                A = att[kind]
                rstd = A["rstd"][:, 0, j] if kind == "mem" else A["rstd"][:, j].rearrange("p a t -> p (a t)")
                done(V.reciprocal(rstd, rstd))

            def norm_k(kind, m):
                wait(act=side_count(kind, m, "act", "root"))
                inverse_root(kind, m, 0)

            def normed(kind, m):
                A = att[kind]
                inverse_root(kind, m, 1)
                chained(kind, m, "norm_q")
                if kind == "mem":
                    for t in range(2):
                        V.scalar_tensor_tensor(A["k_n"][:, t], A["k_raw"][:, t], gkm_s[:, t:t + 1], A["rstd"][:, 0, 0], ALU.mult, ALU.mult)
                        ins = V.scalar_tensor_tensor(A["q_n"][:, t], A["q_raw"][:, t], p1("g_qm", t), A["rstd"][:, 0, 1], ALU.mult, ALU.mult)
                else:
                    V.scalar_tensor_tensor(A["k_n"][:], A["k_raw"][:], gk_s[:, 0:1], A["rstd"][:, 0], ALU.mult, ALU.mult)
                    ins = V.scalar_tensor_tensor(A["q_n"][:], A["q_raw"][:], p1("g_q", 0), A["rstd"][:, 1], ALU.mult, ALU.mult)
                done(ins)

            def row_max(kind, m):
                A = att[kind]
                wait(pe=side_count(kind, m, "pe", "scores"))
                if kind == "mem":
                    done(V.tensor_reduce(stat[:, 0, 0:2], psM[:, 2, :].rearrange("p (a t) -> p a t", a=2), AX_X, ALU.max, negate=True))
                    return
                for h in range(2):
                    S = causal(A["S"])[:, h]
                    done(V.tensor_tensor(S, psM[:, 2 + h, 0:CW], mask[:], ALU.add))
                    chained(kind, m, f"masked{h}")
                    V.tensor_reduce(stat[:, 0, 2 * h:2 * h + 1], S[:, 0:P], AX_X, ALU.max, negate=True)
                    done(V.tensor_reduce(stat[:, 0, 2 * h + 1:2 * h + 2], S[:, P:CW], AX_X, ALU.max, negate=True))

            def weights(kind, m):
                A = att[kind]
                for h in range(2 if kind == "fox" else 1):
                    wait(act=side_count(kind, m, "act", f"exp{h}"))
                    done(V.reciprocal(stat[:, 2, 2 * h:2 * h + 2], stat[:, 1, 2 * h:2 * h + 2]))
                    chained(kind, m, f"row_inv{h}")
                    for qt in range(2):
                        n = 2 * h + qt
                        S = A["S"][:, h, qt] if kind == "mem" else causal(A["S"])[:, h, slice(0, P) if qt == 0 else slice(P, CW)]
                        ins = V.tensor_scalar(S, S, stat[:, 2, n:n + 1], None, ALU.mult)
                    done(ins)

            def attention_lo(kind, m):
                wait(act=side_count(kind, m, "act", "y_hi"))
                br = 0 if kind == "fox" else 2
                ys = Y[:, br, bass.ds(m * 2, 2)]
                done(V.tensor_tensor(ys[:, :, 1, :], psM[:, 2, :].rearrange("p (a t) -> p a t", a=2), f32(ys[:, :, 0, :]), ALU.subtract))

            L = lru

            def taps(kind, m):
                for n in (2, 1, 0):
                    if n == 2:
                        dve.wait_ge(lru_conv0, m + 1)
                    else:
                        dve.wait_ge(lru_taps, m * 3 + (2 - n))
                    for b in range(2):
                        ins = V.scalar_tensor_tensor(L["xr"][:, b], lx_pad[:, b, n:n + T], p1("w_lconv", m * 2 + (n * BT + b)),
                                                     L["xr"][:, b], ALU.mult, ALU.add)
                    ins.then_inc(lru_taps, 1)

            def log_a(kind, m):
                wait(act=side_count("lru", m, "act", "gate_tanh"))
                for b in range(2):
                    ins = V.tensor_scalar(L["ra"][:, b], L["ra"][:, b], 1.0, ls4[:, bass.ds(m * 2 + b, 1)], ALU.add, ALU.mult)
                done(ins)
                done(V.scalar_tensor_tensor(L["ix"][:], L["ix"][:], 1.0, L["xr"][:], ALU.add, ALU.mult))

            def decay_sq(kind, m):
                wait(pool=side_count("lru", m, "pool", "a_sq"), act=side_count("lru", m, "act", "exps"))
                done(V.scalar_tensor_tensor(L["aa"][:], L["aa"][:], 1.0, L["tn"][:], ALU.add, ALU.mult))

            def recurrence(kind, m):
                wait(act=side_count("lru", m, "act", "root"))
                done(V.tensor_tensor(L["ix"][:], L["ix"][:], L["aa"][:], ALU.mult))
                chained("lru", m, "u")
                for b in range(2):
                    ins = V.tensor_tensor_scan(out=L["hs"][:, b], data0=L["a"][:, b], data1=L["ix"][:, b], initial=0.0,
                                               op0=ALU.mult, op1=ALU.add)
                done(ins)

            def gated_y(kind, m):
                wait(act=side_count("lru", m, "act", "gelu_tanh"))
                done(V.scalar_tensor_tensor(L["gg"][:], L["gg"][:], 1.0, L["lg"][:], ALU.add, ALU.mult))
                chained("lru", m, "gelu")
                done(V.scalar_tensor_tensor(L["hs"][:], L["hs"][:], 0.5, L["gg"][:], ALU.mult, ALU.mult))

            def lru_lo(kind, m):
                wait(act=side_count("lru", m, "act", "y_hi"))
                ys = Y[:, 1, bass.ds(m * 2, 2)]
                done(V.tensor_tensor(ys[:, :, 1, :], L["hs"][:], f32(ys[:, :, 0, :]), ALU.subtract))

            def decay_z(kind, m):
                wait(pe=side_count("decay", 0, "pe", "logits"))
                done(V.tensor_copy(dec["e"][:], psM[0:HR, 0, T:]))
                chained("decay", 0, "low")
                done(V.scalar_tensor_tensor(dec["z"][:], psM[0:HR, 0, 0:T], p1("b_f", 0)[0:HR], dec["e"][:], ALU.add, ALU.add))
                chained("decay", 0, "z")
                done(V.scalar_tensor_tensor(dec["r"][:], dec["z"][:], -1.0, dec["z"][:], ALU.mult, ALU.max))

            def decay_one_plus(kind, m):
                wait(act=side_count("decay", 0, "act", "exp"))
                done(V.tensor_scalar(dec["u"][:], dec["e"][:], 1.0, None, ALU.add))

            def decay_inverse(kind, m):
                chained("decay", 0, "one_plus")
                done(V.tensor_scalar(dec["r"][:], dec["u"][:], 1.0, None, ALU.is_equal))
                chained("decay", 0, "is_one")
                wait(act=side_count("decay", 0, "act", "ln"))
                done(V.scalar_tensor_tensor(dec["u"][:], dec["u"][:], -1.0, dec["r"][:], ALU.add, ALU.add))
                chained("decay", 0, "minus_one")
                done(V.reciprocal(dec["u"][:], dec["u"][:]))

            def decay_c(kind, m):
                chained("decay", 0, "inverse")
                done(V.tensor_tensor(dec["u"][:], dec["u"][:], dec_l[:], ALU.mult))
                chained("decay", 0, "ratio")
                done(V.tensor_tensor(dec["u"][:], dec["u"][:], dec["r"][:], ALU.add))
                chained("decay", 0, "ratio1")
                done(V.tensor_tensor(dec["e"][:], dec["u"][:], dec["e"][:], ALU.mult))
                chained("decay", 0, "log1p")
                done(V.scalar_tensor_tensor(dec["z"][:], dec["z"][:], 0.0, dec["e"][:], ALU.min, ALU.subtract))
                chained("decay", 0, "log_f")
                V.memset(dec["r"][:], 1.0).then_inc(setup, 1)
                dve.wait_ge(setup, 2)
                done(V.tensor_tensor_scan(out=dec["u"][:], data0=dec["r"][:], data1=dec["z"][:], initial=0.0,
                                          op0=ALU.mult, op1=ALU.add))

            steps_at = {"mem": {5: [norm_k, normed], 8: [row_max, weights], 11: [attention_lo]},
                        "fox": {4: [norm_k, normed], 7: [row_max, weights], 11: [attention_lo]},
                        "lru": {1: [taps], 6: [log_a], 8: [decay_sq], 9: [recurrence, gated_y], 10: [lru_lo]},
                        "decay": {5: [decay_z], 7: [decay_one_plus], 8: [decay_inverse], 9: [decay_c]}}
            hooks = build_hooks(steps_at)

            def gained_lo(dst, src, gain, tiles):
                for k in tiles:
                    ins = V.scalar_tensor_tensor(dst[:, k, 1, :], src[:, k], p1(gain, k), f32(dst[:, k, 0, :]), ALU.mult, ALU.subtract)
                return ins

            V.memset(ones[:], 1.0).then_inc(ones_set, 1)
            V.memset(f32(ff_w[:, :, :, 8:32]), 0.0)
            for j, e in enumerate((EPS, 256 * EPS, 128 * EPS, 1e-33)):
                V.memset(eps[:, j:j + 1], e)
            for c in range(4):
                split(c)
                for k in range(4 * c, 4 * c + 4):
                    dve.wait_ge(memX_hi, k + 1)
                    gained_lo(XM, mem_raw, "g_mem", (k,)).then_inc(memX_lo, 1)

            def start_steps(u):
                lt = lam_t
                if u == 4:
                    V.tensor_scalar(gk_s[:], p1("g_k", 0), float(np.sqrt(128)), None, ALU.mult)
                    V.tensor_scalar(gkm_s[:], p1("g_km", 0, 2), 16.0, None, ALU.mult)
                    V.tensor_scalar(half_bg[:], p1("b_gate", 0, 3 * KT), 0.5, None, ALU.mult)
                    V.tensor_scalar(half_ba[:], p1("b_a", 0, BT), 0.5, None, ALU.mult)
                    V.tensor_scalar(half_bx[:], p1("b_x", 0, BT), 0.5, None, ALU.mult).then_inc(setup, 1)
                    V.scalar_tensor_tensor(lt["t"][:], p1("lam", 0, BT), -1.0, p1("lam", 0, BT), ALU.mult, ALU.max).then_inc(lam_dve, 1)
                if u == 5:
                    dve.wait_ge(setup, 1)
                if u == 10:
                    dve.wait_ge(ff_hi, 1)
                    for c in (0, 32):
                        ins = V.tensor_tensor(ff_w[:, :, 1, c:c + 8], ff_raw[:], f32(ff_w[:, :, 0, c:c + 8]), ALU.subtract)
                    ins.then_inc(ff_lo, 1)
                if u == 11:
                    dve.wait_ge(lam_act, 1)
                    V.tensor_scalar(lt["u"][:], lt["e"][:], 1.0, None, ALU.add).then_inc(lam_dve, 1)
                    dve.wait_ge(lam_dve, 2)
                    V.tensor_scalar(lt["m"][:], lt["u"][:], 1.0, None, ALU.is_equal).then_inc(lam_dve, 1)
                    dve.wait_ge(lam_dve, 3)
                    V.scalar_tensor_tensor(lt["d"][:], lt["u"][:], -1.0, lt["m"][:], ALU.add, ALU.add).then_inc(lam_dve, 1)
                    dve.wait_ge(lam_dve, 4)
                    V.reciprocal(lt["d"][:], lt["d"][:]).then_inc(lam_dve, 1)
                if u == 13:
                    dve.wait_ge(lam_act, 2)
                    dve.wait_ge(lam_dve, 5)
                    V.tensor_tensor(lt["d"][:], lt["d"][:], lt["l"][:], ALU.mult).then_inc(lam_dve, 1)
                    dve.wait_ge(lam_dve, 6)
                    V.tensor_tensor(lt["d"][:], lt["d"][:], lt["m"][:], ALU.add).then_inc(lam_dve, 1)
                    dve.wait_ge(lam_dve, 7)
                    V.tensor_tensor(lt["e"][:], lt["d"][:], lt["e"][:], ALU.mult).then_inc(lam_dve, 1)
                    dve.wait_ge(lam_dve, 8)
                    V.scalar_tensor_tensor(lt["d"][:], p1("lam", 0, BT), 0.0, lt["e"][:], ALU.min, ALU.subtract).then_inc(lam_dve, 1)
                    dve.wait_ge(lam_dve, 9)
                    V.tensor_scalar(ls4[:], lt["d"][:], 4.0, None, ALU.mult).then_inc(side["dve"], 1)
                if u == 16:
                    dve.wait_ge(root_done, 1)
                    V.reciprocal(rstd0[:], rstd0[:])
                    V.reciprocal(rstd_tok[:], rstd_tok[:]).then_inc(rstd_done, 1)
                if 18 <= u < 22:
                    c = u - 18
                    dve.wait_ge(xX_hi, c + 1)
                    gained_lo(X, x_n, "g_mix", range(4 * c, 4 * c + 4)).then_inc(xX_lo, 1)

            def destination(ph, i, w):
                if ph in ("mv", "v"):
                    c = (2 * i + w) * UC
                    return (mem_v if ph == "mv" else v_all)[:, :, c:c + UC]
                if ph in ("mkq", "qk"):
                    A = att["mem" if ph == "mkq" else "fox"]
                    return A["k_raw" if (w == 0) == (ph == "mkq") else "q_raw"][:]
                return lx_pad[:, :, 3:] if w == 0 else lru["lg"][:]

            def run_units(first, last):
                for u in range(first, last):
                    if u in evac_at:
                        g, ph, i, w = evac_at[u]
                        if ph == "lru" and i == 0 and w == 0:
                            dve.wait_ge(side["pool"], side_count("mem", 3, "pool", "values_staged"))
                            V.memset(lx_pad[:, :, 0:3], 0.0)
                        add_low(g, destination(ph, i, w))
                    split(u)
                    start_steps(u)
                    for f, kind, m in hooks.get(u, []):
                        f(kind, m)

            def iteration(phase, kind, i):
                for k in range(4, 12):
                    if k == 7:
                        if kind == "lru":
                            dve.wait_ge(lru_taps, i * 3)
                        else:
                            chained(kind, i - 1, "normed")
                    if k in (7, 11):
                        add_low(G0[phase] + k // 11, destination(phase, 0, k // 11), i)
                    split(U0[phase] + k, i)
                    for offset, m in ((k, i - 1), (k - 8, i)):
                        for f in steps_at[kind].get(offset, []):
                            f(kind, m)

            run_units(4, U0["mkq"] + 12)
            with dve.Fori(1, 4) as i:
                iteration("mkq", "mem", i)
            run_units(U0["lru"] + 4, U0["lru"] + 12)
            with dve.Fori(1, 4) as i:
                iteration("lru", "lru", i)
            run_units(U0["v"] + 4, U0["qk"] + 12)
            with dve.Fori(1, 4) as i:
                iteration("qk", "fox", i)

            def quarter(q, first=False):
                for k in range(4, QUARTER_UNITS + 4):
                    group = quarter_groups.get(k)
                    if group:
                        kind, i, w, n = group
                        if first and n == 2:
                            dve.wait_ge(side["pe"], side_count("fox", 3, "pe", "scores"))
                        if kind == "gate":
                            if not first and i == 0:
                                dve.wait_ge(acc_added, q * 4)
                            add_low(G0["gate0"] + n, gates[:, i, w], q, groups=QUARTER_GROUPS)
                        else:
                            gated_before = 2 * i + w
                            if not first or gated_before > 0:
                                dve.wait_ge(gated, q * 6 + gated_before)
                            add_low(G0["gate0"] + n, yd[:], q, groups=QUARTER_GROUPS)
                            dve.wait_ge(evac_done, at(G0["gate0"] + n + 1, q, QUARTER_GROUPS))
                            dve.wait_ge(gate_ready, q * 6 + (2 * i + w + 1))
                            dst = acc[:, w] if i == 0 else gates[:, i, w]
                            V.scalar_tensor_tensor(dst, gates[:, i, w], 1.0, yd[:], ALU.add, ALU.mult).then_inc(gated, 1)
                            if i > 0:
                                dve.wait_ge(gated, q * 6 + (gated_before + 1))
                                if i == 2:
                                    dve.wait_ge(acc_added, q * 4 + (1 + w))
                                V.tensor_tensor(acc[:, w], acc[:, w], gates[:, i, w], ALU.add).then_inc(acc_added, 1)
                    split(QUARTER0 + k, q, coef=QUARTER_UNITS)
                    if first:
                        for f, side_kind, m in hooks.get(QUARTER0 + k, []):
                            f(side_kind, m)
                    if group and kind == "branch" and i == 2:
                        dve.wait_ge(merged_hi, q * 2 + (w + 1))
                        m_rows = merged[:, bass.ds(q * 4 + 2 * w, 2)]
                        V.scalar_tensor_tensor(m_rows[:, :, 1, :], acc[:, w], 0.5, f32(m_rows[:, :, 0, :]), ALU.mult, ALU.subtract
                                               ).then_inc(merged_lo, 1)

            quarter(0, first=True)
            with dve.Fori(1, 4) as q:
                quarter(q)

            def out_iteration(i, first=False):
                for k in range(4, 12):
                    w = {7: 0, 11: 1}.get(k)
                    if w is not None:
                        if first and w == 0:
                            dve.wait_ge(gated, 24)
                        else:
                            dve.wait_ge(x2_done, i * 2 + w)
                        add_low(G0["out"] + w, yd[:], i)
                        dve.wait_ge(evac_done, at(G0["out"] + w + 1, i, 2))
                        x_rows = xs[:, bass.ds(i * 4 + 2 * w, 2)]
                        V.tensor_tensor(x_rows, x_rows, yd[:], ALU.add).then_inc(x2_done, 1)
                    split(U0["out"] + k, i)
                    if w is not None:
                        dve.wait_ge(h2_hi, i * 2 + (w + 1))
                        for t in range(2):
                            row = i * 4 + (2 * w + t)
                            x_row = X[:, bass.ds(row, 1)]
                            ins = V.scalar_tensor_tensor(x_row[:, :, 1, :], xs[:, bass.ds(row, 1)], p1("g_ffn", row),
                                                         f32(x_row[:, :, 0, :]), ALU.mult, ALU.subtract)
                        ins.then_inc(h2_lo, 1)

            out_iteration(0, first=True)
            with dve.Fori(1, 4) as i:
                out_iteration(i)

            for w in range(2):
                ins = V.memset(up_pad[w][:, :, 0:2], 0.0)
            ins.then_inc(setup, 1)
            dve.wait_ge(setup, 3)

            def up_scale(i, w):
                dve.wait_ge(evac_done, at(G0["up"] + w + 1, i, 2))
                V.tensor_tensor(up_pad[w][:, :, 2:], up_pad[w][:, :, 2:], rstd2.rearrange("p (a t) -> p a t", a=1).to_broadcast([P, 2, T]),
                                ALU.mult).then_inc(up_scaled, 1)

            def up_taps(i, w):
                for n, s_from, s_to in ((1, conv0, tap1), (0, tap1, tap0)):
                    dve.wait_ge(s_from, i * 2 + (w + 1))
                    for t in range(2):
                        ins = V.scalar_tensor_tensor(up_c[w][:, t], up_pad[w][:, t, n:n + T],
                                                     p1("w_fconv", i * 2 + (n * 2 * FT + w * FT + t)),
                                                     up_c[w][:, t], ALU.mult, ALU.add)
                    ins.then_inc(s_to, 1)

            def up_iteration(i, split_next, first=False):
                U = U0["up"]
                for k in range(4, 7):
                    split(U + k, i)
                add_low(G0["up"], up_pad[0][:, :, 2:], i)
                split(U + 7, i)
                if first:
                    dve.wait_ge(root_done, 2)
                    V.reciprocal(rstd2[:], rstd2[:]).then_inc(rstd_done, 1)
                    dve.wait_ge(rstd_done, 2)
                up_scale(i, 0)
                up_taps(i, 0)
                for k in range(3):
                    split_next(k)
                add_low(G0["up"] + 1, up_pad[1][:, :, 2:], i)
                up_scale(i, 1)
                split_next(3)
                up_taps(i, 1)
                dve.wait_ge(tap0, i * 2 + 2)
                dve.wait_ge(gelu_done, i + 1)
                V.tensor_tensor(up_c[1][:], up_c[0][:], up_c[1][:], ALU.mult).then_inc(prod_done, 1)
                dve.wait_ge(hidden_hi, i + 1)
                hs = hidden[:, bass.ds(i * 2, 2)]
                V.tensor_tensor(hs[:, :, 1, :], up_c[1][:], f32(hs[:, :, 0, :]), ALU.subtract).then_inc(hidden_lo, 1)

            up_iteration(0, lambda k: split(U0["up"] + 8 + k), first=True)
            with dve.Fori(1, FT // 2 - 1) as i:
                up_iteration(i, lambda k: split(U0["up"] + 8 + k, i))
            with dve.Fori(FT // 2 - 1, FT // 2) as i:
                up_iteration(i, lambda k: split(U0["down"] + k))

            def down_iteration(i, more):
                per = FT // UK
                for k in range(4, 4 * per + 4):
                    w = (k - 4) // per
                    if (k - 4) % per == per - 1:
                        g = G0["down"] + w
                        dve.wait_ge(out_done, i * 4 + w) if w else None
                        add_low(g, yd[:], i, groups=4)
                        dve.wait_ge(evac_done, at(g + 1, i, 4))
                        tiles = xs[:, bass.ds(i * 8 + 2 * w, 2)]
                        V.tensor_tensor(tiles, yd[:], tiles, ALU.add).then_inc(out_done, 1)
                    if k < 4 * per or more:
                        split(U0["down"] + k, i, coef=4 * per)

            with dve.Fori(0, 1) as i:
                down_iteration(i, True)
            with dve.Fori(1, 2) as i:
                down_iteration(i, False)

        @block.gpsimd
        def _(pool):
            G = nc.gpsimd

            def wait(**need):
                for e, v in need.items():
                    if not is_zero(v):
                        pool.wait_ge(side[e], v)

            def done(ins):
                ins.then_inc(side["pool"], 1)

            steps = 0

            def step(ins):
                nonlocal steps
                steps += 1
                ins.then_inc(pool_step, 1)

            for j, (src, arrived) in enumerate(((mem_raw, mem_in), (xs, x_in))):
                pool.wait_ge(arrived[0], 16)
                step(G.tensor_tensor(sum0[:, j], src[:, 0:4], src[:, 0:4], ALU.mult))
                for c in range(1, 4):
                    chunk = src[:, 4 * c:4 * c + 4]
                    pool.wait_ge(arrived[c], 16)
                    pool.wait_ge(pool_step, steps)
                    step(G.tensor_tensor(sq0[:], chunk, chunk, ALU.mult))
                    pool.wait_ge(pool_step, steps)
                    step(G.tensor_tensor(sum0[:, j], sum0[:, j], sq0[:], ALU.add))
                pool.wait_ge(pool_step, steps)
                step(G.tensor_tensor(sum0[:, j, 0:2], sum0[:, j, 0:2], sum0[:, j, 2:4], ALU.add))
                pool.wait_ge(pool_step, steps)
                G.tensor_tensor(sum1[:, j], sum0[:, j, 0], sum0[:, j, 1], ALU.add).then_inc(sq_done, 1)

            pool.wait_ge(rstd_done, 1)
            for c in range(4):
                G.tensor_tensor(x_n[:, 4 * c:4 * c + 4], xs[:, 4 * c:4 * c + 4],
                                rstd0[:, 1:2].to_broadcast([P, 4, T]), ALU.mult).then_inc(x_scaled, 1)

            def scale_k(m):
                k_raw = att["mem"]["k_raw"]
                pool.wait_ge(evac_done, at(G0["mkq"] + 1, m, 2))
                done(G.tensor_tensor(k_raw[:], k_raw[:], rstd0[:, 0:1].to_broadcast([P, 2, T]), ALU.mult))

            def add_squares(m):
                S = att["mem"]["S"]
                wait(act=side_count("mem", m, "act", "squares"))
                done(G.tensor_tensor(S[:, :, 0], S[:, :, 0], S[:, :, 1], ALU.add))

            def stage_values(kind, m):
                A = att[kind]
                wait(pe=side_count(kind, m, "pe", None))
                last = G0["mv"] + 3 if kind == "mem" else G0["v"] + 3
                pool.wait_ge(evac_done, last + 1)
                if kind == "mem":
                    for t in range(2):
                        ins = G.tensor_scalar(A["v_cur"][:, t], mem_v[:, t, bass.ds(m * T, T)], rstd_tok[:, t:t + 1], None, ALU.mult)
                    done(ins)
                else:
                    done(G.tensor_copy(A["v_cur"][:], v_all[:, :, bass.ds(m * T, T)]))

            def load_gates(m):
                if is_zero(m):
                    pool.wait_ge(pe_units, U0["lru"])
                wait(pe=side_count("lru", m, "pe", None))
                for j in range(2):
                    G.dma_start(lru["rg"][:, j], w_rg[j, bass.ds(m * 2, 2)].rearrange("b n c -> n b c")).then_inc(rg_in, 16)

            L = lru
            def mem_instance(m):
                scale_k(m)
                add_squares(m)
                stage_values("mem", m)

            def lru_instance(m):
                load_gates(m)
                wait(act=side_count("lru", m, "act", "gelu_square"))
                done(G.tensor_scalar(L["gg"][:], L["gg"][:], GELU_C, 1.0, ALU.mult, ALU.add))
                wait(pool=side_count("lru", m, "pool", "gelu_poly"))
                done(G.tensor_tensor(L["gg"][:], L["gg"][:], L["lg"][:], ALU.mult))
                wait(act=side_count("lru", m, "act", "exps"))
                done(G.tensor_tensor(L["aa"][:], L["a"][:], L["a"][:], ALU.mult))

            for instance in (mem_instance, lru_instance):
                for m in range(4):
                    instance(m)
            wait(dve=side_count("decay", 0, "dve", "c"))
            for h in range(8):
                G.tensor_scalar(rhs_c[:, h], dec["u"][:], rows_sel[0:HR, h:h + 1], ident[0:HR, 32 + h:33 + h], ALU.mult, ALU.add)
            done(G.tensor_scalar(lhs_c[:], dec["u"][:], rows_sel[0:HR, 8:9], rows_sel[0:HR, 9:10], ALU.mult, ALU.add))
            for m in range(4):
                stage_values("fox", m)

            for n in range(8):
                pool.wait_ge(x2_sq, n + 1)
                if n == 0:
                    G.tensor_copy(sum2[:], sq2[:, 0]).then_inc(x2_sum, 1)
                else:
                    pool.wait_ge(x2_sum, n)
                    G.tensor_tensor(sum2[:], sum2[:], sq2[:, n % 2], ALU.add).then_inc(x2_sum, 1)

            with pool.Fori(0, KT // 2 - 1) as i:
                pool.wait_ge(out_done, i + 1)
                G.dma_start(outT[bass.ds(i * UC, UC), :].rearrange("(a p) t -> p a t", p=P), xs[:, bass.ds(i * 2, 2)]).then_inc(out_stored, 16)
            pool.wait_ge(out_stored, 16 * (KT // 2 - 1))


def _columns(v):
    return np.reshape(v, (-1, P)).T


def kernel(x, mem, g_mix, w_in, b_f, g_q_fox, g_k_fox, w_lru_conv, b_lru_conv, w_rg_a, b_rg_a, w_rg_x, b_rg_x,
           lru_lambda, g_mem, w_mem_kv, g_q_mem, g_k_mem, b_gate, w_branch, w_out, g_ffn, w_ffn_up, w_ffn_conv,
           b_ffn_conv, w_ffn_down):
    import concourse.bacc as bacc
    from concourse.bass_utils import run_bass_kernel_spmd

    A = np.asarray
    bf = np.zeros((P, 1), A(b_f).dtype)
    bf[0:8, 0] = A(b_f)[0]
    bf[32:40, 0] = A(b_f)[0]
    packed = [_columns(A(v)[0].reshape(-1)) for v in
              (g_mix, g_mem, g_ffn, b_gate, w_ffn_conv, b_ffn_conv, w_lru_conv, b_lru_conv, b_rg_a, b_rg_x, lru_lambda,
               g_q_fox, g_k_fox, g_q_mem, g_k_mem)]
    par = np.ascontiguousarray(np.concatenate(packed + [bf], axis=1))
    assert par.shape == (P, N_PAR)
    key = np.arange(T)
    mask = [np.where(key[None, :(qt + 1) * P] <= (qt * P + np.arange(P))[:, None], 0.0, MASKED) for qt in range(2)]
    high = ((np.arange(P) >= 32) & (np.arange(P) < 64))[:, None]
    shapes_const = np.concatenate([np.eye(P)] + mask + [-np.eye(P)[:, 0:8], high, ~high], axis=1).astype(np.float32)
    arrays = {
        "xT": np.ascontiguousarray(A(x)[0].T), "memT": np.ascontiguousarray(A(mem)[0].T), "par": par,
        "shapes_const": shapes_const, "w_in": A(w_in)[0], "w_mem_kv": A(w_mem_kv)[0],
        "w_rg": np.stack([A(w_rg_a)[0], A(w_rg_x)[0]]), "w_branch": A(w_branch)[0].reshape(3 * BW, D),
        "w_out": A(w_out)[0], "w_up": A(w_ffn_up)[0], "w_down": A(w_ffn_down)[0],
    }
    nc = bacc.Bacc("TRN2", target_bir_lowering=False, num_devices=1)
    args = [nc.dram_tensor(n, a.shape, mybir.dt.from_np(a.dtype), kind="ExternalInput").ap() for n, a in arrays.items()]
    args.append(nc.dram_tensor("outT", (D, T), F32, kind="ExternalOutput").ap())
    hybrid_layer_kernel(nc, *args)
    r = run_bass_kernel_spmd(nc, [arrays], core_ids=[0])
    return np.ascontiguousarray(r.results[0]["outT"].T)[None]
```
